# Optimizing a Trainium2 kernel written in Bass

```python
import math
import jax, jax.numpy as jnp
from jax import lax
import numpy as np
import jax
import jax.numpy as jnp

D_MODEL = 1024
BATCH = 1
SEQ = 256
DEPTH = 2

N_EVEN = (DEPTH + 1) // 2
N_ODD = DEPTH // 2

MEM_LEN = 256
NORM_EPS = 1e-6

MLA_HEADS = 8
MLA_NOPE = 64
MLA_ROPE = 32
MLA_QK = MLA_NOPE + MLA_ROPE
MLA_V = 64
MLA_Q_RANK = 384
MLA_KV_RANK = 256
ROPE_BASE = 10000.0
Q_BLOCK = 128

RW_HEADS = 8
RW_HEAD = 64
RW_DIM = RW_HEADS * RW_HEAD
RW_DECAY_LORA = 64
RW_AAA_LORA = 64
RW_GATE_LORA = 128
RW_LN_EPS = 64e-5

MLA_IN = MLA_Q_RANK + MLA_KV_RANK + MLA_ROPE
RW_IN = 3 * RW_DIM + RW_DECAY_LORA + RW_AAA_LORA + RW_GATE_LORA
EVEN_IN = MLA_IN + RW_IN
EVEN_MIX = MLA_HEADS * MLA_V + RW_DIM

SSM_INNER = 2 * D_MODEL
SSM_HEAD = 64
SSM_HEADS = SSM_INNER // SSM_HEAD
SSM_GROUPS = 4
SSM_STATE = 128
SSM_CONV = 4
SSM_CHUNK = 256
SSM_CONV_DIM = SSM_INNER + 2 * SSM_GROUPS * SSM_STATE
ODD_IN = SSM_INNER + SSM_CONV_DIM + SSM_HEADS

X_HEADS = 4
X_HEAD = 128
X_DIM = X_HEADS * X_HEAD

FFN_HIDDEN = -((-8 * D_MODEL) // (3 * 256)) * 256


def rms_norm(x, g, eps=NORM_EPS):
    xf = x.astype(jnp.float32)
    y = xf * lax.rsqrt(jnp.mean(xf * xf, axis=-1, keepdims=True) + eps)
    return (y * g.astype(jnp.float32)).astype(x.dtype)

def apply_rope(x, positions):
    half = x.shape[-1] // 2
    inv_freq = ROPE_BASE ** (-jnp.arange(half, dtype=jnp.float32) / half)
    ang = positions.astype(jnp.float32)[:, :, None, None] * inv_freq
    cos, sin = jnp.cos(ang), jnp.sin(ang)
    xf = x.astype(jnp.float32)
    x1, x2 = xf[..., :half], xf[..., half:]
    return jnp.concatenate([x1 * cos - x2 * sin, x2 * cos + x1 * sin], axis=-1).astype(x.dtype)

def causal_block_attention(q, k, v):
    b, s, h, dk = q.shape
    nb = s // Q_BLOCK
    scale = dk ** -0.5
    qb = jnp.moveaxis(q.reshape(b, nb, Q_BLOCK, h, dk), 1, 0)
    k_idx = jnp.arange(s)

    def block(args):
        q_blk, blk = args
        scores = jnp.einsum("bqhd,bkhd->bhqk", q_blk, k, preferred_element_type=jnp.float32) * scale
        q_idx = blk * Q_BLOCK + jnp.arange(Q_BLOCK)
        scores = jnp.where(k_idx[None, :] <= q_idx[:, None], scores, -jnp.inf)
        probs = jax.nn.softmax(scores, axis=-1).astype(v.dtype)
        return jnp.einsum("bhqk,bkhd->bqhd", probs, v)

    out = lax.map(block, (qb, jnp.arange(nb)))
    return jnp.moveaxis(out, 0, 1).reshape(b, s, h, v.shape[-1])

def mla_group(p, positions, q_norm, w_uq, kv_norm, w_ukv, q_hnorm, k_hnorm):
    b, s, _ = p.shape
    c_q = rms_norm(p[..., :MLA_Q_RANK], q_norm)
    c_kv = rms_norm(p[..., MLA_Q_RANK:MLA_Q_RANK + MLA_KV_RANK], kv_norm)
    k_rope = p[..., MLA_Q_RANK + MLA_KV_RANK:]
    q = (c_q @ w_uq).reshape(b, s, MLA_HEADS, MLA_QK)
    kv = (c_kv @ w_ukv).reshape(b, s, MLA_HEADS, MLA_NOPE + MLA_V)
    k_nope, v = kv[..., :MLA_NOPE], kv[..., MLA_NOPE:]
    k = jnp.concatenate([k_nope, jnp.broadcast_to(k_rope[:, :, None, :], (b, s, MLA_HEADS, MLA_ROPE))], axis=-1)
    q = rms_norm(q, q_hnorm)
    k = rms_norm(k, k_hnorm)
    q = jnp.concatenate([q[..., :MLA_NOPE], apply_rope(q[..., MLA_NOPE:], positions)], axis=-1)
    k = jnp.concatenate([k[..., :MLA_NOPE], apply_rope(k[..., MLA_NOPE:], positions)], axis=-1)
    return causal_block_attention(q, k, v).reshape(b, s, MLA_HEADS * MLA_V)

def token_shift(p, mu):
    prev = jnp.pad(p, ((0, 0), (1, 0), (0, 0)))[:, :-1]
    return p + (prev - p) * mu

def wkv7_scan(r, w, k, v, a, bb):
    b, s, h, n = r.shape
    xs = tuple(jnp.moveaxis(t.astype(jnp.float32), 1, 0) for t in (r, w, k, v, a, bb))

    def step(state, inp):
        r_t, w_t, k_t, v_t, a_t, b_t = inp
        sa = jnp.einsum("bhvk,bhk->bhv", state, a_t)
        state = state * w_t[:, :, None, :] + sa[..., None] * b_t[:, :, None, :] + v_t[..., None] * k_t[:, :, None, :]
        return state, jnp.einsum("bhvk,bhk->bhv", state, r_t)

    state0 = jnp.zeros((b, h, n, n), jnp.float32)
    _, ys = lax.scan(step, state0, xs)
    return jnp.moveaxis(ys, 0, 1)

def rwkv7_group(p, mu, w0, w2, a0, a2, g2, k_k, k_a, r_k, ln_g, ln_b):
    b, s, _ = p.shape
    p = token_shift(p, mu)
    r = p[..., :RW_DIM]
    k = p[..., RW_DIM:2 * RW_DIM]
    v = p[..., 2 * RW_DIM:3 * RW_DIM]
    o = 3 * RW_DIM
    xw = p[..., o:o + RW_DECAY_LORA]
    o += RW_DECAY_LORA
    xa = p[..., o:o + RW_AAA_LORA]
    o += RW_AAA_LORA
    xg = p[..., o:o + RW_GATE_LORA]
    w_log = -jax.nn.softplus(-(w0 + jnp.tanh(xw) @ w2)) - 0.5
    decay = jnp.exp(-jnp.exp(w_log.astype(jnp.float32)))
    a = jax.nn.sigmoid(a0 + xa @ a2)
    g = jax.nn.sigmoid(xg) @ g2
    heads = lambda t: t.reshape(b, s, RW_HEADS, RW_HEAD)
    kk = heads(k * k_k).astype(jnp.float32)
    kk = kk / jnp.maximum(jnp.sqrt(jnp.sum(kk * kk, axis=-1, keepdims=True)), 1e-12)
    k = k * (1.0 + (a - 1.0) * k_a)
    r_h, k_h, v_h, a_h = heads(r), heads(k), heads(v), heads(a).astype(jnp.float32)
    y = wkv7_scan(r_h, heads(decay), k_h, v_h, -kk, kk * a_h)
    mean = jnp.mean(y, axis=-1, keepdims=True)
    var = jnp.mean(jnp.square(y - mean), axis=-1, keepdims=True)
    y = ((y - mean) * lax.rsqrt(var + RW_LN_EPS)).reshape(b, s, RW_DIM)
    y = (y * ln_g.astype(jnp.float32) + ln_b.astype(jnp.float32)).astype(p.dtype)
    bonus = jnp.sum(r_h * k_h * r_k, axis=-1, keepdims=True) * v_h
    y = y + bonus.reshape(b, s, RW_DIM)
    return y * g

def even_mixer(h, positions, norm, w_in, q_norm, w_uq, kv_norm, w_ukv, q_hnorm, k_hnorm,
               mu, w0, w2, a0, a2, g2, k_k, k_a, r_k, ln_g, ln_b, w_out):
    proj = rms_norm(h, norm) @ w_in
    y_mla = mla_group(proj[..., :MLA_IN], positions, q_norm, w_uq, kv_norm, w_ukv, q_hnorm, k_hnorm)
    y_rw = rwkv7_group(proj[..., MLA_IN:], mu, w0, w2, a0, a2, g2, k_k, k_a, r_k, ln_g, ln_b)
    return jnp.concatenate([y_mla, y_rw], axis=-1) @ w_out

def causal_depthwise_conv(x, w, bias):
    width, c = w.shape
    out = lax.conv_general_dilated(x, w[:, None, :].astype(x.dtype), window_strides=(1,),
                                   padding=((width - 1, 0),),
                                   dimension_numbers=("NWC", "WIO", "NWC"),
                                   feature_group_count=c)
    return out + bias

def ssd_chunked(x, a, b_in, c_in):
    bsz, s, n_heads, head_p = x.shape
    n_groups, n_state = b_in.shape[2], b_in.shape[3]
    e_per = n_heads // n_groups
    L = SSM_CHUNK
    nc = -(-s // L)
    pad = nc * L - s
    padt = lambda t: jnp.pad(t.astype(jnp.float32), ((0, 0), (0, pad)) + ((0, 0),) * (t.ndim - 2))
    xc = padt(x).reshape(bsz, nc, L, n_groups, e_per, head_p)
    ac = padt(a).reshape(bsz, nc, L, n_groups, e_per)
    bc = padt(b_in).reshape(bsz, nc, L, n_groups, n_state)
    cc = padt(c_in).reshape(bsz, nc, L, n_groups, n_state)
    xs = tuple(jnp.moveaxis(t, 1, 0) for t in (xc, ac, bc, cc))
    causal = jnp.tril(jnp.ones((L, L), dtype=bool))[None, :, :, None, None]

    def step(state, inp):
        x_c, a_c, b_c, c_c = inp
        cum = jnp.cumsum(a_c, axis=1)
        seg = cum[:, :, None] - cum[:, None, :]
        decay = jnp.exp(jnp.where(causal, seg, -jnp.inf))
        cb = jnp.einsum("blgn,bsgn->blsg", c_c, b_c)
        y = jnp.einsum("blsg,blsge,bsgep->blgep", cb, decay, x_c)
        y = y + jnp.einsum("blgn,bgepn->blgep", c_c, state) * jnp.exp(cum)[..., None]
        to_end = jnp.exp(cum[:, -1:] - cum)
        state = state * jnp.exp(cum[:, -1])[..., None, None] + jnp.einsum("blgn,blge,blgep->bgepn", b_c, to_end, x_c)
        return state, y

    state0 = jnp.zeros((bsz, n_groups, e_per, head_p, n_state), jnp.float32)
    _, ys = lax.scan(step, state0, xs)
    return jnp.moveaxis(ys, 0, 1).reshape(bsz, nc * L, n_heads, head_p)[:, :s]

def mamba2_mixer(h, norm, w_in, conv_w, conv_b, dt_bias, a_log, d_skip, gnorm, w_out):
    b, s, _ = h.shape
    proj = rms_norm(h, norm) @ w_in
    z = proj[..., :SSM_INNER]
    xbc = proj[..., SSM_INNER:SSM_INNER + SSM_CONV_DIM]
    dt_raw = proj[..., SSM_INNER + SSM_CONV_DIM:]
    xbc = jax.nn.silu(causal_depthwise_conv(xbc, conv_w, conv_b))
    gn = SSM_GROUPS * SSM_STATE
    xs = xbc[..., :SSM_INNER].reshape(b, s, SSM_HEADS, SSM_HEAD)
    b_in = xbc[..., SSM_INNER:SSM_INNER + gn].reshape(b, s, SSM_GROUPS, SSM_STATE)
    c_in = xbc[..., SSM_INNER + gn:].reshape(b, s, SSM_GROUPS, SSM_STATE)
    dt = jax.nn.softplus(dt_raw.astype(jnp.float32) + dt_bias.astype(jnp.float32))
    A = -jnp.exp(a_log.astype(jnp.float32))
    xf = xs.astype(jnp.float32)
    y = ssd_chunked(xf * dt[..., None], dt * A, b_in, c_in)
    y = y + xf * d_skip.astype(jnp.float32)[:, None]
    y = y.reshape(b, s, SSM_INNER) * jax.nn.silu(z.astype(jnp.float32))
    y = y.reshape(b, s, SSM_GROUPS, SSM_INNER // SSM_GROUPS)
    y = y * lax.rsqrt(jnp.mean(y * y, axis=-1, keepdims=True) + NORM_EPS)
    y = (y.reshape(b, s, SSM_INNER) * gnorm.astype(jnp.float32)).astype(h.dtype)
    return y @ w_out

def memory_cross_attention(h, mem, norm_x, norm_mem, wq, wkv, q_hnorm, k_hnorm, wo):
    b, s, _ = h.shape
    m = mem.shape[1]
    q = (rms_norm(h, norm_x) @ wq).reshape(b, s, X_HEADS, X_HEAD)
    kv = (rms_norm(mem, norm_mem) @ wkv).reshape(b, m, 2, X_HEADS, X_HEAD)
    q = rms_norm(q, q_hnorm)
    k = rms_norm(kv[:, :, 0], k_hnorm)
    v = kv[:, :, 1]
    scores = jnp.einsum("bqhd,bmhd->bhqm", q, k, preferred_element_type=jnp.float32) * (X_HEAD ** -0.5)
    probs = jax.nn.softmax(scores, axis=-1).astype(v.dtype)
    out = jnp.einsum("bhqm,bmhd->bqhd", probs, v).reshape(b, s, X_DIM)
    return out @ wo

def swiglu_ffn(h, norm, w13, w2):
    u = rms_norm(h, norm) @ w13
    return (jax.nn.silu(u[..., :FFN_HIDDEN]) * u[..., FFN_HIDDEN:]) @ w2

def first_inputs(seed: int = 0) -> dict:
    key = jax.random.key(seed)
    ks = iter(jax.random.split(key, 64))
    f32 = jnp.float32

    def nrm(shape, fan_in, scale=1.0):
        return scale * fan_in ** -0.5 * jax.random.normal(next(ks), shape, f32)

    def gain(shape):
        return 1.0 + 0.05 * jax.random.normal(next(ks), shape, f32)

    def unif(shape, lo, hi):
        return jax.random.uniform(next(ks), shape, f32, lo, hi)

    E, O, L = N_EVEN, N_ODD, DEPTH
    x = jax.random.normal(next(ks), (BATCH, SEQ, D_MODEL), f32)
    mem = jax.random.normal(next(ks), (BATCH, MEM_LEN, D_MODEL), f32)
    positions = (jax.random.randint(next(ks), (BATCH, 1), 0, 1024, jnp.int32)
                 + jnp.arange(SEQ, dtype=jnp.int32)[None, :])
    dt0 = jnp.exp(unif((O, SSM_HEADS), math.log(1e-3), math.log(1e-1)))
    return {
        "x": x, "mem": mem, "positions": positions,
        "ev_norm": gain((E, D_MODEL)),
        "ev_w_in": nrm((E, D_MODEL, EVEN_IN), D_MODEL),
        "mla_q_norm": gain((E, MLA_Q_RANK)),
        "mla_w_uq": nrm((E, MLA_Q_RANK, MLA_HEADS * MLA_QK), MLA_Q_RANK),
        "mla_kv_norm": gain((E, MLA_KV_RANK)),
        "mla_w_ukv": nrm((E, MLA_KV_RANK, MLA_HEADS * (MLA_NOPE + MLA_V)), MLA_KV_RANK),
        "mla_q_hnorm": gain((E, MLA_QK)),
        "mla_k_hnorm": gain((E, MLA_QK)),
        "rw_mu": unif((E, RW_IN), 0.0, 1.0),
        "rw_w0": unif((E, RW_DIM), -6.0, -1.0),
        "rw_w2": nrm((E, RW_DECAY_LORA, RW_DIM), RW_DECAY_LORA),
        "rw_a0": 0.1 * jax.random.normal(next(ks), (E, RW_DIM), f32),
        "rw_a2": nrm((E, RW_AAA_LORA, RW_DIM), RW_AAA_LORA),
        "rw_g2": nrm((E, RW_GATE_LORA, RW_DIM), RW_GATE_LORA),
        "rw_k_k": unif((E, RW_DIM), 0.7, 1.0),
        "rw_k_a": unif((E, RW_DIM), 0.8, 1.2),
        "rw_r_k": 0.1 * jax.random.normal(next(ks), (E, RW_HEADS, RW_HEAD), f32),
        "rw_ln_g": gain((E, RW_DIM)),
        "rw_ln_b": 0.02 * jax.random.normal(next(ks), (E, RW_DIM), f32),
        "ev_w_out": nrm((E, EVEN_MIX, D_MODEL), EVEN_MIX),
        "od_norm": gain((O, D_MODEL)),
        "od_w_in": nrm((O, D_MODEL, ODD_IN), D_MODEL),
        "ssm_conv_w": nrm((O, SSM_CONV, SSM_CONV_DIM), SSM_CONV),
        "ssm_conv_b": 0.02 * jax.random.normal(next(ks), (O, SSM_CONV_DIM), f32),
        "ssm_dt_bias": dt0 + jnp.log(-jnp.expm1(-dt0)),
        "ssm_a_log": jnp.log(unif((O, SSM_HEADS), 1.0, 16.0)),
        "ssm_d": gain((O, SSM_HEADS)),
        "ssm_gnorm": gain((O, SSM_INNER)),
        "od_w_out": nrm((O, SSM_INNER, D_MODEL), SSM_INNER),
        "xa_norm_x": gain((L, D_MODEL)),
        "xa_norm_mem": gain((L, D_MODEL)),
        "xa_wq": nrm((L, D_MODEL, X_DIM), D_MODEL),
        "xa_wkv": nrm((L, D_MODEL, 2 * X_DIM), D_MODEL),
        "xa_q_hnorm": gain((L, X_HEAD)),
        "xa_k_hnorm": gain((L, X_HEAD)),
        "xa_wo": nrm((L, X_DIM, D_MODEL), X_DIM),
        "ffn_norm": gain((L, D_MODEL)),
        "ffn_w13": nrm((L, D_MODEL, 2 * FFN_HIDDEN), D_MODEL),
        "ffn_w2": nrm((L, FFN_HIDDEN, D_MODEL), FFN_HIDDEN),
    }

def first_block(x, mem, positions,
              ev_norm, ev_w_in, mla_q_norm, mla_w_uq, mla_kv_norm, mla_w_ukv, mla_q_hnorm, mla_k_hnorm,
              rw_mu, rw_w0, rw_w2, rw_a0, rw_a2, rw_g2, rw_k_k, rw_k_a, rw_r_k, rw_ln_g, rw_ln_b, ev_w_out,
              od_norm, od_w_in, ssm_conv_w, ssm_conv_b, ssm_dt_bias, ssm_a_log, ssm_d, ssm_gnorm, od_w_out,
              xa_norm_x, xa_norm_mem, xa_wq, xa_wkv, xa_q_hnorm, xa_k_hnorm, xa_wo,
              ffn_norm, ffn_w13, ffn_w2):
    h = x
    for i in range(DEPTH):
        j = i // 2
        if i % 2 == 0:
            h = h + even_mixer(h, positions, ev_norm[j], ev_w_in[j], mla_q_norm[j], mla_w_uq[j],
                               mla_kv_norm[j], mla_w_ukv[j], mla_q_hnorm[j], mla_k_hnorm[j],
                               rw_mu[j], rw_w0[j], rw_w2[j], rw_a0[j], rw_a2[j], rw_g2[j],
                               rw_k_k[j], rw_k_a[j], rw_r_k[j], rw_ln_g[j], rw_ln_b[j], ev_w_out[j])
        else:
            h = h + mamba2_mixer(h, od_norm[j], od_w_in[j], ssm_conv_w[j], ssm_conv_b[j],
                                 ssm_dt_bias[j], ssm_a_log[j], ssm_d[j], ssm_gnorm[j], od_w_out[j])
        h = h + memory_cross_attention(h, mem, xa_norm_x[i], xa_norm_mem[i], xa_wq[i], xa_wkv[i],
                                       xa_q_hnorm[i], xa_k_hnorm[i], xa_wo[i])
        h = h + swiglu_ffn(h, ffn_norm[i], ffn_w13[i], ffn_w2[i])
    return h


EPS = 1e-6
CONV_WIDTH = 4
LRU_WIDTH = D_MODEL // 2
LRU_BLOCKS = 8
LRU_BLOCK = LRU_WIDTH // LRU_BLOCKS
LRU_C = 8.0
ATT_HEAD_DIM = 64
ATT_Q_HEADS = (D_MODEL // 2) // ATT_HEAD_DIM
ATT_KV_HEADS = 2
ATT_GROUPS = ATT_Q_HEADS // ATT_KV_HEADS
ATT_Q_WIDTH = ATT_Q_HEADS * ATT_HEAD_DIM
ATT_KV_WIDTH = ATT_KV_HEADS * ATT_HEAD_DIM
WINDOW = 128
ROPE_THETA = 10000.0
EVEN_IN_COLS = 2 * LRU_WIDTH + ATT_Q_WIDTH + 2 * ATT_KV_WIDTH
EVEN_MIX_WIDTH = LRU_WIDTH + ATT_Q_WIDTH
D_FF_DENSE = 2816
GDN_HEADS = 8
GDN_HEAD_DIM = 128
GDN_WIDTH = GDN_HEADS * GDN_HEAD_DIM
GDN_CHUNK = 64
ODD_IN_COLS = 4 * GDN_WIDTH + 2 * GDN_HEADS
N_EXPERTS = 8
TOP_K = 2
D_FF_EXPERT = 3584
N_EVEN_2 = (DEPTH + 1) // 2
N_ODD_2 = DEPTH // 2


def rms_norm_2(x, g):
    xf = x.astype(jnp.float32)
    y = xf * lax.rsqrt(jnp.mean(xf * xf, axis=-1, keepdims=True) + EPS)
    return (y * g.astype(jnp.float32)).astype(x.dtype)

def l2_norm(x):
    return x * lax.rsqrt(jnp.sum(x * x, axis=-1, keepdims=True) + EPS)

def causal_depthwise_conv_2(x, w):
    seq = x.shape[1]
    xp = jnp.pad(x, ((0, 0), (CONV_WIDTH - 1, 0), (0, 0)))
    return sum(w[j] * xp[:, j:j + seq] for j in range(CONV_WIDTH))

def rope(x, pos):
    half = x.shape[-1] // 2
    inv_freq = ROPE_THETA ** (-jnp.arange(half, dtype=jnp.float32) / half)
    ang = pos.astype(jnp.float32)[:, None] * inv_freq[None, :]
    cos = jnp.cos(ang)[None, :, None, :]
    sin = jnp.sin(ang)[None, :, None, :]
    xf = x.astype(jnp.float32)
    x1, x2 = xf[..., :half], xf[..., half:]
    return jnp.concatenate([x1 * cos - x2 * sin, x2 * cos + x1 * sin], axis=-1)

def swiglu(h, w_gate, w_up, w_down):
    return (jax.nn.silu(h @ w_gate) * (h @ w_up)) @ w_down

def rg_lru(xb, conv_w, conv_b, w_a, b_a, w_i, b_i, lam):
    bsz, seq, _ = xb.shape
    xc = causal_depthwise_conv_2(xb, conv_w) + conv_b
    xh = xc.reshape(bsz, seq, LRU_BLOCKS, LRU_BLOCK)
    r = jax.nn.sigmoid(jnp.einsum('bshi,hij->bshj', xh, w_a).reshape(bsz, seq, LRU_WIDTH) + b_a)
    gi = jax.nn.sigmoid(jnp.einsum('bshi,hij->bshj', xh, w_i).reshape(bsz, seq, LRU_WIDTH) + b_i)
    log_a = -LRU_C * r * jax.nn.softplus(-lam)
    a = jnp.exp(log_a)
    u = jnp.sqrt(-jnp.expm1(2.0 * log_a)) * (gi * xc)

    def combine(c1, c2):
        a1, b1 = c1
        a2, b2 = c2
        return a1 * a2, a2 * b1 + b2

    _, h = lax.associative_scan(combine, (a, u), axis=1)
    return h

def sliding_window_attention(q, k, v, sinks):
    bsz, seq = q.shape[:2]
    nb = seq // WINDOW
    qb = q.astype(jnp.float32).reshape(bsz, nb, WINDOW, ATT_KV_HEADS, ATT_GROUPS, ATT_HEAD_DIM)

    def with_prev(t):
        tb = t.astype(jnp.float32).reshape(bsz, nb, WINDOW, ATT_KV_HEADS, ATT_HEAD_DIM)
        prev = jnp.pad(tb, ((0, 0), (1, 0), (0, 0), (0, 0), (0, 0)))[:, :-1]
        return jnp.concatenate([prev, tb], axis=2)

    kb, vb = with_prev(k), with_prev(v)
    s = jnp.einsum('bnqhgd,bnkhd->bnhgqk', qb, kb) * (ATT_HEAD_DIM ** -0.5)
    qi = jnp.arange(WINDOW)[:, None] + WINDOW
    kj = jnp.arange(2 * WINDOW)[None, :]
    rel = qi - kj
    band = (rel >= 0) & (rel < WINDOW)
    valid = band[None] & ((jnp.arange(nb)[:, None, None] > 0) | (kj >= WINDOW)[None])
    s = jnp.where(valid[None, :, None, None], s, -1e30)
    sink = sinks.astype(jnp.float32).reshape(ATT_KV_HEADS, ATT_GROUPS)[None, None, :, :, None, None]
    m = jnp.maximum(jnp.max(s, axis=-1, keepdims=True), sink)
    p = jnp.exp(s - m)
    denom = jnp.sum(p, axis=-1, keepdims=True) + jnp.exp(sink - m)
    o = jnp.einsum('bnhgqk,bnkhd->bnqhgd', p / denom, vb)
    return o.reshape(bsz, seq, ATT_Q_WIDTH)

def even_mixer_2(h, pos, w_in, conv_w, conv_b, w_a, b_a, w_i, b_i, lam, q_norm, k_norm, sinks, w_out):
    bsz, seq, _ = h.shape
    proj = h @ w_in
    cuts = np.cumsum([LRU_WIDTH, LRU_WIDTH, ATT_Q_WIDTH, ATT_KV_WIDTH]).tolist()
    xb, gate, q, k, v = jnp.split(proj, cuts, axis=-1)
    y_lru = rg_lru(xb.astype(jnp.float32), conv_w, conv_b, w_a, b_a, w_i, b_i, lam) \
        * jax.nn.gelu(gate.astype(jnp.float32))
    q = rope(rms_norm_2(q.reshape(bsz, seq, ATT_Q_HEADS, ATT_HEAD_DIM), q_norm), pos)
    k = rope(rms_norm_2(k.reshape(bsz, seq, ATT_KV_HEADS, ATT_HEAD_DIM), k_norm), pos)
    v = v.reshape(bsz, seq, ATT_KV_HEADS, ATT_HEAD_DIM)
    y_att = sliding_window_attention(q, k, v, sinks)
    y = jnp.concatenate([y_lru.astype(h.dtype), y_att.astype(h.dtype)], axis=-1)
    return y @ w_out

def gated_deltanet(h, w_in, conv_w, a_log, dt_bias, out_norm, w_out):
    bsz, seq, _ = h.shape
    nc = seq // GDN_CHUNK
    C = GDN_CHUNK
    proj = (h @ w_in).astype(jnp.float32)
    cuts = [3 * GDN_WIDTH, 4 * GDN_WIDTH, 4 * GDN_WIDTH + GDN_HEADS]
    qkv, gate, a_in, b_in = jnp.split(proj, cuts, axis=-1)
    qkv = jax.nn.silu(causal_depthwise_conv_2(qkv, conv_w.astype(jnp.float32)))
    q, k, v = jnp.split(qkv, 3, axis=-1)
    q = l2_norm(q.reshape(bsz, seq, GDN_HEADS, GDN_HEAD_DIM)) * (GDN_HEAD_DIM ** -0.5)
    k = l2_norm(k.reshape(bsz, seq, GDN_HEADS, GDN_HEAD_DIM))
    v = v.reshape(bsz, seq, GDN_HEADS, GDN_HEAD_DIM)
    beta = jax.nn.sigmoid(b_in)
    g = -jnp.exp(a_log.astype(jnp.float32)) * jax.nn.softplus(a_in + dt_bias.astype(jnp.float32))

    def to_chunks(t):
        return t.reshape(bsz, nc, C, GDN_HEADS, -1).transpose(0, 3, 1, 2, 4)

    qc, kc, vc = to_chunks(q), to_chunks(k), to_chunks(v)
    gc = g.reshape(bsz, nc, C, GDN_HEADS).transpose(0, 3, 1, 2)
    bc = beta.reshape(bsz, nc, C, GDN_HEADS).transpose(0, 3, 1, 2)
    G = jnp.cumsum(gc, axis=-1)
    tri = jnp.tril(jnp.ones((C, C), dtype=bool))
    strict = jnp.tril(jnp.ones((C, C), dtype=bool), -1)
    diff = G[..., :, None] - G[..., None, :]
    decay = jnp.where(tri, jnp.exp(jnp.where(tri, diff, 0.0)), 0.0)
    kk = jnp.einsum('bhnid,bhnjd->bhnij', kc, kc)
    A = jnp.where(strict, bc[..., :, None] * kk * decay, 0.0) + jnp.eye(C, dtype=jnp.float32)
    u = lax.linalg.triangular_solve(A, bc[..., None] * vc, left_side=True, lower=True, unit_diagonal=True)
    w = lax.linalg.triangular_solve(A, bc[..., None] * jnp.exp(G)[..., None] * kc,
                                    left_side=True, lower=True, unit_diagonal=True)
    a_qk = jnp.where(tri, jnp.einsum('bhnid,bhnjd->bhnij', qc, kc) * decay, 0.0)
    q_dec = qc * jnp.exp(G)[..., None]
    k_dec = kc * jnp.exp(G[..., -1:] - G)[..., None]
    g_last = jnp.exp(G[..., -1])
    xs = (jnp.moveaxis(u, 2, 0), jnp.moveaxis(w, 2, 0), jnp.moveaxis(a_qk, 2, 0),
          jnp.moveaxis(q_dec, 2, 0), jnp.moveaxis(k_dec, 2, 0), jnp.moveaxis(g_last, 2, 0))

    def step(state, inp):
        u_c, w_c, a_c, qd_c, kd_c, gl_c = inp
        v_new = u_c - jnp.einsum('bhcd,bhde->bhce', w_c, state)
        o_c = jnp.einsum('bhcd,bhde->bhce', qd_c, state) + jnp.einsum('bhcj,bhje->bhce', a_c, v_new)
        state = state * gl_c[..., None, None] + jnp.einsum('bhcd,bhce->bhde', kd_c, v_new)
        return state, o_c

    s0 = jnp.zeros((bsz, GDN_HEADS, GDN_HEAD_DIM, GDN_HEAD_DIM), jnp.float32)
    _, o = lax.scan(step, s0, xs)
    o = o.transpose(1, 0, 3, 2, 4).reshape(bsz, seq, GDN_HEADS, GDN_HEAD_DIM)
    o = rms_norm_2(o, out_norm) * jax.nn.silu(gate.reshape(bsz, seq, GDN_HEADS, GDN_HEAD_DIM))
    return o.reshape(bsz, seq, GDN_WIDTH).astype(h.dtype) @ w_out

def moe_swiglu(h, router, w_gate, w_up, w_down):
    bsz, seq, d = h.shape
    t = h.reshape(-1, d)
    logits = (t @ router).astype(jnp.float32)
    top_v, top_i = lax.top_k(logits, TOP_K)
    top_w = jax.nn.softmax(top_v, axis=-1)
    gates = jnp.sum(jax.nn.one_hot(top_i, N_EXPERTS, dtype=jnp.float32) * top_w[..., None], axis=1)
    out = jnp.zeros(t.shape, jnp.float32)
    for e in range(N_EXPERTS):
        y_e = swiglu(t, w_gate[e], w_up[e], w_down[e]).astype(jnp.float32)
        out = out + gates[:, e:e + 1] * y_e
    return out.astype(h.dtype).reshape(bsz, seq, d)

def second_inputs(seed: int = 0) -> dict:
    key = jax.random.key(seed)
    ks = jax.random.split(key, 32)
    f32 = jnp.float32
    D = D_MODEL

    def nrm(k, shape, scale):
        return scale * jax.random.normal(k, shape, f32)

    lru_u = jax.random.uniform(ks[10], (N_EVEN_2, LRU_WIDTH), f32, minval=0.9, maxval=0.999)
    lru_s = lru_u ** (1.0 / LRU_C)
    dt = jnp.exp(jax.random.uniform(ks[21], (N_ODD_2, GDN_HEADS), f32,
                                    minval=float(np.log(0.001)), maxval=float(np.log(0.1))))
    return {
        "x": nrm(ks[0], (BATCH, SEQ, D), 1.0),
        "ln_mix": 1.0 + nrm(ks[1], (DEPTH, D), 0.02),
        "ln_ffn": 1.0 + nrm(ks[2], (DEPTH, D), 0.02),
        "e_w_in": nrm(ks[3], (N_EVEN_2, D, EVEN_IN_COLS), D ** -0.5),
        "e_lru_conv_w": nrm(ks[4], (N_EVEN_2, CONV_WIDTH, LRU_WIDTH), CONV_WIDTH ** -0.5),
        "e_lru_conv_b": nrm(ks[5], (N_EVEN_2, LRU_WIDTH), 0.02),
        "e_lru_w_a": nrm(ks[6], (N_EVEN_2, LRU_BLOCKS, LRU_BLOCK, LRU_BLOCK), LRU_BLOCK ** -0.5),
        "e_lru_b_a": nrm(ks[7], (N_EVEN_2, LRU_WIDTH), 0.1),
        "e_lru_w_i": nrm(ks[8], (N_EVEN_2, LRU_BLOCKS, LRU_BLOCK, LRU_BLOCK), LRU_BLOCK ** -0.5),
        "e_lru_b_i": nrm(ks[9], (N_EVEN_2, LRU_WIDTH), 0.1),
        "e_lru_lambda": jnp.log(lru_s) - jnp.log1p(-lru_s),
        "e_q_norm": 1.0 + nrm(ks[11], (N_EVEN_2, ATT_HEAD_DIM), 0.02),
        "e_k_norm": 1.0 + nrm(ks[12], (N_EVEN_2, ATT_HEAD_DIM), 0.02),
        "e_sinks": nrm(ks[13], (N_EVEN_2, ATT_Q_HEADS), 1.0),
        "e_w_out": nrm(ks[14], (N_EVEN_2, EVEN_MIX_WIDTH, D), EVEN_MIX_WIDTH ** -0.5),
        "e_ffn_w_gate": nrm(ks[15], (N_EVEN_2, D, D_FF_DENSE), D ** -0.5),
        "e_ffn_w_up": nrm(ks[16], (N_EVEN_2, D, D_FF_DENSE), D ** -0.5),
        "e_ffn_w_down": nrm(ks[17], (N_EVEN_2, D_FF_DENSE, D), D_FF_DENSE ** -0.5),
        "o_w_in": nrm(ks[18], (N_ODD_2, D, ODD_IN_COLS), D ** -0.5),
        "o_conv_w": nrm(ks[19], (N_ODD_2, CONV_WIDTH, 3 * GDN_WIDTH), CONV_WIDTH ** -0.5),
        "o_a_log": jnp.log(jax.random.uniform(ks[20], (N_ODD_2, GDN_HEADS), f32, minval=1.0, maxval=16.0)),
        "o_dt_bias": dt + jnp.log(-jnp.expm1(-dt)),
        "o_out_norm": 1.0 + nrm(ks[22], (N_ODD_2, GDN_HEAD_DIM), 0.02),
        "o_w_out": nrm(ks[23], (N_ODD_2, GDN_WIDTH, D), GDN_WIDTH ** -0.5),
        "o_router": nrm(ks[24], (N_ODD_2, D, N_EXPERTS), D ** -0.5),
        "o_moe_w_gate": nrm(ks[25], (N_ODD_2, N_EXPERTS, D, D_FF_EXPERT), D ** -0.5),
        "o_moe_w_up": nrm(ks[26], (N_ODD_2, N_EXPERTS, D, D_FF_EXPERT), D ** -0.5),
        "o_moe_w_down": nrm(ks[27], (N_ODD_2, N_EXPERTS, D_FF_EXPERT, D), D_FF_EXPERT ** -0.5),
    }

def second_block(x, ln_mix, ln_ffn,
              e_w_in, e_lru_conv_w, e_lru_conv_b, e_lru_w_a, e_lru_b_a, e_lru_w_i, e_lru_b_i,
              e_lru_lambda, e_q_norm, e_k_norm, e_sinks, e_w_out, e_ffn_w_gate, e_ffn_w_up, e_ffn_w_down,
              o_w_in, o_conv_w, o_a_log, o_dt_bias, o_out_norm, o_w_out, o_router,
              o_moe_w_gate, o_moe_w_up, o_moe_w_down):
    pos = jnp.arange(x.shape[1], dtype=jnp.int32)
    h = x
    for layer in range(DEPTH):
        j = layer // 2
        hn = rms_norm_2(h, ln_mix[layer])
        if layer % 2 == 0:
            h = h + even_mixer_2(hn, pos, e_w_in[j], e_lru_conv_w[j], e_lru_conv_b[j], e_lru_w_a[j],
                               e_lru_b_a[j], e_lru_w_i[j], e_lru_b_i[j], e_lru_lambda[j],
                               e_q_norm[j], e_k_norm[j], e_sinks[j], e_w_out[j]).astype(h.dtype)
            h = h + swiglu(rms_norm_2(h, ln_ffn[layer]), e_ffn_w_gate[j], e_ffn_w_up[j],
                           e_ffn_w_down[j]).astype(h.dtype)
        else:
            h = h + gated_deltanet(hn, o_w_in[j], o_conv_w[j], o_a_log[j], o_dt_bias[j],
                                   o_out_norm[j], o_w_out[j]).astype(h.dtype)
            h = h + moe_swiglu(rms_norm_2(h, ln_ffn[layer]), o_router[j], o_moe_w_gate[j],
                               o_moe_w_up[j], o_moe_w_down[j]).astype(h.dtype)
    return h


def setup_inputs(seed=0):
    out = dict(first_inputs(seed))
    for name, value in second_inputs(seed + 1).items():
        if name != "x":
            out[name + "_2"] = value
    return out


def reference(
    x, mem, positions, ev_norm, ev_w_in, mla_q_norm, mla_w_uq, mla_kv_norm, mla_w_ukv,
    mla_q_hnorm, mla_k_hnorm, rw_mu, rw_w0, rw_w2, rw_a0, rw_a2, rw_g2, rw_k_k, rw_k_a, rw_r_k,
    rw_ln_g, rw_ln_b, ev_w_out, od_norm, od_w_in, ssm_conv_w, ssm_conv_b, ssm_dt_bias,
    ssm_a_log, ssm_d, ssm_gnorm, od_w_out, xa_norm_x, xa_norm_mem, xa_wq, xa_wkv, xa_q_hnorm,
    xa_k_hnorm, xa_wo, ffn_norm, ffn_w13, ffn_w2, ln_mix_2, ln_ffn_2, e_w_in_2, e_lru_conv_w_2,
    e_lru_conv_b_2, e_lru_w_a_2, e_lru_b_a_2, e_lru_w_i_2, e_lru_b_i_2, e_lru_lambda_2,
    e_q_norm_2, e_k_norm_2, e_sinks_2, e_w_out_2, e_ffn_w_gate_2, e_ffn_w_up_2, e_ffn_w_down_2,
    o_w_in_2, o_conv_w_2, o_a_log_2, o_dt_bias_2, o_out_norm_2, o_w_out_2, o_router_2,
    o_moe_w_gate_2, o_moe_w_up_2, o_moe_w_down_2,
):
    x = first_block(
        x, mem, positions, ev_norm, ev_w_in, mla_q_norm, mla_w_uq, mla_kv_norm, mla_w_ukv,
        mla_q_hnorm, mla_k_hnorm, rw_mu, rw_w0, rw_w2, rw_a0, rw_a2, rw_g2, rw_k_k, rw_k_a,
        rw_r_k, rw_ln_g, rw_ln_b, ev_w_out, od_norm, od_w_in, ssm_conv_w, ssm_conv_b,
        ssm_dt_bias, ssm_a_log, ssm_d, ssm_gnorm, od_w_out, xa_norm_x, xa_norm_mem, xa_wq,
        xa_wkv, xa_q_hnorm, xa_k_hnorm, xa_wo, ffn_norm, ffn_w13, ffn_w2,
    )
    return second_block(
        x, ln_mix_2, ln_ffn_2, e_w_in_2, e_lru_conv_w_2, e_lru_conv_b_2, e_lru_w_a_2,
        e_lru_b_a_2, e_lru_w_i_2, e_lru_b_i_2, e_lru_lambda_2, e_q_norm_2, e_k_norm_2,
        e_sinks_2, e_w_out_2, e_ffn_w_gate_2, e_ffn_w_up_2, e_ffn_w_down_2, o_w_in_2,
        o_conv_w_2, o_a_log_2, o_dt_bias_2, o_out_norm_2, o_w_out_2, o_router_2, o_moe_w_gate_2,
        o_moe_w_up_2, o_moe_w_down_2,
    )


_drawn_inputs = setup_inputs


def setup_inputs(seed=0):
    import zlib

    import numpy as np

    out = dict(_drawn_inputs(seed))
    spreads = {}
    factors = {'mla_q_norm': 3.19,
     'mla_q_hnorm': 3.383,
     'mla_k_hnorm': 4.449,
     'xa_norm_x': 3.919,
     'xa_norm_mem': 2.769,
     'xa_q_hnorm': 3.499,
     'xa_k_hnorm': 3.944,
     'ln_mix_2': 2.69,
     'ln_ffn_2': 2.677,
     'e_lru_b_a_2': 8.0,
     'e_lru_b_i_2': 4.09,
     'e_q_norm_2': 8.0,
     'e_k_norm_2': 8.0,
     'e_sinks_2': 24.368,
     'o_out_norm_2': 21.594}
    for name, (base, spread) in spreads.items():
        noise = np.random.default_rng([zlib.crc32(name.encode()), seed]).standard_normal(out[name].shape)
        drawn = base * np.exp(spread * noise) if base else spread * noise
        out[name] = jnp.asarray(drawn.astype(out[name].dtype))
    for name, factor in factors.items():
        out[name] = (out[name] * factor).astype(out[name].dtype)
    return out
```

```python
from contextlib import ExitStack

import numpy as np
import concourse.bass as bass
from concourse import mybir

F32 = mybir.dt.float32
F32R = mybir.dt.float32r
I32 = mybir.dt.int32
U32 = mybir.dt.uint32
ALU = mybir.AluOpType
ACT = mybir.ActivationFunctionType
AX = mybir.AxisListType.X

P = 128
T = 256
TT = T // P
D = 1024
KD = D // P
EPS = 1e-6
NEG = -1e30
LEVELS = [2, 4, 8, 16, 32, 64]
BANKS = 8
BANK = 512
SLOTS = 4
SLOT = 4096
UNIT = 6144
TWO_PI = 2 * np.pi
PI_C1 = 6.28125
PI_C2 = float(np.float32(TWO_PI - PI_C1))
ROUND = 1.5 * 2.0 ** 23


def shape_constants():
    p = np.arange(P)[:, None]
    f = np.arange(P)[None, :]
    q = (np.arange(TT)[None, :, None] * P + p[:, :, None])
    k = np.arange(T)[None, None, :]
    parts = {}
    parts["ident"] = (p == f)
    parts["ones"] = np.ones((P, P))
    parts["upto"] = (p <= f)
    parts["before"] = (p < f)
    parts["upto_mid"] = (p <= f) * 1.0 - (p < P // 2)
    parts["halves"] = np.stack([np.arange(P) < P // 2, np.arange(P) >= P // 2], 1)
    parts["after_neg"] = np.where(p <= f, 0.0, NEG)
    parts["pair_t"] = (p // 2 == f // 2) & (p % 2 == 0) & (f % 2 == 1)
    parts["pair"] = parts["pair_t"].T
    for s in LEVELS:
        parts[f"level{s}"] = (p // (2 * s) == f // (2 * s)) & (p % (2 * s) < s) & (f % (2 * s) >= s)
    parts["quad"] = np.concatenate([p < f, p <= f, p < f, p <= f], 1)
    parts["causal"] = np.where(k <= q, 0.0, NEG).reshape(P, TT * T)
    parts["band"] = np.where((k <= q) & (q - k < 128), 0.0, NEG).reshape(P, TT * T)
    inv16 = np.float32(10000.0) ** (-np.arange(16, dtype=np.float32) / np.float32(16))
    parts["inv_freq"] = np.broadcast_to(inv16.astype(np.float32)[None], (P, 16))
    inv32 = np.float32(10000.0) ** (-np.arange(32, dtype=np.float32) / np.float32(32))
    ang = (q[:, :, 0].astype(np.float32)[:, :, None] * inv32.astype(np.float32)).astype(np.float32)
    parts["rope_cos"] = np.cos(ang).reshape(P, -1)
    parts["rope_sin"] = np.sin(ang).reshape(P, -1)
    parts["ramp"] = np.broadcast_to(f, (P, P))
    parts["minus_half"] = np.full((P, 16), -0.5)
    at, where = 0, {}
    for name, a in parts.items():
        where[name] = (at, a.shape[1])
        at += a.shape[1]
    return np.concatenate([np.asarray(a, np.float32) for a in parts.values()], 1), where


CONSTANTS, CONST_AT = shape_constants()


class Lane:

    def __init__(self, new_semaphore, engine):
        self.new_semaphore, self.engine, self.sem, self.count = new_semaphore, engine, None, 0

    def enter(self, stage):
        self.sem, self.count = self.new_semaphore(f"{stage}_{self.engine}_done"), 0

    def tick(self):
        self.count += 1
        return self.sem, 1

    def at(self):
        return self.sem, self.count


class Bank:

    def __init__(self, ap):
        self.ap, self.free = ap, None


class Slot:

    def __init__(self, ap, sem):
        self.ap, self.sem, self.loads, self.free = ap, sem, 0, None


def build(nc, a, out, stages=None):
    with ExitStack() as ctx:
        def new_semaphore(name):
            return ctx.enter_context(nc.semaphore(name))

        def sb(name, cols, dt=F32):
            return ctx.enter_context(nc.sbuf_tensor(name, [P, cols], dt))

        consts = sb("consts", CONSTANTS.shape[1])
        h_sb = sb("h", TT * D)
        xT_sb = sb("xT", KD * T)
        memT_sb = sb("memT", KD * T)
        ring = sb("ring", SLOTS * SLOT)
        ARENA = 27040
        arena_base = nc.sbuf_base
        arena = sb("arena", ARENA)
        psum = ctx.enter_context(nc.psum_tensor("banks", [P, BANKS * BANK], F32))

        h = h_sb[:].rearrange("p (t d) -> p t d", t=TT)
        xT = xT_sb[:].rearrange("p (k t) -> p k t", t=T)
        memT = memT_sb[:].rearrange("p (k t) -> p k t", t=T)

        def const(name):
            at, n = CONST_AT[name]
            return consts[:, at:at + n]

        ident = const("ident")
        banks = [Bank(psum[:, b * BANK:(b + 1) * BANK]) for b in range(BANKS)]
        turn = [0]

        def take_bank():
            turn[0] += 1
            return banks[(turn[0] - 1) % BANKS]

        slots = [Slot(ring[:, s * SLOT:(s + 1) * SLOT], new_semaphore(f"ring{s}_landed")) for s in range(SLOTS)]
        slot_turn = [0]

        top = [0]

        def room(cols, dt=F32):
            ap = arena[:, top[0]:top[0] + cols]
            top[0] += cols
            assert top[0] <= ARENA, top[0]
            return ap if dt == F32 else ap.bitcast(dt)

        def room3(n, m):
            return room(n * m).rearrange("p (n m) -> p n m", m=m)

        V, S, M, G = (Lane(new_semaphore, n) for n in ("vector", "scalar", "tensor", "gpsimd"))
        block = ctx.enter_context(nc.Block())
        waited = {}

        def unseen(eng, *marks):
            for m in marks:
                if isinstance(m, list):
                    yield from unseen(eng, *m)
                elif m is not None and m[1] > waited.get((eng.engine, m[0].name), 0):
                    waited[eng.engine, m[0].name] = m[1]
                    yield m

        def enter(stage, keep=0):
            before = [lane.at() for lane in (V, S, M, G) if lane.count]
            for lane in (V, S, M, G):
                lane.enter(stage)

            @block.vector
            def _(dve):
                for due in unseen(dve, before):
                    dve.wait_ge(*due)

            @block.scalar
            def _(act):
                for due in unseen(act, before):
                    act.wait_ge(*due)

            @block.tensor
            def _(pe):
                for due in unseen(pe, before):
                    pe.wait_ge(*due)

            @block.gpsimd
            def _(pool):
                for due in unseen(pool, before):
                    pool.wait_ge(*due)

            top[0] = keep

        class Params:

            def __init__(self, stage):
                self.sem, self.loads = new_semaphore(f"{stage}_params_landed"), 0

            def load(self, dst, src):
                self.loads += 1

                @block.gpsimd
                def _(pool):
                    pool.dma_start(dst, src, allow_slow_non_contiguous=True).then_inc(self.sem, 16)
                return dst

            def rows(self, src, n):
                return self.load(room(n), src.partition_broadcast(P))

            def cols(self, src, n):
                return self.load(room(n // P), src.rearrange("(k p) -> p k", p=P))

            def landed(self):
                return self.sem, 16 * self.loads

        def load_weights(src, shape3):
            slot = slots[slot_turn[0] % SLOTS]
            slot_turn[0] += 1
            n = shape3[1] * shape3[2]
            view = slot.ap[0:shape3[0], 0:n].rearrange("p (k n) -> p k n", n=shape3[2])

            @block.sync
            def _(sp):
                for due in unseen(sp, slot.free):
                    sp.wait_ge(*due)
                sp.dma_start(view, src.rearrange("(k p) n -> p k n", p=shape3[0])).then_inc(slot.sem, 16)
            slot.loads += 1
            return slot, view, (slot.sem, 16 * slot.loads)

        def transpose_tiles(src, n_k, ready, dst, gain=None, gain_ready=None):
            marks = []
            for k0 in range(0, n_k, 2):
                ks = range(k0, min(k0 + 2, n_k))
                bank = take_bank()

                @block.tensor
                def _(pe):
                    for due in unseen(pe, bank.free, ready):
                        pe.wait_ge(*due)
                    for k in ks:
                        for t in range(TT):
                            at = (k - k0) * T + t * P
                            last = pe.transpose(bank.ap[:, at:at + P], src[:, t, k * P:(k + 1) * P], ident)
                    last.then_inc(*M.tick())
                turned = M.at()

                if gain is None:
                    @block.scalar
                    def _(act):
                        act.wait_ge(*turned)
                        act.copy(dst[:, k0:k0 + len(ks), :],
                                 bank.ap[:, 0:len(ks) * T].rearrange("p (k t) -> p k t", t=T)).then_inc(*S.tick())
                    bank.free = S.at()
                else:
                    @block.vector
                    def _(dve):
                        for due in unseen(dve, gain_ready):
                            dve.wait_ge(*due)
                        dve.wait_ge(*turned)
                        for k in ks:
                            dve.tensor_scalar(dst[:, k, :], bank.ap[:, (k - k0) * T:(k - k0 + 1) * T],
                                              gain[:, k:k + 1], None, ALU.mult).then_inc(*V.tick())
                    bank.free = V.at()
            return V.at() if gain is not None else S.at()

        def reciprocal_root(x, n, ready):
            @block.gpsimd
            def _(pool):
                for due in unseen(pool, ready):
                    pool.wait_ge(*due)
                pool.tensor_tensor(x, x, const("minus_half")[:, 0:n], ALU.pow).then_inc(*G.tick())
            return G.at()

        def row_rstd(src, n, ready, eps=EPS):
            square = room(n)
            rstd = room(TT)

            @block.scalar
            def _(act):
                for due in unseen(act, ready):
                    act.wait_ge(*due)
                for t in range(TT):
                    for due in unseen(act, S.at() if t else None):
                        act.wait_ge(*due)
                    act.activation(square, src[:, t, :], ACT.Square, accum_out=rstd[:, t:t + 1]).then_inc(*S.tick())
            summed = S.at()

            @block.vector
            def _(dve):
                dve.wait_ge(*summed)
                dve.tensor_scalar(rstd, rstd, 1.0 / n, eps, ALU.mult, ALU.add).then_inc(*V.tick())
            return rstd, reciprocal_root(rstd, TT, V.at())

        def norm_turned(src, n, ready, dst, gain, gain_ready, eps=EPS):
            n_k = n // P
            rstd, have = row_rstd(src, n, ready, eps)
            scaled = room3(TT, n)

            @block.vector
            def _(dve):
                dve.wait_ge(*have)
                for t in range(TT):
                    dve.tensor_scalar(scaled[:, t, :], src[:, t, :], rstd[:, t:t + 1], None,
                                      ALU.mult).then_inc(*V.tick())
            return transpose_tiles(scaled, n_k, V.at(), dst, gain, gain_ready)

        def project(lhs, n_k, w, n_cols, ready, take, first_col=0, rows=P):
            chunk = 512 if n_k <= 8 else 256
            for c0 in range(0, n_cols, chunk):
                n = min(chunk, n_cols - c0)
                slot, view, landed = load_weights(w[:, first_col + c0:first_col + c0 + n], (rows, n_k, n))
                for t in range(TT):
                    bank = take_bank()

                    @block.tensor
                    def _(pe):
                        for due in unseen(pe, bank.free, ready, landed):
                            pe.wait_ge(*due)
                        for k in range(n_k):
                            last = pe.matmul(bank.ap[:, 0:n], lhs[0:rows, k, t * P:(t + 1) * P], view[:, k, :],
                                             start=(k == 0), stop=(k == n_k - 1))
                        last.then_inc(*M.tick())
                    slot.free = M.at()
                    bank.free = take(bank.ap[:, 0:n], M.at(), t, c0, n)

        flip = [0]

        def copy_out(dst):
            def take(ps, mark, t, c0, n):
                flip[0] += 1
                if flip[0] % 2:
                    @block.scalar
                    def _(act):
                        act.wait_ge(*mark)
                        act.copy(dst[:, t, c0:c0 + n], ps).then_inc(*S.tick())
                    return S.at()

                @block.vector
                def _(dve):
                    dve.wait_ge(*mark)
                    dve.tensor_copy(dst[:, t, c0:c0 + n], ps).then_inc(*V.tick())
                return V.at()
            return take

        def add_to_h(ps, mark, t, c0, n):
            @block.vector
            def _(dve):
                dve.wait_ge(*mark)
                dve.tensor_tensor(h[:, t, c0:c0 + n], h[:, t, c0:c0 + n], ps, ALU.add).then_inc(*V.tick())
            return V.at()

        def both():
            return [V.at(), S.at()]

        def per_head_rstd(x, n_heads, width, ready, mean, eps, scratch):
            r = room(n_heads)

            @block.vector
            def _(dve):
                for due in unseen(dve, ready):
                    dve.wait_ge(*due)
                dve.tensor_tensor(scratch, x, x, ALU.mult).then_inc(*V.tick())
                dve.wait_ge(*V.at())
                dve.tensor_reduce(r, scratch, AX, ALU.add).then_inc(*V.tick())
                dve.wait_ge(*V.at())
                dve.tensor_scalar(r, r, 1.0 / width if mean else 1.0, eps, ALU.mult, ALU.add).then_inc(*V.tick())
            return r, reciprocal_root(r, n_heads, V.at())

        def head_norm(x, n_heads, width, ready, gain, scratch):
            r, have = per_head_rstd(x, n_heads, width, ready, True, EPS, scratch)

            @block.vector
            def _(dve):
                dve.wait_ge(*have)
                dve.tensor_tensor(x, x, r.unsqueeze(2).to_broadcast([P, n_heads, width]), ALU.mult).then_inc(*V.tick())
                dve.wait_ge(*V.at())
                dve.tensor_tensor(x, x, gain.unsqueeze(1).to_broadcast([P, n_heads, width]), ALU.mult).then_inc(*V.tick())
            return V.at()

        def rotate(x1, x2, cos, sin, shape, ready, scratch):
            a1, a2 = scratch

            @block.vector
            def _(dve):
                for due in unseen(dve, ready):
                    dve.wait_ge(*due)
                dve.tensor_tensor(a1, x2, sin, ALU.mult).then_inc(*V.tick())
                dve.tensor_tensor(a2, x1, sin, ALU.mult).then_inc(*V.tick())
                dve.wait_ge(*V.at())
                dve.tensor_tensor(x1, x1, cos, ALU.mult).then_inc(*V.tick())
                dve.tensor_tensor(x2, x2, cos, ALU.mult).then_inc(*V.tick())
                dve.wait_ge(*V.at())
                dve.tensor_tensor(x1, x1, a1, ALU.subtract).then_inc(*V.tick())
                dve.tensor_tensor(x2, x2, a2, ALU.add).then_inc(*V.tick())
            return V.at()

        def attention(q, k, v, heads, d, dv, scale, y, ready, mask=None, causal=False, sink=None):
            bufs = [{n: room(512) for n in ("qk", "s", "p", "pt")} | {n: room(TT) for n in ("m", "nm", "sum", "es")}
                    for _ in range(2)]
            used = [None, None]

            def scores(i):
                b = bufs[i % 2]
                bank = take_bank()

                @block.tensor
                def _(pe):
                    for due in unseen(pe, bank.free, ready):
                        pe.wait_ge(*due)
                    for j, x in enumerate((q, k)):
                        for t in range(TT):
                            at = j * T + t * P
                            last = pe.transpose(bank.ap[0:d, at:at + P], x(t, i), ident)
                    last.then_inc(*M.tick())
                turned = M.at()

                @block.scalar
                def _(act):
                    for due in unseen(act, used[i % 2]):
                        act.wait_ge(*due)
                    act.wait_ge(*turned)
                    act.copy(b["qk"][0:d, :], bank.ap[0:d, :]).then_inc(*S.tick())
                bank.free = S.at()
                copied = S.at()
                bank2 = take_bank()

                @block.tensor
                def _(pe):
                    for due in unseen(pe, bank2.free):
                        pe.wait_ge(*due)
                    pe.wait_ge(*copied)
                    for t in range(TT):
                        last = pe.matmul(bank2.ap[:, t * T:(t + 1) * T], b["qk"][0:d, t * P:(t + 1) * P],
                                         b["qk"][0:d, T:2 * T], start=True, stop=True)
                    last.then_inc(*M.tick())
                have = M.at()
                sv = b["s"].rearrange("p (t k) -> p t k", t=TT)

                @block.vector
                def _(dve):
                    for due in unseen(dve, used[i % 2]):
                        dve.wait_ge(*due)
                    dve.wait_ge(*have)
                    if mask is not None:
                        dve.scalar_tensor_tensor(out=b["s"], in0=bank2.ap, scalar=scale, in1=mask,
                                                 op0=ALU.mult, op1=ALU.add).then_inc(*V.tick())
                    else:
                        dve.tensor_scalar(b["s"], bank2.ap, scale, None, ALU.mult).then_inc(*V.tick())
                    dve.wait_ge(*V.at())
                    dve.tensor_reduce(b["m"], sv, AX, ALU.max).then_inc(*V.tick())
                    dve.wait_ge(*V.at())
                    if sink is not None:
                        dve.tensor_scalar(b["m"], b["m"], sink[:, i:i + 1], None, ALU.max).then_inc(*V.tick())
                        dve.wait_ge(*V.at())
                    dve.tensor_scalar(b["nm"], b["m"], -1.0, None, ALU.mult).then_inc(*V.tick())
                bank2.free = V.at()
                have = V.at()

                @block.scalar
                def _(act):
                    act.wait_ge(*have)
                    for t in range(TT):
                        act.activation(b["p"][:, t * T:(t + 1) * T], sv[:, t, :], ACT.Exp, bias=b["nm"][:, t:t + 1],
                                       accum_out=b["sum"][:, t:t + 1]).then_inc(*S.tick())
                    if sink is not None:
                        act.activation(b["es"], b["nm"], ACT.Exp, bias=sink[:, i:i + 1]).then_inc(*S.tick())
                have = S.at()

                @block.vector
                def _(dve):
                    dve.wait_ge(*have)
                    if sink is not None:
                        dve.tensor_tensor(b["sum"], b["sum"], b["es"], ALU.add).then_inc(*V.tick())
                        dve.wait_ge(*V.at())
                    dve.reciprocal(b["sum"], b["sum"]).then_inc(*V.tick())
                return have, V.at()

            def values(i, weights, inverse):
                b = bufs[i % 2]
                bank = take_bank()

                @block.tensor
                def _(pe):
                    for due in unseen(pe, bank.free, weights):
                        pe.wait_ge(*due)
                    for kt in range(TT):
                        for t in range(TT):
                            at = kt * T + t * P
                            last = pe.transpose(bank.ap[:, at:at + P], b["p"][:, t * T + kt * P:t * T + (kt + 1) * P],
                                                ident)
                    last.then_inc(*M.tick())
                turned = M.at()

                @block.scalar
                def _(act):
                    act.wait_ge(*turned)
                    act.copy(b["pt"], bank.ap).then_inc(*S.tick())
                bank.free = S.at()
                copied = S.at()
                bank2 = take_bank()

                @block.tensor
                def _(pe):
                    for due in unseen(pe, bank2.free):
                        pe.wait_ge(*due)
                    pe.wait_ge(*copied)
                    for t in range(TT):
                        kts = range(t + 1) if causal else range(TT)
                        for kt in kts:
                            at = kt * T + t * P
                            last = pe.matmul(bank2.ap[:, t * dv:(t + 1) * dv], b["pt"][:, at:at + P], v(kt, i),
                                             start=(kt == 0), stop=(kt == kts[-1]))
                    last.then_inc(*M.tick())
                have = M.at()

                @block.vector
                def _(dve):
                    for due in unseen(dve, inverse):
                        dve.wait_ge(*due)
                    dve.wait_ge(*have)
                    dve.tensor_tensor(y(i), bank2.ap[:, 0:TT * dv].rearrange("p (t n) -> p t n", t=TT),
                                      b["sum"].unsqueeze(2).to_broadcast([P, TT, dv]), ALU.mult).then_inc(*V.tick())
                bank2.free = V.at()
                used[i % 2] = V.at()

            waiting = None
            for i in range(heads + 1):
                now = scores(i) if i < heads else None
                if waiting is not None:
                    values(i - 1, *waiting)
                waiting = now
            return V.at()

        def invert(groups):
            r4 = lambda ap: ap.rearrange("p (g n) -> p g n", g=4)
            wide = lambda ap: ap.unsqueeze(1).to_broadcast([P, 4, P])
            for g in groups:
                @block.vector
                def _(dve):
                    for due in unseen(dve, g["ready"]):
                        dve.wait_ge(*due)
                    dve.tensor_tensor(r4(g["X"]), r4(g["N"].ap), wide(const("pair")), ALU.mult).then_inc(*V.tick())
                    dve.tensor_tensor(r4(g["XT"]), g["NT"], wide(const("pair_t")), ALU.mult).then_inc(*V.tick())
                    dve.wait_ge(*V.at())
                    dve.tensor_tensor(r4(g["X"]), r4(g["X"]), wide(ident), ALU.add).then_inc(*V.tick())
                    dve.tensor_tensor(r4(g["XT"]), r4(g["XT"]), wide(ident), ALU.add).then_inc(*V.tick())
                g["N"].free = V.at()
                g["have"] = V.at()
            for n, s in enumerate(LEVELS):
                for g in groups:
                    @block.gpsimd
                    def _(pool):
                        for due in unseen(pool, g["ready"], g.get("level_used")):
                            pool.wait_ge(*due)
                        pool.tensor_tensor(r4(g["NL"]), g["NT"], wide(const(f"level{s}")), ALU.mult).then_inc(*G.tick())
                    level = G.at()
                    bank = take_bank()

                    @block.tensor
                    def _(pe):
                        for due in unseen(pe, bank.free, level, g["have"]):
                            pe.wait_ge(*due)
                        for j in range(4):
                            c = slice(j * P, (j + 1) * P)
                            last = pe.matmul(bank.ap[:, c], g["NL"][:, c], g["X"][:, c], start=True, stop=True)
                        last.then_inc(*M.tick())
                    g["level_used"] = M.at()
                    have = M.at()

                    @block.scalar
                    def _(act):
                        for due in unseen(act, g.get("y_used")):
                            act.wait_ge(*due)
                        act.wait_ge(*have)
                        act.copy(g["Y"], bank.ap).then_inc(*S.tick())
                    bank.free = S.at()
                    have = S.at()
                    bz, bzt = take_bank(), take_bank()
                    final = n == len(LEVELS) - 1

                    @block.tensor
                    def _(pe):
                        for due in unseen(pe, bz.free, bzt.free):
                            pe.wait_ge(*due)
                        pe.wait_ge(*have)
                        for j in range(4):
                            c = slice(j * P, (j + 1) * P)
                            if not final:
                                pe.matmul(bz.ap[:, c], g["XT"][:, c], g["Y"][:, c], start=True, stop=True)
                            last = pe.matmul(bzt.ap[:, c], g["Y"][:, c], g["XT"][:, c], start=True, stop=True)
                        last.then_inc(*M.tick())
                    have = M.at()
                    g["y_used"] = M.at()

                    @block.vector
                    def _(dve):
                        dve.wait_ge(*have)
                        if not final:
                            dve.tensor_tensor(g["X"], g["X"], bz.ap, ALU.add).then_inc(*V.tick())
                        dve.tensor_tensor(g["XT"], g["XT"], bzt.ap, ALU.add).then_inc(*V.tick())
                    if not final:
                        bz.free = V.at()
                    bzt.free = V.at()
                    g["have"] = V.at()

        def mla_and_rwkv():
            QR, KVR, RO, NO, HD = 384, 256, 32, 64, 96
            H = 8
            RW = 512
            MI = QR + KVR + RO
            IN = MI + 3 * RW + 256
            enter("mix0")
            par = Params("mix0")
            g_in = par.cols(a["ev_norm"][0], D)
            g_q = par.cols(a["mla_q_norm"][0], QR)
            g_kv = par.cols(a["mla_kv_norm"][0], KVR)
            gh_q = par.rows(a["mla_q_hnorm"][0], HD)
            gh_k = par.rows(a["mla_k_hnorm"][0], HD)
            pos = par.load(room(TT, I32), a["positions"][0].rearrange("(t p) -> p t", p=P))
            proj = room3(TT, IN)
            y = room3(TT, D)
            keep = top[0]
            normed = norm_turned(h, D, None, xT, g_in, par.landed())
            project(xT, KD, a["ev_w_in"][0], IN, normed, copy_out(proj))
            have = both()

            top[0] = keep
            cqT = room(3 * T).rearrange("p (k t) -> p k t", t=T)
            ckvT = room(2 * T).rearrange("p (k t) -> p k t", t=T)
            q = room3(TT, H * HD)
            kv = room3(TT, H * 128)
            k = room3(TT, H * HD)
            ang = room3(TT, 16)
            turns = room3(TT, 16)
            tables = [room3(TT, 16), room3(TT, 16)]
            posf = room(TT)

            @block.vector
            def _(dve):
                dve.wait_ge(*par.landed())
                for due in unseen(dve, have):
                    dve.wait_ge(*due)
                dve.tensor_copy(posf, pos).then_inc(*V.tick())
                dve.wait_ge(*V.at())
                for t in range(TT):
                    dve.tensor_scalar(ang[:, t, :], const("inv_freq"), posf[:, t:t + 1], None, ALU.mult).then_inc(*V.tick())
                dve.wait_ge(*V.at())
                dve.tensor_scalar(turns, ang, 1 / TWO_PI, ROUND, ALU.mult, ALU.add).then_inc(*V.tick())
                dve.wait_ge(*V.at())
                dve.tensor_scalar(turns, turns, ROUND, None, ALU.subtract).then_inc(*V.tick())
                dve.wait_ge(*V.at())
                for c in (PI_C1, PI_C2):
                    dve.scalar_tensor_tensor(out=ang, in0=turns, scalar=-c, in1=ang, op0=ALU.mult,
                                             op1=ALU.add).then_inc(*V.tick())
                    dve.wait_ge(*V.at())
                dve.tensor_scalar(tables[0], ang, np.pi / 2, None, ALU.add).then_inc(*V.tick())
                dve.wait_ge(*V.at())
                dve.tensor_scalar(turns, tables[0], np.pi, -TWO_PI, ALU.is_gt, ALU.mult).then_inc(*V.tick())
                dve.wait_ge(*V.at())
                dve.tensor_tensor(tables[0], tables[0], turns, ALU.add).then_inc(*V.tick())
                dve.wait_ge(*V.at())
                for x, o in ((tables[0], tables[0]), (ang, tables[1])):
                    dve.tensor_scalar(o, x, 3.1415925, -3.1415925, ALU.min, ALU.max).then_inc(*V.tick())
            reduced = V.at()

            @block.scalar
            def _(act):
                act.wait_ge(*reduced)
                for x in tables:
                    act.activation(x, x, ACT.Sin).then_inc(*S.tick())
            rope_ready = S.at()

            n1 = norm_turned(proj[:, :, 0:QR], QR, have, cqT, g_q, par.landed())
            project(cqT, 3, a["mla_w_uq"][0], H * HD, n1, copy_out(q))
            q_have = both()
            n2 = norm_turned(proj[:, :, QR:QR + KVR], KVR, have, ckvT, g_kv, par.landed())
            project(ckvT, 2, a["mla_w_ukv"][0], H * 128, n2, copy_out(kv))
            kv_have = both()
            kvh = [kv[:, t, :].rearrange("p (h n) -> p h n", h=H) for t in range(TT)]
            qh = [q[:, t, :].rearrange("p (h n) -> p h n", h=H) for t in range(TT)]
            kh = [k[:, t, :].rearrange("p (h n) -> p h n", h=H) for t in range(TT)]

            @block.gpsimd
            def _(pool):
                for due in unseen(pool, kv_have):
                    pool.wait_ge(*due)
                for t in range(TT):
                    pool.tensor_copy(kh[t][:, :, 0:NO], kvh[t][:, :, 0:NO]).then_inc(*G.tick())
                    pool.tensor_copy(kh[t][:, :, NO:HD], proj[:, t, QR + KVR:MI].unsqueeze(1).to_broadcast([P, H, RO])
                                     ).then_inc(*G.tick())
            k_have = G.at()
            scratch = room(TT * H * HD).rearrange("p (n m) -> p n m", m=HD)
            flat = lambda x: x.rearrange("p t (h n) -> p (t h) n", n=HD)
            done_q = head_norm(flat(q), TT * H, HD, q_have, gh_q, scratch)
            done_k = head_norm(flat(k), TT * H, HD, k_have, gh_k, scratch)
            hs = [room(H * 16).rearrange("p (h n) -> p h n", h=H) for _ in range(2)]
            for xh in (qh, kh):
                for t in range(TT):
                    cos, sin = (x[:, t, :].unsqueeze(1).to_broadcast([P, H, 16]) for x in tables)
                    rotated = rotate(xh[t][:, :, NO:NO + 16], xh[t][:, :, NO + 16:HD], cos, sin, None,
                                     [done_q, done_k, rope_ready, V.at()], hs)
            attention(lambda t, i: qh[t][:, i, :], lambda t, i: kh[t][:, i, :], lambda t, i: kvh[t][:, i, NO:128],
                      H, HD, 64, HD ** -0.5, lambda i: y[:, :, i * 64:(i + 1) * 64], rotated,
                      mask=const("causal"), causal=True)

            rwkv(proj[:, :, MI:IN], y[:, :, RW:2 * RW], keep)
            turned = transpose_tiles(y, KD, both(), xT)
            project(xT, KD, a["ev_w_out"][0], D, turned, add_to_h)

        def rwkv(p, y, keep):
            RW, H, N = 512, 8, 64
            enter("rwkv", keep)
            par = Params("rwkv")
            names = ("rw_w0", "rw_a0", "rw_k_k", "rw_k_a", "rw_ln_g", "rw_ln_b")
            dead_rows = arena[:, top[0]:top[0] + 4 * RW]
            rows = {n: par.rows(a[n][0], RW) for n in names}
            r_k = par.rows(a["rw_r_k"][0].rearrange("h n -> (h n)"), RW)
            decay, lr, gate, kk = (room3(TT, RW) for _ in range(4))
            base = top[0]
            w2a2 = [par.load(room(RW)[0:64, :], a[n][0]) for n in ("rw_w2", "rw_a2")]
            g2 = par.load(room(RW), a["rw_g2"][0])
            mark0 = top[0]
            mu = par.rows(a["rw_mu"][0], 3 * RW + 256)
            prev = room3(TT, 3 * RW + 256)
            shift_sem = new_semaphore("rwkv_shift_landed")

            @block.vector
            def _(dve):
                dve.memset(prev[0:1, 0, :], 0.0).then_inc(*V.tick())
            zeroed = V.at()

            @block.scalar
            def _(act):
                act.dma_start(prev[1:P, 0, :], p[0:P - 1, 0, :]).then_inc(shift_sem, 16)
                act.dma_start(prev[1:P, 1, :], p[0:P - 1, 1, :]).then_inc(shift_sem, 16)
                act.dma_start(prev[0:1, 1, :], p[P - 1:P, 0, :]).then_inc(shift_sem, 16)

            @block.vector
            def _(dve):
                for due in unseen(dve, (shift_sem, 48)):
                    dve.wait_ge(*due)
                dve.wait_ge(*par.landed())
                dve.wait_ge(*zeroed)
                dve.tensor_tensor(prev, prev, p, ALU.subtract).then_inc(*V.tick())
                dve.wait_ge(*V.at())
                dve.tensor_tensor(prev, prev, mu.unsqueeze(1).to_broadcast([P, TT, 3 * RW + 256]), ALU.mult).then_inc(*V.tick())
                dve.wait_ge(*V.at())
                dve.tensor_tensor(p, p, prev, ALU.add).then_inc(*V.tick())
            shifted = V.at()
            top[0] = mark0
            r, k, v = (p[:, :, i * RW:(i + 1) * RW] for i in range(3))
            lora = p[:, :, 3 * RW:]

            @block.scalar
            def _(act):
                for due in unseen(act, shifted):
                    act.wait_ge(*due)
                act.activation(lora[:, :, 0:64], lora[:, :, 0:64], ACT.Tanh).then_inc(*S.tick())
                act.activation(lora[:, :, 128:256], lora[:, :, 128:256], ACT.Sigmoid).then_inc(*S.tick())
            squashed = S.at()
            lT = room(3 * T).rearrange("p (k t) -> p k t", t=T)
            widths = (64, 64, 128)
            for j, w in enumerate(widths):
                bank = take_bank()

                @block.tensor
                def _(pe):
                    for due in unseen(pe, bank.free):
                        pe.wait_ge(*due)
                    pe.wait_ge(*squashed)
                    for t in range(TT):
                        last = pe.transpose(bank.ap[0:w, t * P:(t + 1) * P], lora[:, t, j * 64:j * 64 + w], ident)
                    last.then_inc(*M.tick())
                turned = M.at()

                @block.vector
                def _(dve):
                    for due in unseen(dve, shifted):
                        dve.wait_ge(*due)
                    dve.wait_ge(*turned)
                    dve.tensor_copy(lT[0:w, j, :], bank.ap[0:w, 0:T]).then_inc(*V.tick())
                bank.free = V.at()
            turned = V.at()
            for j, (w, dst, bias) in enumerate(((64, decay, rows["rw_w0"]), (64, lr, rows["rw_a0"]), (128, gate, None))):
                wt = w2a2[j] if j < 2 else g2
                for t in range(TT):
                    bank = take_bank()

                    @block.tensor
                    def _(pe):
                        for due in unseen(pe, bank.free):
                            pe.wait_ge(*due)
                        pe.wait_ge(*turned)
                        pe.wait_ge(*par.landed())
                        pe.matmul(bank.ap, lT[0:w, j, t * P:(t + 1) * P], wt[0:w, :], start=True, stop=True).then_inc(*M.tick())
                    have = M.at()

                    @block.vector
                    def _(dve):
                        dve.wait_ge(*have)
                        if bias is not None:
                            dve.tensor_tensor(dst[:, t, :], bank.ap, bias, ALU.add).then_inc(*V.tick())
                        else:
                            dve.tensor_copy(dst[:, t, :], bank.ap).then_inc(*V.tick())
                    bank.free = V.at()
            have = V.at()

            @block.scalar
            def _(act):
                act.wait_ge(*have)
                act.activation(decay, decay, ACT.Sigmoid).then_inc(*S.tick())
                act.activation(lr, lr, ACT.Sigmoid).then_inc(*S.tick())
            sig = S.at()
            scratch = room3(TT, RW)
            by_head = lambda x: x.rearrange("p t (h n) -> p (t h) n", n=N)
            both_tiles = lambda x: x.unsqueeze(1).to_broadcast([P, TT, RW])
            norm = room(TT * H)

            @block.vector
            def _(dve):
                dve.wait_ge(*sig)
                dve.tensor_scalar(decay, decay, -float(np.exp(-0.5)), None, ALU.mult).then_inc(*V.tick())
                dve.tensor_tensor(kk, k, both_tiles(rows["rw_k_k"]), ALU.mult).then_inc(*V.tick())
                dve.wait_ge(*V.at())
                dve.tensor_tensor(scratch, kk, kk, ALU.mult).then_inc(*V.tick())
                dve.wait_ge(*V.at())
                dve.tensor_reduce(norm, by_head(scratch), AX, ALU.add).then_inc(*V.tick())
                dve.wait_ge(*V.at())
                dve.tensor_scalar(norm, norm, 1e-24, None, ALU.max).then_inc(*V.tick())
                dve.tensor_scalar(scratch, lr, 1.0, None, ALU.subtract).then_inc(*V.tick())
                dve.wait_ge(*V.at())
                dve.tensor_tensor(scratch, scratch, both_tiles(rows["rw_k_a"]), ALU.mult).then_inc(*V.tick())
                dve.wait_ge(*V.at())
                dve.scalar_tensor_tensor(out=k, in0=scratch, scalar=1.0, in1=k, op0=ALU.add, op1=ALU.mult).then_inc(*V.tick())
            log_decay = V.at()
            root = reciprocal_root(norm, TT * H, V.at())

            @block.vector
            def _(dve):
                dve.wait_ge(*root)
                dve.tensor_tensor(by_head(kk), by_head(kk), norm.unsqueeze(2).to_broadcast([P, TT * H, N]),
                                  ALU.mult).then_inc(*V.tick())
            have_kk = V.at()

            up, down = room3(TT, RW), room3(TT, RW)
            for t in range(TT):
                bank = take_bank()

                @block.tensor
                def _(pe):
                    for due in unseen(pe, bank.free, log_decay):
                        pe.wait_ge(*due)
                    pe.matmul(bank.ap, const("upto_mid"), decay[:, t, :], start=True, stop=True).then_inc(*M.tick())
                have = M.at()

                @block.scalar
                def _(act):
                    act.wait_ge(*have)
                    act.activation(up[:, t, :], bank.ap, ACT.Exp).then_inc(*S.tick())
                    act.activation(down[:, t, :], bank.ap, ACT.Exp, scale=-1.0).then_inc(*S.tick())

                @block.vector
                def _(dve):
                    for due in unseen(dve, S.at()):
                        dve.wait_ge(*due)
                    dve.wait_ge(*have)
                    dve.tensor_tensor(scratch[:, t, :], bank.ap, decay[:, t, :], ALU.subtract).then_inc(*V.tick())
                bank.free = [V.at(), S.at()]
            excl = V.at()

            @block.scalar
            def _(act):
                act.wait_ge(*excl)
                act.activation(scratch, scratch, ACT.Exp).then_inc(*S.tick())
            powers = S.at()
            bank = take_bank()
            carry = room(H)

            @block.tensor
            def _(pe):
                for due in unseen(pe, bank.free, log_decay):
                    pe.wait_ge(*due)
                for i in range(H):
                    c = slice(i * N, (i + 1) * N)
                    pe.matmul(bank.ap[0:N, i:i + 1], decay[:, 0, c], const("halves")[:, 1:2], start=True, stop=False)
                    last = pe.matmul(bank.ap[0:N, i:i + 1], decay[:, 1, c], const("halves")[:, 0:1], start=False, stop=True)
                last.then_inc(*M.tick())
            have = M.at()

            @block.scalar
            def _(act):
                act.wait_ge(*have)
                act.activation(carry[0:N, :], bank.ap[0:N, 0:H], ACT.Exp).then_inc(*S.tick())
            bank.free = S.at()
            carried = S.at()
            bonus = room(TT * H)
            rk = room3(TT, RW)

            @block.vector
            def _(dve):
                for due in unseen(dve, log_decay):
                    dve.wait_ge(*due)
                dve.tensor_tensor(rk, r, k, ALU.mult).then_inc(*V.tick())
                dve.wait_ge(*V.at())
                dve.tensor_tensor(rk, rk, both_tiles(r_k), ALU.mult).then_inc(*V.tick())
                dve.wait_ge(*V.at())
                dve.tensor_reduce(bonus, by_head(rk), AX, ALU.add).then_inc(*V.tick())
                for due in unseen(dve, powers, have_kk, V.at()):
                    dve.wait_ge(*due)
                dve.tensor_tensor(lr, lr, kk, ALU.mult).then_inc(*V.tick())
                dve.wait_ge(*V.at())
                dve.tensor_tensor(lr, lr, down, ALU.mult).then_inc(*V.tick())
                dve.scalar_tensor_tensor(out=kk, in0=kk, scalar=-1.0, in1=scratch, op0=ALU.mult,
                                         op1=ALU.mult).then_inc(*V.tick())
                dve.tensor_tensor(k, k, down, ALU.mult).then_inc(*V.tick())
                dve.tensor_tensor(r, r, up, ALU.mult).then_inc(*V.tick())
            scaled = V.at()
            top[0] = base
            keep_small = room(TT * H)
            small2 = room(H)

            @block.vector
            def _(dve):
                for due in unseen(dve, scaled, carried):
                    dve.wait_ge(*due)
                dve.tensor_copy(small2[0:N, :], carry[0:N, :]).then_inc(*V.tick())
                dve.tensor_copy(keep_small, bonus).then_inc(*V.tick())
            bonus, carry = keep_small, small2
            scaled = V.at()
            stats = room(TT * H)
            state = room(H * N)
            state_ready = None
            names = ("X", "XT", "Y", "NL")
            homes = (xT_sb, dead_rows)
            work = [{n: homes[g][:, j * 512:(j + 1) * 512] for j, n in enumerate(names)} | {"turned": room(4 * 512), "TTm": room(4 * 512), "rhs": room(256),
                                                      "sa": room(256)} for g in range(2)]
            idle = [None, None]
            for t in range(TT):
                groups = []
                for g in range(2):
                    w = work[g]
                    heads = range(4 * g, 4 * g + 4)
                    tv = w["turned"].rearrange("p (h n) -> p h n", h=4)
                    mv = w["TTm"].rearrange("p (h n) -> p h n", h=4)
                    for j, i in enumerate(heads):
                        c = slice(i * N, (i + 1) * N)
                        bank = take_bank()

                        @block.tensor
                        def _(pe):
                            for due in unseen(pe, bank.free, scaled):
                                pe.wait_ge(*due)
                            for m, x in enumerate((lr, k, kk, r)):
                                last = pe.transpose(bank.ap[0:N, m * P:(m + 1) * P], x[:, t, c], ident)
                            last.then_inc(*M.tick())
                        turned = M.at()

                        @block.scalar
                        def _(act):
                            for due in unseen(act, turned, idle[g], scaled):
                                act.wait_ge(*due)
                            act.copy(tv[0:N, j, :], bank.ap[0:N, :]).then_inc(*S.tick())
                        bank.free = S.at()
                        copied = S.at()
                        bank = take_bank()

                        @block.tensor
                        def _(pe):
                            for due in unseen(pe, bank.free):
                                pe.wait_ge(*due)
                            pe.wait_ge(*copied)
                            pe.matmul(bank.ap[:, 0:256], tv[0:N, j, 0:P], tv[0:N, j, 256:512], start=True, stop=True)
                            pe.matmul(bank.ap[:, 256:512], tv[0:N, j, P:256], tv[0:N, j, 256:512], start=True,
                                      stop=True).then_inc(*M.tick())
                        have = M.at()

                        @block.vector
                        def _(dve):
                            for due in unseen(dve, have, idle[g]):
                                dve.wait_ge(*due)
                            dve.tensor_tensor(mv[:, j, :], bank.ap, const("quad"), ALU.mult).then_inc(*V.tick())
                        bank.free = V.at()
                    groups.append(dict(w, NT=mv[:, :, 0:P], masked=V.at(), copied=copied, tv=tv, mv=mv))
                for w in groups:
                    w["N"] = bank = take_bank()
                    tv = w["tv"]

                    @block.tensor
                    def _(pe):
                        for due in unseen(pe, bank.free, w["copied"]):
                            pe.wait_ge(*due)
                        for j in range(4):
                            last = pe.matmul(bank.ap[:, j * P:(j + 1) * P], tv[0:N, j, 256:384], tv[0:N, j, 0:P],
                                             start=True, stop=True)
                        last.then_inc(*M.tick())
                    w["ready"] = [w["masked"], M.at()]
                invert(groups)
                for g, w in enumerate(groups):
                    tv, mv = w["tv"], w["mv"]
                    hv = slice(4 * g * N, 4 * (g + 1) * N)
                    bank = take_bank()

                    @block.tensor
                    def _(pe):
                        for due in unseen(pe, bank.free, w["have"], state_ready):
                            pe.wait_ge(*due)
                        for j in range(4):
                            c = slice((4 * g + j) * N, (4 * g + j + 1) * N)
                            last = pe.matmul(bank.ap[:, j * N:(j + 1) * N], mv[:, j, 256:384], v[:, t, c],
                                             start=True, stop=(t == 0))
                            if t:
                                last = pe.matmul(bank.ap[:, j * N:(j + 1) * N], tv[0:N, j, 256:384], state[0:N, c],
                                                 start=False, stop=True)
                        last.then_inc(*M.tick())
                    have = M.at()

                    @block.scalar
                    def _(act):
                        act.wait_ge(*have)
                        act.copy(w["rhs"], bank.ap[:, 0:256]).then_inc(*S.tick())
                    bank.free = S.at()
                    have = S.at()
                    bank = take_bank()

                    @block.tensor
                    def _(pe):
                        for due in unseen(pe, bank.free):
                            pe.wait_ge(*due)
                        pe.wait_ge(*have)
                        for j in range(4):
                            last = pe.matmul(bank.ap[:, j * N:(j + 1) * N], w["XT"][:, j * P:(j + 1) * P],
                                             w["rhs"][:, j * N:(j + 1) * N], start=True, stop=True)
                        last.then_inc(*M.tick())
                    have = M.at()

                    @block.scalar
                    def _(act):
                        act.wait_ge(*have)
                        act.copy(w["sa"], bank.ap[:, 0:256]).then_inc(*S.tick())
                    bank.free = S.at()
                    have = S.at()
                    bank = take_bank()
                    bank2 = take_bank()

                    @block.tensor
                    def _(pe):
                        for due in unseen(pe, bank.free, bank2.free):
                            pe.wait_ge(*due)
                        pe.wait_ge(*have)
                        for j in range(4):
                            c = slice((4 * g + j) * N, (4 * g + j + 1) * N)
                            sa = w["sa"][:, j * N:(j + 1) * N]
                            o = bank.ap[:, j * N:(j + 1) * N]
                            pe.matmul(o, mv[:, j, P:256], sa, start=True, stop=False)
                            last = pe.matmul(o, mv[:, j, 384:512], v[:, t, c], start=False, stop=(t == 0))
                            if t:
                                last = pe.matmul(o, tv[0:N, j, 384:512], state[0:N, c], start=False, stop=True)
                            else:
                                o = bank2.ap[0:N, j * N:(j + 1) * N]
                                pe.matmul(o, lr[:, t, c], sa, start=True, stop=False)
                                last = pe.matmul(o, k[:, t, c], v[:, t, c], start=False, stop=True)
                        last.then_inc(*M.tick())
                    have = M.at()
                    idle[g] = M.at()

                    @block.scalar
                    def _(act):
                        act.wait_ge(*have)
                        act.copy(y[:, t, hv], bank.ap[:, 0:256]).then_inc(*S.tick())
                    bank.free = S.at()
                    if t == 0:
                        @block.vector
                        def _(dve):
                            dve.wait_ge(*have)
                            dve.tensor_tensor(state[0:N, hv].rearrange("p (h n) -> p h n", h=4),
                                              bank2.ap[0:N, 0:256].rearrange("p (h n) -> p h n", h=4),
                                              carry[0:N, 4 * g:4 * g + 4].unsqueeze(2).to_broadcast([N, 4, N]),
                                              ALU.mult).then_inc(*V.tick())
                        bank2.free = V.at()
                if t == 0:
                    state_ready = V.at()
            out_ready = S.at()
            yh = [y[:, t, :].rearrange("p (h n) -> p h n", n=N) for t in range(TT)]
            vh = [v[:, t, :].rearrange("p (h n) -> p h n", n=N) for t in range(TT)]
            sv = stats.rearrange("p (t h) -> p t h", t=TT)
            bv = bonus.rearrange("p (t h) -> p t h", t=TT)
            spare = kk
            sh = [spare[:, t, :].rearrange("p (h n) -> p h n", n=N) for t in range(TT)]
            wide = lambda x: x.unsqueeze(2).to_broadcast([P, H, N])

            @block.vector
            def _(dve):
                for due in unseen(dve, out_ready, idle[0], idle[1]):
                    dve.wait_ge(*due)
                for t in range(TT):
                    dve.tensor_reduce(sv[:, t, :], yh[t], AX, ALU.add).then_inc(*V.tick())
                dve.wait_ge(*V.at())
                dve.tensor_scalar(stats, stats, 1.0 / N, None, ALU.mult).then_inc(*V.tick())
                dve.wait_ge(*V.at())
                for t in range(TT):
                    dve.tensor_tensor(yh[t], yh[t], wide(sv[:, t, :]), ALU.subtract).then_inc(*V.tick())
                dve.wait_ge(*V.at())
                dve.tensor_tensor(spare, y, y, ALU.mult).then_inc(*V.tick())
                dve.wait_ge(*V.at())
                for t in range(TT):
                    dve.tensor_reduce(sv[:, t, :], sh[t], AX, ALU.add).then_inc(*V.tick())
                dve.wait_ge(*V.at())
                dve.tensor_scalar(stats, stats, 1.0 / N, 64e-5, ALU.mult, ALU.add).then_inc(*V.tick())
            root = reciprocal_root(stats, TT * H, V.at())

            @block.vector
            def _(dve):
                dve.wait_ge(*root)
                for t in range(TT):
                    dve.tensor_tensor(yh[t], yh[t], wide(sv[:, t, :]), ALU.mult).then_inc(*V.tick())
                    dve.tensor_tensor(sh[t], vh[t], wide(bv[:, t, :]), ALU.mult).then_inc(*V.tick())
                dve.wait_ge(*V.at())
                dve.tensor_tensor(y, y, both_tiles(rows["rw_ln_g"]), ALU.mult).then_inc(*V.tick())
                dve.tensor_tensor(spare, spare, both_tiles(rows["rw_ln_b"]), ALU.add).then_inc(*V.tick())
                dve.wait_ge(*V.at())
                dve.tensor_tensor(y, y, spare, ALU.add).then_inc(*V.tick())
                dve.wait_ge(*V.at())
                dve.tensor_tensor(y, y, gate, ALU.mult).then_inc(*V.tick())

        def project_turned(w, first_col, n_tiles, ready, take):
            for c0 in range(0, n_tiles, 4):
                slot, view, landed = load_weights(w[:, first_col + c0 * P:first_col + (c0 + 4) * P], (P, KD, 4 * P))
                for j in range(4):
                    bank = take_bank()

                    @block.tensor
                    def _(pe):
                        for due in unseen(pe, bank.free, ready, landed):
                            pe.wait_ge(*due)
                        for k in range(KD):
                            last = pe.matmul(bank.ap[:, 0:T], view[:, k, j * P:(j + 1) * P], xT[:, k, :],
                                             start=(k == 0), stop=(k == KD - 1))
                        last.then_inc(*M.tick())
                    slot.free = M.at()
                    bank.free = take(c0 + j, bank.ap[:, 0:T], M.at())

        def conv_project(w, first_col, n_tiles, taps, bias, params_ready, ready, func, finish):
            raw = [room(T) for _ in range(4)]
            done = [room(T) for _ in range(4)]
            raw_free, done_free = [None] * 4, [None] * 4

            def take(i, ps, mark):
                b = i % 4

                @block.vector
                def _(dve):
                    for due in unseen(dve, mark, params_ready, raw_free[b]):
                        dve.wait_ge(*due)
                    if bias is not None:
                        dve.tensor_scalar(raw[b], ps, taps[:, i, 3:4], bias[:, i:i + 1], ALU.mult,
                                          ALU.add).then_inc(*V.tick())
                    else:
                        dve.tensor_scalar(raw[b], ps, taps[:, i, 3:4], None, ALU.mult).then_inc(*V.tick())
                    for back in (1, 2, 3):
                        dve.wait_ge(*V.at())
                        dve.scalar_tensor_tensor(out=raw[b][:, back:T], in0=ps[:, 0:T - back],
                                                 scalar=taps[:, i, 3 - back:4 - back], in1=raw[b][:, back:T],
                                                 op0=ALU.mult, op1=ALU.add).then_inc(*V.tick())
                have = V.at()

                def squash(dst, after):
                    @block.scalar
                    def _(act):
                        for due in unseen(act, after):
                            act.wait_ge(*due)
                        act.wait_ge(*have)
                        act.activation(dst, raw[b], func).then_inc(*S.tick())
                    raw_free[b] = S.at()
                    return S.at()
                done_free[b] = finish(i, squash, done[b], done_free[b])
                return have
            project_turned(w, first_col, n_tiles, ready, take)

        def softplus(x, scratch, ready):
            e, w, lw = scratch

            @block.vector
            def _(dve):
                for due in unseen(dve, ready):
                    dve.wait_ge(*due)
                dve.scalar_tensor_tensor(out=e, in0=x, scalar=-1.0, in1=x, op0=ALU.mult, op1=ALU.max).then_inc(*V.tick())
                dve.wait_ge(*V.at())
                dve.tensor_scalar(x, x, 0.0, None, ALU.max).then_inc(*V.tick())
            have = V.at()

            @block.scalar
            def _(act):
                act.wait_ge(*have)
                act.activation(e, e, ACT.Exp, scale=-1.0).then_inc(*S.tick())
            have = S.at()

            @block.vector
            def _(dve):
                dve.wait_ge(*have)
                dve.tensor_scalar(w, e, 1.0, None, ALU.add).then_inc(*V.tick())
            have = V.at()

            @block.scalar
            def _(act):
                act.wait_ge(*have)
                act.activation(lw, w, ACT.Ln).then_inc(*S.tick())
            have = S.at()

            @block.vector
            def _(dve):
                dve.wait_ge(*have)
                dve.tensor_scalar(w, w, 1.0, None, ALU.subtract).then_inc(*V.tick())
                dve.wait_ge(*V.at())
                dve.scalar_tensor_tensor(out=lw, in0=w, scalar=0.0, in1=lw, op0=ALU.is_equal, op1=ALU.add).then_inc(*V.tick())
                dve.wait_ge(*V.at())
                dve.scalar_tensor_tensor(out=w, in0=w, scalar=0.0, in1=w, op0=ALU.is_equal, op1=ALU.add).then_inc(*V.tick())
                dve.wait_ge(*V.at())
                dve.reciprocal(w, w).then_inc(*V.tick())
                dve.wait_ge(*V.at())
                dve.tensor_tensor(lw, lw, w, ALU.mult).then_inc(*V.tick())
                dve.wait_ge(*V.at())
                dve.tensor_tensor(lw, lw, e, ALU.mult).then_inc(*V.tick())
                dve.wait_ge(*V.at())
                dve.tensor_tensor(x, x, lw, ALU.add).then_inc(*V.tick())
            return V.at()

        def mamba():
            INNER, NH, HDM, GR, NS = 2048, 32, 64, 4, 128
            CONV = INNER + 2 * GR * NS
            enter("mamba")
            par = Params("mamba")
            g_in = par.cols(a["od_norm"][0], D)
            taps = room(24 * 4).rearrange("p (i j) -> p i j", j=4)
            for j in range(4):
                par.load(taps[:, :, j], a["ssm_conv_w"][0][j].rearrange("(i p) -> p i", p=P))
            bias = par.cols(a["ssm_conv_b"][0], CONV)
            dtb = par.rows(a["ssm_dt_bias"][0], NH)
            alog = par.rows(a["ssm_a_log"][0], NH)
            dsk = par.rows(a["ssm_d"][0], NH)
            g_out = par.cols(a["ssm_gnorm"][0], INNER)
            dt = room3(TT, NH)
            keep = top[0]
            normed = norm_turned(h, D, None, xT, g_in, par.landed())
            top[0] = keep
            have_x = normed
            x = room3(TT, INNER)
            BT = room(GR * T).rearrange("p (g t) -> p g t", t=T)
            CT = room(GR * T).rearrange("p (g t) -> p g t", t=T)
            z = room3(TT, INNER)

            def finish(i, squash, done, free):
                if i >= 16:
                    dst = (BT if i < 20 else CT)[:, (i - 16) % 4, :]
                    squash(dst, normed)
                    return None
                ready = squash(done, [free, normed])
                bank = take_bank()

                @block.tensor
                def _(pe):
                    for due in unseen(pe, bank.free, ready):
                        pe.wait_ge(*due)
                    for t in range(TT):
                        last = pe.transpose(bank.ap[:, t * P:(t + 1) * P], done[:, t * P:(t + 1) * P], ident)
                    last.then_inc(*M.tick())
                turned = M.at()

                @block.scalar
                def _(act):
                    act.wait_ge(*turned)
                    act.copy(x[:, :, i * P:(i + 1) * P], bank.ap[:, 0:T].rearrange("p (t n) -> p t n", t=TT)).then_inc(*S.tick())
                bank.free = S.at()
                return turned

            conv_project(a["od_w_in"][0], INNER, 24, taps, bias, par.landed(), normed, ACT.Silu, finish)
            project(xT, KD, a["od_w_in"][0], NH, normed, copy_out(dt), first_col=INNER + CONV)
            dt_have = both()
            enter("ssd", top[0])
            soft = [room3(TT, NH) for _ in range(3)]
            dA = room3(TT, NH)
            wide = lambda r: r.unsqueeze(1).to_broadcast([P, TT, NH])

            @block.vector
            def _(dve):
                for due in unseen(dve, dt_have):
                    dve.wait_ge(*due)
                dve.tensor_tensor(dt, dt, wide(dtb), ALU.add).then_inc(*V.tick())

            @block.scalar
            def _(act):
                act.activation(alog, alog, ACT.Exp).then_inc(*S.tick())
            rate = S.at()
            have = softplus(dt, soft, V.at())

            @block.vector
            def _(dve):
                for due in unseen(dve, rate):
                    dve.wait_ge(*due)
                dve.wait_ge(*have)
                dve.scalar_tensor_tensor(out=dA, in0=dt, scalar=-1.0, in1=wide(alog), op0=ALU.mult,
                                         op1=ALU.mult).then_inc(*V.tick())
            have = V.at()
            cumT, cum = cumulate(dA, NH, have)
            project(xT, KD, a["od_w_in"][0], INNER, None, copy_out(z))
            z_have = both()
            y = z
            xdt = room3(TT, INNER)
            xh = lambda ap, t: ap[:, t, :].rearrange("p (h n) -> p h n", n=HDM)

            @block.gpsimd
            def _(pool):
                pool.wait_ge(*have)
                for t in range(TT):
                    pool.tensor_tensor(xh(xdt, t), xh(x, t), dt[:, t, :].unsqueeze(2).to_broadcast([P, NH, HDM]),
                                       ALU.mult).then_inc(*G.tick())
            scaled = G.at()

            @block.vector
            def _(dve):
                for due in unseen(dve, scaled):
                    dve.wait_ge(*due)
                for t in range(TT):
                    dve.tensor_tensor(xh(x, t), xh(x, t), dsk.unsqueeze(2).to_broadcast([P, NH, HDM]),
                                      ALU.mult).then_inc(*V.tick())
            skip_ready = V.at()

            @block.scalar
            def _(act):
                for due in unseen(act, z_have):
                    act.wait_ge(*due)
                act.activation(z, z, ACT.Silu).then_inc(*S.tick())
            gate_ready = S.at()
            cb = [room(384) for _ in range(GR)]
            for g in range(GR):
                bank = take_bank()

                @block.tensor
                def _(pe):
                    for due in unseen(pe, bank.free):
                        pe.wait_ge(*due)
                    pe.matmul(bank.ap[:, 0:T], BT[:, g, 0:P], CT[:, g, :], start=True, stop=True)
                    pe.matmul(bank.ap[:, T:T + P], BT[:, g, P:T], CT[:, g, P:T], start=True, stop=True).then_inc(*M.tick())
                have = M.at()

                @block.scalar
                def _(act):
                    act.wait_ge(*have)
                    act.copy(cb[g], bank.ap[:, 0:384]).then_inc(*S.tick())
                bank.free = S.at()
            cb_ready = S.at()
            seg = [room(384) for _ in range(4)]
            seg_free = [None] * 4
            NB = 4
            ybank = None
            gate_done = []
            for i in range(NH):
                b = i % 4
                bank = take_bank()

                @block.tensor
                def _(pe):
                    for due in unseen(pe, bank.free, cumT["ready"]):
                        pe.wait_ge(*due)
                    pe.matmul(bank.ap[:, 0:T], ident[0:NH, i:i + 1].to_broadcast([NH, P]), cumT["ap"][0:NH, :],
                              start=True, stop=True).then_inc(*M.tick())
                have = M.at()

                @block.vector
                def _(dve):
                    for due in unseen(dve, seg_free[b], cum["ready"]):
                        dve.wait_ge(*due)
                    dve.wait_ge(*have)
                    dve.scalar_tensor_tensor(out=seg[b][:, 0:P], in0=bank.ap[:, 0:P], scalar=cum["ap"][:, 0, i:i + 1],
                                             in1=const("after_neg"), op0=ALU.subtract, op1=ALU.add).then_inc(*V.tick())
                    dve.tensor_scalar(seg[b][:, P:T], bank.ap[:, P:T], cum["ap"][:, 0, i:i + 1], None,
                                      ALU.subtract).then_inc(*V.tick())
                    dve.scalar_tensor_tensor(out=seg[b][:, T:T + P], in0=bank.ap[:, P:T],
                                             scalar=cum["ap"][:, 1, i:i + 1], in1=const("after_neg"),
                                             op0=ALU.subtract, op1=ALU.add).then_inc(*V.tick())
                bank.free = V.at()
                have = V.at()

                @block.scalar
                def _(act):
                    act.wait_ge(*have)
                    act.activation(seg[b], seg[b], ACT.Exp).then_inc(*S.tick())
                have = S.at()

                @block.gpsimd
                def _(pool):
                    for due in unseen(pool, cb_ready):
                        pool.wait_ge(*due)
                    pool.wait_ge(*have)
                    pool.tensor_tensor(seg[b], seg[b], cb[i // 8], ALU.mult).then_inc(*G.tick())
                have = G.at()
                if i % 4 == 0:
                    ybank = take_bank()

                @block.tensor
                def _(pe):
                    for due in unseen(pe, ybank.free, scaled):
                        pe.wait_ge(*due)
                    pe.wait_ge(*have)
                    c = slice(i * HDM, (i + 1) * HDM)
                    j = i % 4
                    pe.matmul(ybank.ap[:, j * HDM:(j + 1) * HDM], seg[b][:, 0:P], xdt[:, 0, c], start=True, stop=True)
                    o = ybank.ap[:, 256 + j * HDM:256 + (j + 1) * HDM]
                    pe.matmul(o, seg[b][:, P:T], xdt[:, 0, c], start=True, stop=False)
                    pe.matmul(o, seg[b][:, T:T + P], xdt[:, 1, c], start=False, stop=True).then_inc(*M.tick())
                seg_free[b] = M.at()
                if i % 4 == 3:
                    have = M.at()
                    c = slice((i - 3) * HDM, (i + 1) * HDM)

                    @block.vector
                    def _(dve):
                        for due in unseen(dve, skip_ready, gate_ready):
                            dve.wait_ge(*due)
                        dve.wait_ge(*have)
                        dve.tensor_tensor(x[:, :, c], x[:, :, c], ybank.ap.rearrange("p (t n) -> p t n", t=TT),
                                          ALU.add).then_inc(*V.tick())
                        dve.wait_ge(*V.at())
                        dve.tensor_tensor(y[:, :, c], y[:, :, c], x[:, :, c], ALU.mult).then_inc(*V.tick())
                    ybank.free = V.at()
            have = V.at()
            y8 = y.rearrange("p t (g n) -> p (t g) n", n=512)
            r, root = per_head_rstd(y8, TT * GR, 512, have, True, EPS, x.rearrange("p t (g n) -> p (t g) n", n=512))

            @block.vector
            def _(dve):
                dve.wait_ge(*root)
                dve.tensor_tensor(y8, y8, r.unsqueeze(2).to_broadcast([P, TT * GR, 512]), ALU.mult).then_inc(*V.tick())
            have = V.at()
            yT = xdt.rearrange("p t n -> p (t n)").rearrange("p (k t) -> p k t", t=T)
            turned = transpose_tiles(y, 16, have, yT, g_out, None)
            project(yT, 16, a["od_w_out"][0], D, turned, add_to_h)

        def cumulate(x, n, ready):
            cum = room3(TT, n)
            cumT = room(T)
            bank = take_bank()

            @block.tensor
            def _(pe):
                for due in unseen(pe, bank.free, ready):
                    pe.wait_ge(*due)
                pe.matmul(bank.ap[:, 0:n], const("upto"), x[:, 0, :], start=True, stop=True)
                pe.matmul(bank.ap[:, n:2 * n], const("ones"), x[:, 0, :], start=True, stop=False)
                pe.matmul(bank.ap[:, n:2 * n], const("upto"), x[:, 1, :], start=False, stop=True).then_inc(*M.tick())
            have = M.at()

            @block.vector
            def _(dve):
                dve.wait_ge(*have)
                dve.tensor_copy(cum, bank.ap[:, 0:2 * n].rearrange("p (t n) -> p t n", t=TT)).then_inc(*V.tick())
            bank.free = V.at()
            copied = V.at()
            bank = take_bank()

            @block.tensor
            def _(pe):
                for due in unseen(pe, bank.free):
                    pe.wait_ge(*due)
                pe.wait_ge(*copied)
                for t in range(TT):
                    last = pe.transpose(bank.ap[0:n, t * P:(t + 1) * P], cum[:, t, :], ident)
                last.then_inc(*M.tick())
            have = M.at()

            @block.vector
            def _(dve):
                dve.wait_ge(*have)
                dve.tensor_copy(cumT[0:n, :], bank.ap[0:n, 0:T]).then_inc(*V.tick())
            bank.free = V.at()
            return {"ap": cumT, "ready": V.at()}, {"ap": cum, "ready": copied}

        def cross(layer):
            H, N = 4, 128
            enter(f"cross{layer}")
            par = Params(f"cross{layer}")
            g_x = par.cols(a["xa_norm_x"][layer], D)
            g_m = par.cols(a["xa_norm_mem"][layer], D)
            gq = par.rows(a["xa_q_hnorm"][layer], N)
            gk = par.rows(a["xa_k_hnorm"][layer], N)
            q = room3(TT, H * N)
            kv = room3(TT, 2 * H * N)
            y = room3(TT, H * N)
            yT = room(4 * T).rearrange("p (k t) -> p k t", t=T)
            mT = room(KD * T).rearrange("p (k t) -> p k t", t=T)

            @block.vector
            def _(dve):
                dve.wait_ge(*par.landed())
                for k in range(KD):
                    dve.tensor_scalar(mT[:, k, :], memT[:, k, :], g_m[:, k:k + 1], None, ALU.mult).then_inc(*V.tick())
            m_have = V.at()
            project(mT, KD, a["xa_wkv"][layer], 2 * H * N, m_have, copy_out(kv))
            kv_have = both()
            normed = norm_turned(h, D, None, xT, g_x, par.landed())
            project(xT, KD, a["xa_wq"][layer], H * N, normed, copy_out(q))
            q_have = both()
            scratch = room(TT * H * N).rearrange("p (n m) -> p n m", m=N)
            parts = {}
            for t in range(TT):
                kt = kv[:, t, 0:H * N].rearrange("p (h n) -> p h n", n=N)
                parts[t] = head_norm(kt, H, N, [kv_have, V.at()], gk, scratch[:, 0:H, :])
            q_done = head_norm(q.rearrange("p t (h n) -> p (t h) n", n=N), TT * H, N, [q_have, V.at()], gq, scratch)
            have = attention(lambda t, i: q[:, t, i * N:(i + 1) * N], lambda t, i: kv[:, t, i * N:(i + 1) * N],
                             lambda t, i: kv[:, t, (H + i) * N:(H + i + 1) * N], H, N, N, N ** -0.5,
                             lambda i: y[:, :, i * N:(i + 1) * N], [q_done, parts[1]])
            turned = transpose_tiles(y, 4, have, yT)
            project(yT, 4, a["xa_wo"][layer], D, turned, add_to_h)

        def memory_once():
            enter("mem")
            mem = room3(TT, D)
            par = Params("mem")
            par.load(mem, a["mem"][0].rearrange("(t p) d -> p t d", p=P))
            rstd, have = row_rstd(mem, D, par.landed())

            @block.vector
            def _(dve):
                dve.wait_ge(*have)
                for t in range(TT):
                    dve.tensor_scalar(mem[:, t, :], mem[:, t, :], rstd[:, t:t + 1], None, ALU.mult).then_inc(*V.tick())
            return transpose_tiles(mem, KD, V.at(), memT)

        def swiglu(stage, gain, src, n_pairs):
            enter(stage)
            par = Params(stage)
            g = par.cols(gain, D)
            sg = [room(T) for _ in range(4)]
            hT = [room(T) for _ in range(4)]
            normed = norm_turned(h, D, None, xT, g, par.landed())
            steps = 2 * n_pairs
            up_landed = [new_semaphore(f"{stage}_up{b}_landed") for b in range(2)]
            down_landed = [new_semaphore(f"{stage}_down{b}_landed") for b in range(2)]
            up_done, silu_done, hidden_done, down_done = (
                new_semaphore(f"{stage}_{n}_done") for n in ("up", "silu", "hidden", "down"))
            units = [ring[:, b * UNIT:(b + 1) * UNIT] for b in range(2)]
            wg = [u[:, 0:2048].rearrange("p (k n) -> p k n", n=256) for u in units]
            wu = [u[:, 2048:4096].rearrange("p (k n) -> p k n", n=256) for u in units]
            wd = [u[:, 4096:6144].rearrange("p (k n) -> p k n", n=D) for u in units]
            up_banks, acc = banks[0:4], banks[4:8]
            ring_before = [s.free for s in slots]
            banks_before = [b.free for b in banks]

            def run(body, eng):
                rounds, left = steps // 4, steps % 4
                body(0, True, 4)
                if rounds > 1:
                    with eng.Fori(1, rounds) as i:
                        body(i, False, 4)
                if left:
                    body(rounds, False, left)

            @block.sync
            def _(sp):
                for due in unseen(sp, ring_before):
                    sp.wait_ge(*due)

                def body(i, first, count):
                    for j in range(0, count, 2):
                        b = (j // 2) % 2
                        unit_start = i * 4 + j
                        c = i * (4 * P) + j * P
                        reused = not first or j >= 4
                        if reused:
                            sp.wait_ge(up_done, unit_start - 2)
                        sp.dma_start(wg[b], src("gate", c).rearrange("(k p) n -> p k n", p=P)).then_inc(up_landed[b], 16)
                        sp.dma_start(wu[b], src("up", c).rearrange("(k p) n -> p k n", p=P)).then_inc(up_landed[b], 16)
                        if reused:
                            sp.wait_ge(down_done, unit_start - 2)
                        sp.dma_start(wd[b], src("down", c).rearrange("(k p) n -> p k n", p=P)).then_inc(down_landed[b], 16)
                run(body, sp)

            @block.tensor
            def _(pe):
                for due in unseen(pe, normed, banks_before):
                    pe.wait_ge(*due)

                def up(i, first, j):
                    b = j // 2
                    if j % 2 == 0:
                        pe.wait_ge(up_landed[b], i * 32 + 32)
                    if not first:
                        pe.wait_ge(hidden_done, i * 4 + (j - 3))
                    ps = up_banks[j].ap
                    for which, w in enumerate((wg, wu)):
                        for k in range(KD):
                            last = pe.matmul(ps[:, which * T:(which + 1) * T], w[b][:, k, (j % 2) * P:(j % 2 + 1) * P],
                                             xT[:, k, :], start=(k == 0), stop=(k == KD - 1))
                    last.then_inc(up_done, 1)

                def down(i, j, start=False, stop=False):
                    b = j // 2
                    if j % 2 == 0:
                        pe.wait_ge(down_landed[b], i * 16 + 16)
                    pe.wait_ge(hidden_done, i * 4 + (j + 1))
                    for t in range(TT):
                        for n in range(2):
                            last = pe.matmul(acc[t * 2 + n].ap, hT[j][:, t * P:(t + 1) * P],
                                             wd[b][:, j % 2, n * 512:(n + 1) * 512], start=start, stop=stop)
                    last.then_inc(down_done, 1)

                def body(i, first, count):
                    for j in range(count):
                        up(i, first, j)
                        if j >= 2:
                            down(i, j - 2, start=(first and j == 2))
                        elif not first:
                            down(i - 1, j + 2)
                run(body, pe)
                i, j = (steps // 4 - 1, 2) if steps % 4 == 0 else (steps // 4, 0)
                down(i, j)
                down(i, j + 1, stop=True)

            @block.scalar
            def _(act):
                def body(i, first, count):
                    for j in range(count):
                        act.wait_ge(up_done, i * 4 + (j + 1))
                        act.activation(sg[j], up_banks[j].ap[:, 0:T], ACT.Silu).then_inc(silu_done, 1)
                run(body, act)

            @block.vector
            def _(dve):
                def body(i, first, count):
                    for b in range(count):
                        at = i * 4 + b
                        dve.wait_ge(silu_done, at + 1)
                        if not first:
                            dve.wait_ge(down_done, at - 3)
                        dve.tensor_tensor(hT[b], sg[b], up_banks[b].ap[:, T:2 * T], ALU.mult).then_inc(hidden_done, 1)
                run(body, dve)
                dve.wait_ge(down_done, steps)
                for t in range(TT):
                    for n in range(2):
                        c = slice(n * 512, (n + 1) * 512)
                        dve.tensor_tensor(h[:, t, c], h[:, t, c], acc[t * 2 + n].ap, ALU.add).then_inc(*V.tick())
            for b in banks:
                b.free = V.at()
            for s in slots:
                s.free = (down_done, steps)

        def experts_by_tile():
            E, FE, C = 8, 3584, 512
            NC = FE // C
            MAX_TILES = TT * 2 + E - 1
            TILES = MAX_TILES + 1
            enter("route")
            par = Params("moe")
            g_col = par.cols(a["ln_ffn_2"][1], D)
            g_row = par.rows(a["ln_ffn_2"][1], D)
            rt = par.load(room3(KD, E), a["o_router_2"][0].rearrange("(k p) n -> p k n", p=P))
            slot_of, gate_of = room3(TT, TILES), room3(TT, TILES)
            expert_row = room(TILES, I32)
            n_tiles_cell = room(4, I32)
            pick, pick_gate = room3(TT, P), room3(TT, P)
            combine = room(T)
            silu, hid, y_sb = room(C), room(C), room(D)
            rows = room3(TT, D)
            split_at = top[0]
            rstd, have = row_rstd(h, D, None)

            @block.vector
            def _(dve):
                dve.wait_ge(*have)
                for t in range(TT):
                    dve.tensor_scalar(rows[:, t, :], h[:, t, :], rstd[:, t:t + 1], None, ALU.mult).then_inc(*V.tick())
            normed = transpose_tiles(rows, KD, V.at(), xT, g_col, par.landed())

            @block.vector
            def _(dve):
                dve.wait_ge(*normed)
                dve.tensor_tensor(rows, rows, g_row.unsqueeze(1).to_broadcast([P, TT, D]), ALU.mult).then_inc(*V.tick())
            logits, gates, chosen = room3(TT, E), room3(TT, E), room3(TT, E)
            best, second = room3(TT, E), room3(TT, E)
            index, rank = room(TT * E, U32).rearrange("p (t e) -> p t e", t=TT), room3(TT, E)
            w1, w2 = room(TT), room(TT)
            bank = take_bank()

            @block.tensor
            def _(pe):
                for due in unseen(pe, bank.free):
                    pe.wait_ge(*due)
                pe.wait_ge(*normed)
                for t in range(TT):
                    for k in range(KD):
                        last = pe.matmul(bank.ap[:, t * E:(t + 1) * E], xT[:, k, t * P:(t + 1) * P], rt[:, k, :],
                                         start=(k == 0), stop=(k == KD - 1))
                last.then_inc(*M.tick())
            have = M.at()

            @block.vector
            def _(dve):
                dve.wait_ge(*have)
                dve.tensor_copy(logits, bank.ap[:, 0:TT * E].rearrange("p (t e) -> p t e", t=TT)).then_inc(*V.tick())
                dve.wait_ge(*V.at())
                for t in range(TT):
                    dve.max(best[:, t, :], logits[:, t, :]).then_inc(*V.tick())
                dve.wait_ge(*V.at())
                for t in range(TT):
                    dve.max_index(index[:, t, :], best[:, t, :], logits[:, t, :]).then_inc(*V.tick())
                dve.tensor_tensor(w2, best[:, :, 1], best[:, :, 0], ALU.subtract).then_inc(*V.tick())
            bank.free = V.at()
            have = V.at()

            @block.scalar
            def _(act):
                act.wait_ge(*have)
                act.activation(w2, w2, ACT.Exp).then_inc(*S.tick())
            have = S.at()

            @block.vector
            def _(dve):
                dve.wait_ge(*have)
                dve.tensor_copy(rank, index).then_inc(*V.tick())
                dve.tensor_scalar(w1, w2, 1.0, None, ALU.add).then_inc(*V.tick())
                dve.wait_ge(*V.at())
                dve.reciprocal(w1, w1).then_inc(*V.tick())
                dve.wait_ge(*V.at())
                dve.tensor_tensor(w2, w2, w1, ALU.mult).then_inc(*V.tick())
                dve.wait_ge(*V.at())
                for t in range(TT):
                    for n, w in enumerate((w1, w2)):
                        dve.tensor_scalar((gates, second)[n][:, t, :], const("ramp")[:, 0:E], rank[:, t, n:n + 1],
                                          w[:, t:t + 1], ALU.is_equal, ALU.mult).then_inc(*V.tick())
                        dve.tensor_scalar((chosen, logits)[n][:, t, :], const("ramp")[:, 0:E], rank[:, t, n:n + 1],
                                          None, ALU.is_equal).then_inc(*V.tick())
                dve.wait_ge(*V.at())
                dve.tensor_tensor(gates, gates, second, ALU.add).then_inc(*V.tick())
                dve.tensor_tensor(chosen, chosen, logits, ALU.add).then_inc(*V.tick())
            have = V.at()
            bank = take_bank()

            @block.tensor
            def _(pe):
                for due in unseen(pe, bank.free):
                    pe.wait_ge(*due)
                pe.wait_ge(*have)
                pe.matmul(bank.ap[:, 0:E], const("before"), chosen[:, 0, :], start=True, stop=True)
                pe.matmul(bank.ap[:, E:2 * E], const("ones"), chosen[:, 0, :], start=True, stop=False)
                pe.matmul(bank.ap[:, E:2 * E], const("before"), chosen[:, 1, :], start=False, stop=True)
                pe.matmul(bank.ap[:, 2 * E:3 * E], const("ones"), chosen[:, 0, :], start=True, stop=False)
                pe.matmul(bank.ap[:, 2 * E:3 * E], const("ones"), chosen[:, 1, :], start=False, stop=True).then_inc(*M.tick())
            have = M.at()
            place = room3(TT, E)
            count, tiles, over, first, zero = (room(E) for _ in range(5))
            off, low = (room(TILES * E).rearrange("p (n e) -> p n e", e=E) for _ in range(2))
            eid = room(TILES)
            tile_ramp = const("ramp")[:, 0:TILES]
            by_tile = lambda x: x.unsqueeze(1).to_broadcast([P, TILES, E])

            @block.vector
            def _(dve):
                dve.wait_ge(*have)
                dve.memset(zero, 0.0).then_inc(*V.tick())
                dve.tensor_copy(count, bank.ap[:, 2 * E:3 * E]).then_inc(*V.tick())
                dve.tensor_copy(place, bank.ap[:, 0:2 * E].rearrange("p (t e) -> p t e", t=TT)).then_inc(*V.tick())
                dve.wait_ge(*V.at())
                dve.tensor_scalar(over, count, float(P), None, ALU.is_gt).then_inc(*V.tick())
                dve.wait_ge(*V.at())
                dve.scalar_tensor_tensor(out=tiles, in0=count, scalar=0.0, in1=over, op0=ALU.is_gt, op1=ALU.add).then_inc(*V.tick())
                dve.wait_ge(*V.at())
                dve.tensor_tensor_scan(first, tiles, zero, 0.0, ALU.add, ALU.add).then_inc(*V.tick())
                dve.wait_ge(*V.at())
                dve.tensor_copy(n_tiles_cell[:, 0:1], first[:, E - 1:E]).then_inc(*V.tick())
                dve.tensor_scalar(n_tiles_cell[:, 1:2], first[:, E - 1:E], 1.0, None, ALU.subtract).then_inc(*V.tick())
                dve.tensor_tensor(over, first, tiles, ALU.subtract).then_inc(*V.tick())
                dve.wait_ge(*V.at())
                dve.scalar_tensor_tensor(out=place, in0=over.unsqueeze(1).to_broadcast([P, TT, E]), scalar=float(P),
                                         in1=place, op0=ALU.mult, op1=ALU.add).then_inc(*V.tick())
                dve.wait_ge(*V.at())
                dve.scalar_tensor_tensor(out=place, in0=place, scalar=1.0, in1=chosen, op0=ALU.add, op1=ALU.mult).then_inc(*V.tick())
                dve.wait_ge(*V.at())
                dve.tensor_scalar(place, place, 1.0, None, ALU.subtract).then_inc(*V.tick())
                dve.tensor_tensor(off, tile_ramp.unsqueeze(2).to_broadcast([P, TILES, E]), by_tile(first),
                                  ALU.is_ge).then_inc(*V.tick())
                dve.wait_ge(*V.at())
                dve.tensor_reduce(eid, off, AX, ALU.add).then_inc(*V.tick())
                dve.wait_ge(*V.at())
                dve.tensor_scalar(eid, eid, float(E - 1), None, ALU.min).then_inc(*V.tick())
                dve.wait_ge(*V.at())
                dve.tensor_copy(expert_row, eid).then_inc(*V.tick())
                for t in range(TT):
                    dve.scalar_tensor_tensor(out=off, in0=tile_ramp.unsqueeze(2).to_broadcast([P, TILES, E]),
                                             scalar=-float(P), in1=by_tile(place[:, t, :]), op0=ALU.mult,
                                             op1=ALU.add).then_inc(*V.tick())
                    dve.wait_ge(*V.at())
                    dve.tensor_scalar(low, off, float(P), None, ALU.is_lt).then_inc(*V.tick())
                    dve.wait_ge(*V.at())
                    dve.scalar_tensor_tensor(out=low, in0=off, scalar=0.0, in1=low, op0=ALU.is_ge,
                                             op1=ALU.mult).then_inc(*V.tick())
                    dve.wait_ge(*V.at())
                    dve.scalar_tensor_tensor(out=off, in0=off, scalar=1.0, in1=low, op0=ALU.add,
                                             op1=ALU.mult).then_inc(*V.tick())
                    dve.tensor_tensor(low, low, by_tile(gates[:, t, :]), ALU.mult).then_inc(*V.tick())
                    dve.wait_ge(*V.at())
                    dve.tensor_reduce(slot_of[:, t, :], off, AX, ALU.add).then_inc(*V.tick())
                    dve.tensor_reduce(gate_of[:, t, :], low, AX, ALU.add).then_inc(*V.tick())
                    dve.wait_ge(*V.at())
                dve.tensor_scalar(slot_of, slot_of, 1.0, None, ALU.subtract).then_inc(*V.tick())
                dve.wait_ge(*V.at())
                for t in range(TT):
                    dve.tensor_scalar(pick[:, t, :], const("ramp"), slot_of[:, t, 0:1], None, ALU.is_equal).then_inc(*V.tick())
            before_moe = V.at()
            enter("moe", split_at)

            def tiles_on(eng):
                return eng.value_load(n_tiles_cell[0:1, 0:1], min_val=4, max_val=MAX_TILES)

            def last_tile_on(eng):
                return eng.value_load(n_tiles_cell[0:1, 1:2], min_val=3, max_val=MAX_TILES - 1)

            at = [split_at]

            def split(name, cols):
                tensor = nc.alloc_sbuf_tensor_at(name, [P, cols], F32R, offset=arena_base + 4 * at[0])
                at[0] += cols
                assert at[0] <= ARENA
                return tensor
            NB = 6
            hi, lo = split("weights_high", NB * 1024), split("weights_low", NB * 1024)
            xh, xl = split("rows_high", D), split("rows_low", D)
            hh, hl = split("hidden_high", C), split("hidden_low", C)
            HALVES, HALF = 42, SLOT // 2
            SLOTS_HERE = 7
            raw = [ring[:, s * HALF:(s + 1) * HALF] for s in range(SLOTS_HERE)]
            names = ("hi_done", "lo_done", "sub_used", "silu_done", "hid_done", "turn_done", "hh_done", "hl_done",
                     "pick_done", "gather_done", "xh_done", "xl_done", "y_done", "combine_turned", "combine_done",
                     "products_done", "combine_copied")
            sems = {n: new_semaphore(f"moe_{n}") for n in names}
            landed = [new_semaphore(f"moe_raw{s}_landed") for s in range(SLOTS_HERE)]
            G_, U_, D_ = range(3)
            pieces = [(G_, 0), (U_, 0)]
            for c in range(1, NC):
                pieces += [(G_, c), (U_, c), (D_, c - 1)]
            pieces.append((D_, NC - 1))
            SUBS = 4 * len(pieces)
            assert HALVES == 2 * len(pieces) and HALVES % SLOTS_HERE == 0
            end = {piece: 4 * n + 4 for n, piece in enumerate(pieces)}
            bg, bu, bt, by0, by1, bc0, bc1, bx = (b.ap for b in banks)
            banks_before = [b.free for b in banks]
            ring_before = [s.free for s in slots]

            @block.sync
            def _(sp):
                for due in unseen(sp, ring_before, before_moe):
                    sp.wait_ge(*due)

                def body(i, first):
                    e = sp.value_load(expert_row[0:1, bass.ds(i, 1)], min_val=0, max_val=E - 1)
                    for u in range(HALVES):
                        p, c = pieces[u // 2]
                        part, s = u % 2, u % SLOTS_HERE
                        if not first or u >= SLOTS_HERE:
                            sp.wait_ge(sems["lo_done"], i * SUBS + 2 * (u - SLOTS_HERE + 1))
                        w = a[("o_moe_w_gate_2", "o_moe_w_up_2", "o_moe_w_down_2")[p]][0].rearrange("e r n -> (e r) n")
                        if p == D_:
                            src = w[bass.ds(e * FE + (c * C + part * C // 2), C // 2), :]
                            width = D
                        else:
                            src = w[bass.ds(e * D + part * D // 2, D // 2), c * C:(c + 1) * C]
                            width = C
                        sp.dma_start(raw[s].rearrange("p (k n) -> p k n", n=width),
                                     src.rearrange("(k p) n -> p k n", p=P)).then_inc(landed[s], 16)
                body(0, True)
                with sp.Fori(1, tiles_on(sp)) as i:
                    body(i, False)

            @block.tensor
            def _(pe):
                def gather():
                    for k in range(KD):
                        out_ = (bc0, bc1)[k // 4][:, (k % 4) * P:(k % 4 + 1) * P]
                        for t in range(TT):
                            last = pe.matmul(out_, rows[:, t, k * P:(k + 1) * P], pick[:, t, :], start=(t == 0),
                                             stop=(t == TT - 1))
                    last.then_inc(sems["gather_done"], 1)

                def passes(out_, left, right, start, stop):
                    (lh, ll), (rh, rl) = left, right
                    pe.matmul(out_, lh, rh, start=start, stop=False)
                    pe.matmul(out_, ll, rh, start=False, stop=False)
                    return pe.matmul(out_, lh, rl, start=False, stop=stop)

                def combine_products(i):
                    pe.wait_ge(sems["y_done"], i + 1)
                    for n in range(4):
                        t, half = n // 2, n % 2
                        if n >= 2:
                            pe.wait_ge(sems["combine_done"], i * 4 + n - 1)
                        pe.matmul((bc0, bc1)[half], combine[:, t * P:(t + 1) * P], y_sb[:, half * 512:(half + 1) * 512],
                                  start=True, stop=True).then_inc(sems["products_done"], 1)

                def body(i, first):
                    for n, (p, c) in enumerate(pieces):
                        if p == G_ and c == 0:
                            pe.wait_ge(sems["xl_done"], i + 1)
                        if p == G_ and not (first and c == 0):
                            pe.wait_ge(sems["silu_done"], i * NC + c)
                        if p == U_ and not (first and c == 0):
                            pe.wait_ge(sems["hid_done"], i * NC + c)
                        if p == D_ and c == 0 and not first:
                            pe.wait_ge(sems["y_done"], i)
                        if p == D_:
                            pe.wait_ge(sems["hl_done"], i * NC + c + 1)
                        for s in range(4):
                            m = 4 * n + s
                            b = slice((m % NB) * 1024, (m % NB) * 1024 + 1024)
                            pe.wait_ge(sems["lo_done"], i * SUBS + m + 1)
                            if p == D_:
                                f = slice(s * P, (s + 1) * P)
                                wh, wl = (w[:, b].rearrange("p (n c) -> p n c", n=2) for w in (hi, lo))
                                for half in range(2):
                                    last = passes((by0, by1)[half], (hh[:, f], hl[:, f]), (wh[:, half], wl[:, half]),
                                                  start=(c == 0 and s == 0), stop=(c == NC - 1 and s == 3))
                            else:
                                wh, wl = (w[:, b].rearrange("p (k c) -> p k c", k=2) for w in (hi, lo))
                                for k2 in range(2):
                                    k = slice((2 * s + k2) * P, (2 * s + k2 + 1) * P)
                                    last = passes((bg, bu)[p], (xh[:, k], xl[:, k]), (wh[:, k2], wl[:, k2]),
                                                  start=(s == 0 and k2 == 0), stop=(s == 3 and k2 == 1))
                            last.then_inc(sems["sub_used"], 1)
                        if p == U_ and c == 0 and not first:
                            combine_products(i - 1)
                        if p == U_ and c == NC - 2:
                            pe.wait_ge(sems["pick_done"], i + 1)
                            if not first:
                                pe.wait_ge(sems["combine_copied"], i)
                            for t in range(TT):
                                last = pe.transpose(bx[:, t * P:(t + 1) * P], pick_gate[:, t, :], ident)
                            last.then_inc(sems["combine_turned"], 1)
                        if p == U_ and c == NC - 1:
                            pe.wait_ge(sems["pick_done"], i + 1)
                            if not first:
                                pe.wait_ge(sems["combine_done"], i * 4)
                            gather()
                        if (p == G_ and c) or (p == D_ and c == NC - 2):
                            ct = c - 1 if p == G_ else NC - 1
                            pe.wait_ge(sems["hid_done"], i * NC + ct + 1)
                            if not (first and ct == 0):
                                pe.wait_ge(sems["hl_done"], i * NC + ct)
                            for s in range(4):
                                last = pe.transpose(bt[:, s * P:(s + 1) * P], hid[:, s * P:(s + 1) * P], ident)
                            last.then_inc(sems["turn_done"], 1)

                for due in unseen(pe, banks_before):
                    pe.wait_ge(*due)
                gather()
                body(0, True)
                with pe.Fori(1, tiles_on(pe)) as i:
                    body(i, False)
                combine_products(last_tile_on(pe))

            @block.scalar
            def _(act):
                def rows_high(i):
                    act.wait_ge(sems["gather_done"], i + 1)
                    for n, b in enumerate((bc0, bc1)):
                        last = act.copy(xh[:, n * 512:(n + 1) * 512], b)
                    last.then_inc(sems["xh_done"], 1)

                def y_out(i):
                    act.wait_ge(sems["sub_used"], i * SUBS + SUBS)
                    act.copy(y_sb[:, 0:512], by0)
                    act.copy(y_sb[:, 512:1024], by1).then_inc(sems["y_done"], 1)

                def body(i, first):
                    for m in range(SUBS):
                        p, c = pieces[m // 4]
                        b = m % NB
                        u = m // 2
                        piece = raw[u % SLOTS_HERE][:, (m % 2) * 1024:(m % 2 + 1) * 1024]
                        if m % 2 == 0:
                            act.wait_ge(landed[u % SLOTS_HERE], i * (16 * HALVES // SLOTS_HERE) + 16 * (u // SLOTS_HERE + 1))
                        if not (first and m < NB):
                            act.wait_ge(sems["sub_used"], i * SUBS + m - NB + 1)
                        act.copy(hi[:, b * 1024:(b + 1) * 1024], piece).then_inc(sems["hi_done"], 1)
                        if m == 5 and not first:
                            y_out(i - 1)
                        for cc in range(NC):
                            if m == end[G_, cc] + 3:
                                act.wait_ge(sems["sub_used"], i * SUBS + end[G_, cc])
                                if not (first and cc == 0):
                                    act.wait_ge(sems["hid_done"], i * NC + cc)
                                act.activation(silu, bg, ACT.Silu).then_inc(sems["silu_done"], 1)
                            turned_at = end[G_, cc + 1] + 4 if cc < NC - 1 else SUBS - 1
                            if m == turned_at:
                                act.wait_ge(sems["turn_done"], i * NC + cc + 1)
                                act.copy(hh[:], bt).then_inc(sems["hh_done"], 1)
                        if m == end[U_, NC - 1] + 5:
                            rows_high(i + 1)
                        if m == end[U_, NC - 2] + 3:
                            act.wait_ge(sems["combine_turned"], i + 1)
                            act.copy(combine, bx[:, 0:T]).then_inc(sems["combine_copied"], 1)

                rows_high(0)
                body(0, True)
                with act.Fori(1, tiles_on(act)) as i:
                    body(i, False)
                y_out(last_tile_on(act))

            @block.vector
            def _(dve):
                def rows_low(i):
                    dve.wait_ge(sems["xh_done"], i + 1)
                    for n, b in enumerate((bc0, bc1)):
                        last = dve.tensor_tensor(xl[:, n * 512:(n + 1) * 512], b, xh[:, n * 512:(n + 1) * 512].bitcast(F32),
                                                 ALU.subtract)
                    last.then_inc(sems["xl_done"], 1)

                def add_rows(i):
                    for n in range(4):
                        t, c = n // 2, slice((n % 2) * 512, (n % 2 + 1) * 512)
                        dve.wait_ge(sems["products_done"], i * 4 + n + 1)
                        dve.tensor_tensor(h[:, t, c], h[:, t, c], (bc0, bc1)[n % 2], ALU.add).then_inc(sems["combine_done"], 1)

                def body(i, first):
                    for m in range(SUBS):
                        p, c = pieces[m // 4]
                        b = slice((m % NB) * 1024, (m % NB + 1) * 1024)
                        dve.wait_ge(sems["hi_done"], i * SUBS + m + 1)
                        piece = raw[(m // 2) % SLOTS_HERE][:, (m % 2) * 1024:(m % 2 + 1) * 1024]
                        dve.tensor_tensor(lo[:, b], piece, hi[:, b].bitcast(F32),
                                          ALU.subtract).then_inc(sems["lo_done"], 1)
                        for cc in range(NC):
                            if m == end[U_, cc] + 3:
                                dve.wait_ge(sems["sub_used"], i * SUBS + end[U_, cc])
                                dve.wait_ge(sems["silu_done"], i * NC + cc + 1)
                                if not (first and cc == 0):
                                    dve.wait_ge(sems["turn_done"], i * NC + cc)
                                dve.tensor_tensor(hid, silu, bu, ALU.mult).then_inc(sems["hid_done"], 1)
                            turned_at = end[G_, cc + 1] + 4 if cc < NC - 1 else SUBS - 1
                            if m == turned_at:
                                dve.wait_ge(sems["hh_done"], i * NC + cc + 1)
                                dve.tensor_tensor(hl[:], bt, hh[:].bitcast(F32), ALU.subtract).then_inc(sems["hl_done"], 1)
                        if m == end[U_, 0] + 4 and not first:
                            add_rows(i - 1)
                        if m == end[U_, 2] + 6:
                            if not first:
                                dve.wait_ge(sems["combine_turned"], i)
                            dve.wait_ge(sems["gather_done"], i + 1)
                            for t in range(TT):
                                dve.tensor_scalar(pick_gate[:, t, :], const("ramp"), slot_of[:, t, bass.ds(i, 1)],
                                                  gate_of[:, t, bass.ds(i, 1)], ALU.is_equal, ALU.mult)
                                last = dve.tensor_scalar(pick[:, t, :], const("ramp"), slot_of[:, t, bass.ds(i + 1, 1)],
                                                         None, ALU.is_equal)
                            last.then_inc(sems["pick_done"], 1)
                        if m == end[U_, NC - 1] + 5:
                            rows_low(i + 1)

                rows_low(0)
                body(0, True)
                with dve.Fori(1, tiles_on(dve)) as i:
                    body(i, False)
                add_rows(last_tile_on(dve))
                dve.memset(hid[:, 0:1], 0.0).then_inc(*V.tick())

        def lru_and_window():
            LW, H, KVH, N = 512, 8, 2, 64
            NT4 = LW // P
            enter("mix2")
            par = Params("mix2")
            g_in = par.cols(a["ln_mix_2"][0], D)
            taps = room(NT4 * 4).rearrange("p (i j) -> p i j", j=4)
            for j in range(4):
                par.load(taps[:, :, j], a["e_lru_conv_w_2"][0][j].rearrange("(i p) -> p i", p=P))
            bias = par.cols(a["e_lru_conv_b_2"][0], LW)
            b_a = par.cols(a["e_lru_b_a_2"][0], LW)
            b_i = par.cols(a["e_lru_b_i_2"][0], LW)
            lam = par.cols(a["e_lru_lambda_2"][0], LW)
            gq = par.rows(a["e_q_norm_2"][0], N)
            gk = par.rows(a["e_k_norm_2"][0], N)
            sinks = par.rows(a["e_sinks_2"][0], H)
            blocks_a, blocks_i = room3(NT4, P), room3(NT4, P)

            @block.vector
            def _(dve):
                dve.memset(blocks_a, 0.0).then_inc(*V.tick())
                dve.memset(blocks_i, 0.0).then_inc(*V.tick())
            zeroed = V.at()

            @block.gpsimd
            def _(pool):
                pool.wait_ge(*zeroed)
            for dst, src in ((blocks_a, a["e_lru_w_a_2"][0]), (blocks_i, a["e_lru_w_i_2"][0])):
                for half in range(2):
                    r = slice(half * N, (half + 1) * N)
                    par.load(dst[r, :, r], src.rearrange("(i two) p q -> two p i q", two=2)[half])
            soft = [room(NT4) for _ in range(3)]

            @block.vector
            def _(dve):
                dve.wait_ge(*par.landed())
                dve.tensor_scalar(lam, lam, -1.0, None, ALU.mult).then_inc(*V.tick())
            lam_ready = softplus(lam, soft, V.at())
            yT = room3(KD, T)
            x = room3(NT4, T)
            gate = room3(NT4, T)
            qkv = room3(TT, (H + 2 * KVH) * N)
            y = room3(TT, H * N)
            keep = top[0]
            normed = norm_turned(h, D, None, xT, g_in, par.landed())

            def finish(i, squash, done, free):
                squash(x[:, i, :], normed)
                return None
            conv_project(a["e_w_in_2"][0], 0, NT4, taps, bias, par.landed(), normed, ACT.Identity, finish)
            x_ready = S.at()

            def take(i, ps, mark):
                @block.scalar
                def _(act):
                    act.wait_ge(*mark)
                    act.activation(gate[:, i, :], ps, ACT.Gelu_apprx_tanh).then_inc(*S.tick())
                return S.at()
            project_turned(a["e_w_in_2"][0], LW, NT4, normed, take)
            gate_ready = S.at()
            project(xT, KD, a["e_w_in_2"][0], (H + 2 * KVH) * N, normed, copy_out(qkv), first_col=2 * LW)
            qkv_have = both()
            top[0] = keep
            r, gi = room3(NT4, T), room3(NT4, T)
            for i in range(NT4):
                bank = take_bank()

                @block.tensor
                def _(pe):
                    for due in unseen(pe, bank.free, x_ready, qkv_have):
                        pe.wait_ge(*due)
                    pe.wait_ge(*par.landed())
                    pe.matmul(bank.ap[:, 0:T], blocks_a[:, i, :], x[:, i, :], start=True, stop=True)
                    pe.matmul(bank.ap[:, T:2 * T], blocks_i[:, i, :], x[:, i, :], start=True, stop=True).then_inc(*M.tick())
                have = M.at()

                @block.scalar
                def _(act):
                    for due in unseen(act, qkv_have):
                        act.wait_ge(*due)
                    act.wait_ge(*have)
                    act.activation(r[:, i, :], bank.ap[:, 0:T], ACT.Sigmoid, bias=b_a[:, i:i + 1]).then_inc(*S.tick())
                    act.activation(gi[:, i, :], bank.ap[:, T:2 * T], ACT.Sigmoid, bias=b_i[:, i:i + 1]).then_inc(*S.tick())
                bank.free = S.at()
            have = S.at()
            root = room3(NT4, T)

            @block.vector
            def _(dve):
                for due in unseen(dve, lam_ready):
                    dve.wait_ge(*due)
                dve.wait_ge(*have)
                for i in range(NT4):
                    dve.tensor_scalar(r[:, i, :], r[:, i, :], lam[:, i:i + 1], -8.0, ALU.mult, ALU.mult).then_inc(*V.tick())
                dve.tensor_tensor(gi, gi, x, ALU.mult).then_inc(*V.tick())
            have = V.at()

            @block.scalar
            def _(act):
                act.wait_ge(*have)
                act.activation(root, r, ACT.Tanh).then_inc(*S.tick())
                act.wait_ge(*S.at())
                act.activation(r, r, ACT.Exp).then_inc(*S.tick())
            have = S.at()

            @block.vector
            def _(dve):
                dve.wait_ge(*have)
                dve.tensor_scalar(x, root, -1.0, 1.0, ALU.mult, ALU.add).then_inc(*V.tick())
                dve.wait_ge(*V.at())
                dve.reciprocal(x, x).then_inc(*V.tick())
                dve.wait_ge(*V.at())
                dve.scalar_tensor_tensor(out=root, in0=root, scalar=-2.0, in1=x, op0=ALU.mult, op1=ALU.mult).then_inc(*V.tick())
                dve.wait_ge(*V.at())
                dve.tensor_scalar(root, root, 1e-30, None, ALU.max).then_inc(*V.tick())
            have = V.at()

            @block.scalar
            def _(act):
                act.wait_ge(*have)
                act.activation(root, root, ACT.Sqrt).then_inc(*S.tick())
            have = S.at()

            @block.vector
            def _(dve):
                for due in unseen(dve, gate_ready):
                    dve.wait_ge(*due)
                dve.wait_ge(*have)
                dve.tensor_tensor(gi, gi, root, ALU.mult).then_inc(*V.tick())
                dve.wait_ge(*V.at())
                for i in range(NT4):
                    dve.tensor_tensor_scan(x[:, i, :], r[:, i, :], gi[:, i, :], 0.0, ALU.mult, ALU.add).then_inc(*V.tick())
                dve.wait_ge(*V.at())
                dve.tensor_tensor(yT[:, 0:NT4, :], x, gate, ALU.mult).then_inc(*V.tick())
            lru_ready = V.at()

            HK = H + KVH
            scratch = room(HK * N).rearrange("p (n m) -> p n m", m=N)
            halves = [room(HK * 32).rearrange("p (n m) -> p n m", m=32) for _ in range(2)]
            view = [qkv[:, t, :].rearrange("p (n m) -> p n m", m=N) for t in range(TT)]
            for t in range(TT):
                head_norm(view[t][:, 0:H, :], H, N, [qkv_have, V.at()], gq, scratch[:, 0:H, :])
                done = head_norm(view[t][:, H:HK, :], KVH, N, V.at(), gk, scratch[:, 0:KVH, :])
                cos, sin = (const(n).rearrange("p (t m) -> p t m", t=TT)[:, t, :].unsqueeze(1).to_broadcast([P, HK, 32])
                            for n in ("rope_cos", "rope_sin"))
                have = rotate(view[t][:, 0:HK, 0:32], view[t][:, 0:HK, 32:64], cos, sin, None, done, halves)
            have = attention(lambda t, i: view[t][:, i, :], lambda t, i: view[t][:, H + i // (H // KVH), :],
                             lambda t, i: view[t][:, HK + i // (H // KVH), :], H, N, N, N ** -0.5,
                             lambda i: y[:, :, i * N:(i + 1) * N], have, mask=const("band"), causal=True, sink=sinks)
            turned = transpose_tiles(y, 4, have, yT[:, NT4:KD, :])
            project(yT, KD, a["e_w_out_2"][0], D, [turned, lru_ready], add_to_h)

        def deltanet():
            H, N, W = 8, 128, 1024
            enter("gdn")
            par = Params("gdn")
            g_in = par.cols(a["ln_mix_2"][1], D)
            taps = room(24 * 4).rearrange("p (i j) -> p i j", j=4)
            for j in range(4):
                par.load(taps[:, :, j], a["o_conv_w_2"][0][j].rearrange("(i p) -> p i", p=P))
            alog = par.rows(a["o_a_log_2"][0], H)
            dtb = par.rows(a["o_dt_bias_2"][0], H)
            g_out = par.rows(a["o_out_norm_2"][0], N)
            qkv = room3(TT, 3 * W)
            gab = room3(TT, W + 2 * H)
            small = {n: room3(TT, H) for n in ("log_decay", "beta", "cum", "grow", "to_end")}
            soft = [room3(TT, H) for _ in range(3)]
            cumT, betaT = room(T), room(T)
            keep = top[0]
            normed = norm_turned(h, D, None, xT, g_in, par.landed())
            top[0] = keep

            def finish(i, squash, done, free):
                ready = squash(done, [free, normed])
                bank = take_bank()

                @block.tensor
                def _(pe):
                    for due in unseen(pe, bank.free, ready):
                        pe.wait_ge(*due)
                    for t in range(TT):
                        last = pe.transpose(bank.ap[:, t * P:(t + 1) * P], done[:, t * P:(t + 1) * P], ident)
                    last.then_inc(*M.tick())
                turned = M.at()

                @block.scalar
                def _(act):
                    act.wait_ge(*turned)
                    act.copy(qkv[:, :, i * P:(i + 1) * P], bank.ap[:, 0:T].rearrange("p (t n) -> p t n", t=TT)).then_inc(*S.tick())
                bank.free = S.at()
                return turned
            conv_project(a["o_w_in_2"][0], 0, 24, taps, None, par.landed(), normed, ACT.Silu, finish)
            project(xT, KD, a["o_w_in_2"][0], W + 2 * H, normed, copy_out(gab), first_col=3 * W)
            have = both()
            enter("delta", keep)
            qk = qkv[:, :, 0:2 * W]
            scratch = room3(TT, W)
            roots = [None, None]
            for j in range(2):
                x = qkv[:, :, j * W:(j + 1) * W].rearrange("p t (h n) -> p t h n", n=N)
                for t in range(TT):
                    xt = x[:, t]
                    r, root = per_head_rstd(xt, H, N, V.at(), False, EPS,
                                            scratch[:, t, :].rearrange("p (h n) -> p h n", n=N))

                    @block.vector
                    def _(dve):
                        dve.wait_ge(*root)
                        if j == 0:
                            dve.tensor_scalar(r, r, N ** -0.5, None, ALU.mult).then_inc(*V.tick())
                            dve.wait_ge(*V.at())
                        dve.tensor_tensor(xt, xt, r.unsqueeze(2).to_broadcast([P, H, N]), ALU.mult).then_inc(*V.tick())
            qk_done = V.at()
            ld, beta, cum, grow, to_end = (small[n] for n in ("log_decay", "beta", "cum", "grow", "to_end"))
            wide = lambda r: r.unsqueeze(1).to_broadcast([P, TT, H])

            @block.vector
            def _(dve):
                dve.tensor_tensor(ld, gab[:, :, W:W + H], wide(dtb), ALU.add).then_inc(*V.tick())
            have = softplus(ld, soft, V.at())

            @block.scalar
            def _(act):
                act.activation(alog, alog, ACT.Exp).then_inc(*S.tick())
                act.activation(beta, gab[:, :, W + H:W + 2 * H], ACT.Sigmoid).then_inc(*S.tick())
                act.activation(gab[:, :, 0:W], gab[:, :, 0:W], ACT.Silu).then_inc(*S.tick())
            rate = S.at()

            @block.vector
            def _(dve):
                for due in unseen(dve, rate):
                    dve.wait_ge(*due)
                dve.wait_ge(*have)
                dve.scalar_tensor_tensor(out=ld, in0=ld, scalar=-1.0, in1=wide(alog), op0=ALU.mult,
                                         op1=ALU.mult).then_inc(*V.tick())
            have = V.at()
            bank = take_bank()

            @block.tensor
            def _(pe):
                for due in unseen(pe, bank.free):
                    pe.wait_ge(*due)
                pe.wait_ge(*have)
                flat = ld.rearrange("p t h -> p (t h)")
                pe.matmul(bank.ap[:, 0:2 * H], const("upto"), flat, start=True, stop=True)
                pe.matmul(bank.ap[:, 2 * H:4 * H], const("ones"), flat, start=True, stop=True).then_inc(*M.tick())
            have = M.at()

            @block.vector
            def _(dve):
                dve.wait_ge(*have)
                dve.tensor_copy(cum, bank.ap[:, 0:2 * H].rearrange("p (t h) -> p t h", t=TT)).then_inc(*V.tick())
                dve.wait_ge(*V.at())
                dve.tensor_tensor(to_end, bank.ap[:, 2 * H:4 * H].rearrange("p (t h) -> p t h", t=TT), cum,
                                  ALU.subtract).then_inc(*V.tick())
            bank.free = V.at()
            have = V.at()

            @block.scalar
            def _(act):
                act.wait_ge(*have)
                act.activation(grow, cum, ACT.Exp).then_inc(*S.tick())
                act.activation(to_end, to_end, ACT.Exp).then_inc(*S.tick())
            exp_done = S.at()
            bank = take_bank()

            @block.tensor
            def _(pe):
                for due in unseen(pe, bank.free, rate):
                    pe.wait_ge(*due)
                pe.wait_ge(*have)
                for j, x in enumerate((cum, beta)):
                    for t in range(TT):
                        at = j * T + t * P
                        last = pe.transpose(bank.ap[0:H, at:at + P], x[:, t, :], ident)
                last.then_inc(*M.tick())
            have = M.at()

            @block.vector
            def _(dve):
                dve.wait_ge(*have)
                dve.tensor_copy(cumT[0:H, :], bank.ap[0:H, 0:T]).then_inc(*V.tick())
                dve.tensor_copy(betaT[0:H, :], bank.ap[0:H, T:2 * T]).then_inc(*V.tick())
            bank.free = V.at()
            rows_ready = V.at()
            top[0] = keep
            qkT = room3(16, T)
            turned = transpose_tiles(qk, 16, [qk_done, rows_ready], qkT)
            qT, kT = qkT[:, 0:8, :], qkT[:, 8:16, :]
            q, k, v = (qkv[:, :, j * W:(j + 1) * W] for j in range(3))
            y = q

            @block.vector
            def _(dve):
                for due in unseen(dve, exp_done):
                    dve.wait_ge(*due)
                dve.wait_ge(*turned)
                kh = k[:, 0, :].rearrange("p (h n) -> p h n", n=N)
                dve.tensor_tensor(kh, kh, to_end[:, 0, :].unsqueeze(2).to_broadcast([P, H, N]), ALU.mult).then_inc(*V.tick())
            decayed = V.at()
            state = room(H * N)
            state_ready = None
            names = ("X", "XT", "Y", "NL", "NT", "QK", "DT", "DS", "rhs", "new")
            work = [{n: room(512) for n in names} for _ in range(2)]
            idle = [None, None]
            r4 = lambda ap: ap.rearrange("p (g n) -> p g n", g=4)
            for t in range(TT):
                tok = slice(t * P, (t + 1) * P)
                groups = []
                for g in range(2):
                    w = dict(work[g])
                    hs = range(4 * g, 4 * g + 4)
                    cols = slice(4 * g * N, 4 * (g + 1) * N)
                    bank = take_bank()

                    @block.tensor
                    def _(pe):
                        for due in unseen(pe, bank.free, rows_ready):
                            pe.wait_ge(*due)
                        for j, i in enumerate(hs):
                            last = pe.matmul(bank.ap[:, j * P:(j + 1) * P], ident[0:H, i:i + 1].to_broadcast([H, P]),
                                             cumT[0:H, tok], start=True, stop=True)
                        last.then_inc(*M.tick())
                    have = M.at()

                    @block.vector
                    def _(dve):
                        for due in unseen(dve, have, idle[g]):
                            dve.wait_ge(*due)
                        for j, i in enumerate(hs):
                            c = slice(j * P, (j + 1) * P)
                            dve.scalar_tensor_tensor(out=w["DT"][:, c], in0=bank.ap[:, c], scalar=cum[:, t, i:i + 1],
                                                     in1=const("after_neg"), op0=ALU.subtract,
                                                     op1=ALU.add).then_inc(*V.tick())
                    bank.free = V.at()
                    have = V.at()

                    @block.scalar
                    def _(act):
                        act.wait_ge(*have)
                        act.activation(w["DT"], w["DT"], ACT.Exp).then_inc(*S.tick())
                    have = S.at()

                    @block.gpsimd
                    def _(pool):
                        for due in unseen(pool, have, idle[g]):
                            pool.wait_ge(*due)
                        pool.tensor_tensor(r4(w["DS"]), r4(w["DT"]), const("before").unsqueeze(1).to_broadcast([P, 4, P]),
                                           ALU.mult).then_inc(*G.tick())
                    strict = G.at()
                    bk, bq, bb = take_bank(), take_bank(), take_bank()

                    @block.tensor
                    def _(pe):
                        for due in unseen(pe, bk.free, bq.free, bb.free):
                            pe.wait_ge(*due)
                        pe.wait_ge(*turned)
                        for j, i in enumerate(hs):
                            c = slice(j * P, (j + 1) * P)
                            pe.matmul(bk.ap[:, c], kT[:, i, tok], kT[:, i, tok], start=True, stop=True)
                            pe.matmul(bq.ap[:, c], kT[:, i, tok], qT[:, i, tok], start=True, stop=True)
                            last = pe.matmul(bb.ap[:, c], ident[0:H, i:i + 1].to_broadcast([H, P]), betaT[0:H, tok],
                                             start=True, stop=True)
                        last.then_inc(*M.tick())
                    have = M.at()

                    @block.vector
                    def _(dve):
                        for due in unseen(dve, strict):
                            dve.wait_ge(*due)
                        dve.wait_ge(*have)
                        dve.scalar_tensor_tensor(out=w["NT"], in0=bk.ap, scalar=-1.0, in1=w["DS"], op0=ALU.mult,
                                                 op1=ALU.mult).then_inc(*V.tick())
                        dve.tensor_tensor(w["QK"], bq.ap, w["DT"], ALU.mult).then_inc(*V.tick())
                        dve.wait_ge(*V.at())
                        dve.tensor_tensor(w["NT"], w["NT"], bb.ap, ALU.mult).then_inc(*V.tick())
                    bk.free = bq.free = bb.free = V.at()
                    w.update(made=V.at(), hs=hs, cols=cols)
                    groups.append(w)
                for w in groups:
                    w["N"] = bank = take_bank()

                    @block.tensor
                    def _(pe):
                        for due in unseen(pe, bank.free, w["made"]):
                            pe.wait_ge(*due)
                        for j in range(4):
                            c = slice(j * P, (j + 1) * P)
                            last = pe.transpose(bank.ap[:, c], w["NT"][:, c], ident)
                        last.then_inc(*M.tick())
                    w["ready"] = [w["made"], M.at()]
                    w["NT"] = r4(w["NT"])
                invert(groups)
                for g, w in enumerate(groups):
                    hs, cols = w["hs"], w["cols"]
                    have = None
                    vt = v[:, t, cols]
                    if t:
                        bank = take_bank()

                        @block.tensor
                        def _(pe):
                            for due in unseen(pe, bank.free, state_ready):
                                pe.wait_ge(*due)
                            for j, i in enumerate(hs):
                                last = pe.matmul(bank.ap[:, j * P:(j + 1) * P], kT[:, i, tok], state[:, i * N:(i + 1) * N],
                                                 start=True, stop=True)
                            last.then_inc(*M.tick())
                        have = M.at()

                    @block.vector
                    def _(dve):
                        for due in unseen(dve, have, idle[g]):
                            dve.wait_ge(*due)
                        if t:
                            dve.tensor_tensor(r4(w["rhs"]), r4(bank.ap), grow[:, t, hs[0]:hs[0] + 4].unsqueeze(2).to_broadcast([P, 4, N]),
                                              ALU.mult).then_inc(*V.tick())
                            dve.wait_ge(*V.at())
                            dve.tensor_tensor(w["rhs"], vt, w["rhs"], ALU.subtract).then_inc(*V.tick())
                            dve.wait_ge(*V.at())
                        dve.tensor_tensor(r4(w["rhs"]), r4(w["rhs"] if t else vt),
                                          beta[:, t, hs[0]:hs[0] + 4].unsqueeze(2).to_broadcast([P, 4, N]),
                                          ALU.mult).then_inc(*V.tick())
                    if t:
                        bank.free = V.at()
                    have = V.at()
                    bank = take_bank()

                    @block.tensor
                    def _(pe):
                        for due in unseen(pe, bank.free, w["have"]):
                            pe.wait_ge(*due)
                        pe.wait_ge(*have)
                        for j in range(4):
                            c = slice(j * P, (j + 1) * P)
                            last = pe.matmul(bank.ap[:, c], w["XT"][:, c], w["rhs"][:, c], start=True, stop=True)
                        last.then_inc(*M.tick())
                    have = M.at()

                    @block.scalar
                    def _(act):
                        for due in unseen(act, have, idle[g]):
                            act.wait_ge(*due)
                        act.copy(w["new"], bank.ap).then_inc(*S.tick())
                    bank.free = S.at()
                    have = S.at()
                    bo, bs = take_bank(), take_bank()

                    @block.tensor
                    def _(pe):
                        for due in unseen(pe, bo.free, bs.free, decayed):
                            pe.wait_ge(*due)
                        pe.wait_ge(*have)
                        for j, i in enumerate(hs):
                            c = slice(j * P, (j + 1) * P)
                            hc = slice(i * N, (i + 1) * N)
                            pe.matmul(bo.ap[:, c], w["QK"][:, c], w["new"][:, c], start=True, stop=True)
                            if t:
                                last = pe.matmul(bs.ap[:, c], qT[:, i, tok], state[:, hc], start=True, stop=True)
                            else:
                                last = pe.matmul(bs.ap[:, c], k[:, 0, hc], w["new"][:, c], start=True, stop=True)
                        last.then_inc(*M.tick())
                    have = M.at()
                    idle[g] = M.at()

                    @block.scalar
                    def _(act):
                        act.wait_ge(*have)
                        act.copy(y[:, t, cols], bo.ap).then_inc(*S.tick())
                        if not t:
                            act.copy(state[:, cols], bs.ap).then_inc(*S.tick())
                    bo.free = bs.free = S.at()
                    if t:
                        have = S.at()

                        @block.vector
                        def _(dve):
                            dve.wait_ge(*have)
                            dve.tensor_tensor(r4(w["rhs"]), r4(bs.ap), grow[:, t, hs[0]:hs[0] + 4].unsqueeze(2).to_broadcast([P, 4, N]),
                                              ALU.mult).then_inc(*V.tick())
                            dve.wait_ge(*V.at())
                            dve.tensor_tensor(y[:, t, cols], y[:, t, cols], w["rhs"], ALU.add).then_inc(*V.tick())
                        bs.free = V.at()
                state_ready = S.at()
            have = both()
            top[0] = keep
            scratch = v[:, :, :].rearrange("p t (h n) -> p t h n", n=N)
            for t in range(TT):
                yt = y[:, t, :].rearrange("p (h n) -> p h n", n=N)
                head_norm(yt, H, N, [have, idle[0], idle[1], V.at()], g_out, scratch[:, t])

            @block.vector
            def _(dve):
                for due in unseen(dve, V.at(), rate):
                    dve.wait_ge(*due)
                dve.tensor_tensor(y, y, gab[:, :, 0:W], ALU.mult).then_inc(*V.tick())
            turned = transpose_tiles(y, KD, V.at(), xT)
            project(xT, KD, a["o_w_out_2"][0], D, turned, add_to_h)

        enter("start")
        const_sem = new_semaphore("constants_landed")
        x_sem = new_semaphore("x_landed")

        @block.sync
        def _(sp):
            sp.dma_start(consts[:], a["constants"]).then_inc(const_sem, 16)
            sp.dma_start(h, a["x"][0].rearrange("(t p) d -> p t d", p=P)).then_inc(x_sem, 16)

        @block.vector
        def _(dve):
            dve.wait_ge(const_sem, 16)
            dve.wait_ge(x_sem, 16)

        @block.scalar
        def _(act):
            act.wait_ge(const_sem, 16)
            act.wait_ge(x_sem, 16)

        @block.tensor
        def _(pe):
            pe.wait_ge(const_sem, 16)
            pe.wait_ge(x_sem, 16)

        @block.gpsimd
        def _(pool):
            pool.wait_ge(const_sem, 16)
            pool.wait_ge(x_sem, 16)
        F = 2816

        def ffn_src(layer):
            w13, w2 = a["ffn_w13"][layer], a["ffn_w2"][layer]

            def src(which, c):
                if which == "down":
                    return w2[bass.ds(c, 256), :]
                return w13[:, bass.ds(c if which == "gate" else c + F, 256)]
            return src

        def dense_src(which, c):
            if which == "down":
                return a["e_ffn_w_down_2"][0][bass.ds(c, 256), :]
            return a[f"e_ffn_w_{which}_2"][0][:, bass.ds(c, 256)]

        plan = {
            "mem": memory_once,
            "mix0": mla_and_rwkv,
            "cross0": lambda: cross(0),
            "ffn0": lambda: swiglu("ffn0", a["ffn_norm"][0], ffn_src(0), F // 256),
            "mamba": mamba,
            "cross1": lambda: cross(1),
            "ffn1": lambda: swiglu("ffn1", a["ffn_norm"][1], ffn_src(1), F // 256),
            "mix2": lru_and_window,
            "ffn2": lambda: swiglu("ffn2", a["ln_ffn_2"][0], dense_src, F // 256),
            "gdn": deltanet,
            "moe": experts_by_tile,
        }
        for name, emit in plan.items():
            if stages is None or name in stages:
                emit()
        stored = new_semaphore("output_stored")
        last = [lane.at() for lane in (V, S, M, G) if lane.count]

        @block.sync
        def _(sp):
            for due in unseen(sp, last):
                sp.wait_ge(*due)
            sp.dma_start(out[0].rearrange("(t p) d -> p t d", p=P), h).then_inc(stored, 16)
            sp.wait_ge(stored, 16)


def kernel(**inputs):
    from concourse import bacc
    from concourse.bass_utils import run_bass_kernel_spmd

    nc = bacc.Bacc("TRN2", target_bir_lowering=False, num_devices=1)
    arrays, aps = {}, {}
    for name, value in [*inputs.items(), ("constants", CONSTANTS)]:
        value = np.ascontiguousarray(value)
        arrays[f"in_{name}"] = value
        aps[name] = nc.dram_tensor(f"in_{name}", value.shape, mybir.dt.from_np(value.dtype), kind="ExternalInput").ap()
    out = nc.dram_tensor("out", (1, T, D), F32, kind="ExternalOutput").ap()
    build(nc, aps, out)
    result = run_bass_kernel_spmd(nc, [arrays], core_ids=[0])
    return result.results[0]["out"]
```

```python
from contextlib import ExitStack

import numpy as np
import concourse.bass as bass
from concourse import mybir

F32 = mybir.dt.float32
F32R = mybir.dt.float32r
I32 = mybir.dt.int32
U32 = mybir.dt.uint32
ALU = mybir.AluOpType
ACT = mybir.ActivationFunctionType
AX = mybir.AxisListType.X

P = 128
T = 256
TT = T // P
D = 1024
KD = D // P
EPS = 1e-6
NEG = -1e30
LEVELS = [2, 4, 8, 16, 32, 64]
BANKS = 8
BANK = 512
SLOTS = 4
SLOT = 4096
UNIT = 6144
TWO_PI = 2 * np.pi
PI_C1 = 6.28125
PI_C2 = float(np.float32(TWO_PI - PI_C1))
ROUND = 1.5 * 2.0 ** 23


def shape_constants():
    p = np.arange(P)[:, None]
    f = np.arange(P)[None, :]
    q = (np.arange(TT)[None, :, None] * P + p[:, :, None])
    k = np.arange(T)[None, None, :]
    parts = {}
    parts["ident"] = (p == f)
    parts["ones"] = np.ones((P, P))
    parts["upto"] = (p <= f)
    parts["before"] = (p < f)
    parts["upto_mid"] = (p <= f) * 1.0 - (p < P // 2)
    parts["halves"] = np.stack([np.arange(P) < P // 2, np.arange(P) >= P // 2], 1)
    parts["after_neg"] = np.where(p <= f, 0.0, NEG)
    parts["pair_t"] = (p // 2 == f // 2) & (p % 2 == 0) & (f % 2 == 1)
    parts["pair"] = parts["pair_t"].T
    for s in LEVELS:
        parts[f"level{s}"] = (p // (2 * s) == f // (2 * s)) & (p % (2 * s) < s) & (f % (2 * s) >= s)
    parts["quad"] = np.concatenate([p < f, p <= f, p < f, p <= f], 1)
    parts["causal"] = np.where(k <= q, 0.0, NEG).reshape(P, TT * T)
    parts["band"] = np.where((k <= q) & (q - k < 128), 0.0, NEG).reshape(P, TT * T)
    inv16 = np.float32(10000.0) ** (-np.arange(16, dtype=np.float32) / np.float32(16))
    parts["inv_freq"] = np.broadcast_to(inv16.astype(np.float32)[None], (P, 16))
    inv32 = np.float32(10000.0) ** (-np.arange(32, dtype=np.float32) / np.float32(32))
    ang = (q[:, :, 0].astype(np.float32)[:, :, None] * inv32.astype(np.float32)).astype(np.float32)
    parts["rope_cos"] = np.cos(ang).reshape(P, -1)
    parts["rope_sin"] = np.sin(ang).reshape(P, -1)
    parts["ramp"] = np.broadcast_to(f, (P, P))
    parts["minus_half"] = np.full((P, 16), -0.5)
    at, where = 0, {}
    for name, a in parts.items():
        where[name] = (at, a.shape[1])
        at += a.shape[1]
    return np.concatenate([np.asarray(a, np.float32) for a in parts.values()], 1), where


CONSTANTS, CONST_AT = shape_constants()


class Lane:

    def __init__(self, new_semaphore, engine):
        self.new_semaphore, self.engine, self.sem, self.count = new_semaphore, engine, None, 0

    def enter(self, stage):
        self.sem, self.count = self.new_semaphore(f"{stage}_{self.engine}_done"), 0

    def tick(self):
        self.count += 1
        return self.sem, 1

    def at(self):
        return self.sem, self.count


class Bank:

    def __init__(self, ap):
        self.ap, self.free = ap, None


class Slot:

    def __init__(self, ap, low, sem):
        self.ap, self.low, self.sem, self.loads, self.free, self.lent = ap, low, sem, 0, None, False


def build(nc, a, out, stages=None):
    with ExitStack() as ctx:
        def new_semaphore(name):
            return ctx.enter_context(nc.semaphore(name))

        def sb(name, cols, dt=F32):
            return ctx.enter_context(nc.sbuf_tensor(name, [P, cols], dt))

        consts = sb("consts", CONSTANTS.shape[1])
        h_sb = sb("h", TT * D)
        xT_base = nc.sbuf_base
        xT_sb = sb("xT", KD * T)
        memT_sb = sb("memT", KD * T)
        ring_base = nc.sbuf_base
        ring = sb("ring", SLOTS * SLOT)
        ring_low = nc.alloc_sbuf_tensor_at("ring_low", [P, SLOTS * SLOT], F32R, offset=ring_base)
        SMALL = 1560
        small = sb("small_tensors", SMALL)
        small_top = [0]
        ARENA = 27040 - SMALL
        arena_base = nc.sbuf_base
        arena = sb("arena", ARENA)
        psum = ctx.enter_context(nc.psum_tensor("banks", [P, BANKS * BANK], F32))

        h = h_sb[:].rearrange("p (t d) -> p t d", t=TT)
        xT = xT_sb[:].rearrange("p (k t) -> p k t", t=T)
        in_three = lambda tensor: tensor[:].rearrange("p (k t) -> p k t", t=T)
        x_high = in_three(nc.alloc_sbuf_tensor_at("x_high", [P, KD * T], F32R, offset=xT_base))
        x_low = in_three(nc.alloc_sbuf_tensor_at("x_low", [P, KD * T], F32R, offset=arena_base + 4 * (ARENA - KD * T)))
        x_parts = (x_high, x_low)
        PIECES, PIECE = 6, 1024
        piece_ring = nc.alloc_sbuf_tensor_at("pieces_high", [P, PIECES * PIECE], F32R,
                                             offset=arena_base + 4 * (ARENA - KD * T - PIECES * PIECE))
        piece_turn, piece_free = [0], [None] * PIECES
        memT = memT_sb[:].rearrange("p (k t) -> p k t", t=T)

        def const(name):
            at, n = CONST_AT[name]
            return consts[:, at:at + n]

        ident = const("ident")
        banks = [Bank(psum[:, b * BANK:(b + 1) * BANK]) for b in range(BANKS)]
        turn = [0]

        def take_bank():
            turn[0] += 1
            return banks[(turn[0] - 1) % BANKS]

        part_turn = {}

        def take_bank_of(n, first):
            part_turn[first] = part_turn.get(first, -1) + 1
            return banks[first + part_turn[first] % n]

        slots = [Slot(ring[:, s * SLOT:(s + 1) * SLOT], ring_low[:, s * SLOT:(s + 1) * SLOT], new_semaphore(f"ring{s}_landed")) for s in range(SLOTS)]
        slot_turn = [0]

        top = [0]

        def room(cols, dt=F32):
            ap = arena[:, top[0]:top[0] + cols]
            top[0] += cols
            assert top[0] <= ARENA, top[0]
            return ap if dt == F32 else ap.bitcast(dt)

        def split_room(name, cols):
            top[0] = -(-top[0] // 8) * 8
            tensor = nc.alloc_sbuf_tensor_at(name, [P, cols], F32R, offset=arena_base + 4 * top[0])
            top[0] += cols
            assert top[0] <= ARENA, top[0]
            return tensor[:]

        def passes(pe, out_, left, right, start, stop):
            (lh, ll), (rh, rl) = left, right
            pe.matmul(out_, lh, rh, start=start, stop=False)
            pe.matmul(out_, ll, rh, start=False, stop=False)
            return pe.matmul(out_, lh, rl, start=False, stop=stop)

        def room3(n, m):
            return room(n * m).rearrange("p (n m) -> p n m", m=m)

        V, S, M, G = (Lane(new_semaphore, n) for n in ("vector", "scalar", "tensor", "gpsimd"))
        block = ctx.enter_context(nc.Block())
        waited = {}

        def unseen(eng, *marks):
            for m in marks:
                if isinstance(m, list):
                    yield from unseen(eng, *m)
                elif m is not None and m[1] > waited.get((eng.engine, m[0].name), 0):
                    waited[eng.engine, m[0].name] = m[1]
                    yield m

        def enter(stage, keep=0):
            before = [lane.at() for lane in (V, S, M, G) if lane.count]
            for lane in (V, S, M, G):
                lane.enter(stage)

            @block.vector
            def _(dve):
                for due in unseen(dve, before):
                    dve.wait_ge(*due)

            @block.scalar
            def _(act):
                for due in unseen(act, before):
                    act.wait_ge(*due)

            @block.tensor
            def _(pe):
                for due in unseen(pe, before):
                    pe.wait_ge(*due)

            @block.gpsimd
            def _(pool):
                for due in unseen(pool, before):
                    pool.wait_ge(*due)

            top[0] = keep

        class Params:

            def __init__(self, stage, local=False, by_sync=None):
                self.sem, self.loads, self.local = new_semaphore(f"{stage}_params_landed"), 0, local
                self.by_sync = not local if by_sync is None else by_sync

            def space(self, cols, dt=F32):
                if self.local:
                    return room(cols, dt)
                ap = small[:, small_top[0]:small_top[0] + cols]
                small_top[0] += cols
                assert small_top[0] <= SMALL, small_top[0]
                return ap if dt == F32 else ap.bitcast(dt)

            def load(self, dst, src):
                self.loads += 1
                if self.by_sync:
                    @block.sync
                    def _(sp):
                        sp.dma_start(dst, src, allow_slow_non_contiguous=True).then_inc(self.sem, 16)
                    return dst

                @block.gpsimd
                def _(pool):
                    pool.dma_start(dst, src, allow_slow_non_contiguous=True).then_inc(self.sem, 16)
                return dst

            def rows(self, src, n):
                return self.load(self.space(n), src.partition_broadcast(P))

            def cols(self, src, n):
                return self.load(self.space(n // P), src.rearrange("(k p) -> p k", p=P))

            def landed(self):
                return self.sem, 16 * self.loads

        def take_slot():
            while slots[slot_turn[0] % SLOTS].lent:
                slot_turn[0] += 1
            slot_turn[0] += 1
            return slots[(slot_turn[0] - 1) % SLOTS]

        def load_weights(src, shape3):
            slot = take_slot()
            n = shape3[1] * shape3[2]
            view = slot.ap[0:shape3[0], 0:n].rearrange("p (k n) -> p k n", n=shape3[2])
            low = slot.low[0:shape3[0], 0:n].rearrange("p (k n) -> p k n", n=shape3[2])

            @block.sync
            def _(sp):
                for due in unseen(sp, slot.free):
                    sp.wait_ge(*due)
                sp.dma_start(view, src.rearrange("(k p) n -> p k n", p=shape3[0])).then_inc(slot.sem, 16)
            slot.loads += 1
            return slot, view, low, (slot.sem, 16 * slot.loads)

        def transpose_tiles(src, n_k, ready, dst, gain=None, gain_ready=None):
            marks = []
            for k0 in range(0, n_k, 2):
                ks = range(k0, min(k0 + 2, n_k))
                bank = take_bank()

                @block.tensor
                def _(pe):
                    for due in unseen(pe, bank.free, ready):
                        pe.wait_ge(*due)
                    for k in ks:
                        for t in range(TT):
                            at = (k - k0) * T + t * P
                            last = pe.transpose(bank.ap[:, at:at + P], src[:, t, k * P:(k + 1) * P], ident)
                    last.then_inc(*M.tick())
                turned = M.at()

                if gain is None:
                    @block.scalar
                    def _(act):
                        act.wait_ge(*turned)
                        act.copy(dst[:, k0:k0 + len(ks), :],
                                 bank.ap[:, 0:len(ks) * T].rearrange("p (k t) -> p k t", t=T)).then_inc(*S.tick())
                    bank.free = S.at()
                else:
                    @block.vector
                    def _(dve):
                        for due in unseen(dve, gain_ready):
                            dve.wait_ge(*due)
                        dve.wait_ge(*turned)
                        for k in ks:
                            dve.tensor_scalar(dst[:, k, :], bank.ap[:, (k - k0) * T:(k - k0 + 1) * T],
                                              gain[:, k:k + 1], None, ALU.mult).then_inc(*V.tick())
                    bank.free = V.at()
            return V.at() if gain is not None else S.at()

        def transpose_split(src, n_k, ready, high, low, gain, gain_ready):
            for k0 in range(0, n_k, 2):
                ks = range(k0, min(k0 + 2, n_k))
                bank = take_bank()

                @block.tensor
                def _(pe):
                    for due in unseen(pe, bank.free, ready):
                        pe.wait_ge(*due)
                    for k in ks:
                        for t in range(TT):
                            at = (k - k0) * T + t * P
                            last = pe.transpose(bank.ap[:, at:at + P], src[:, t, k * P:(k + 1) * P], ident)
                    last.then_inc(*M.tick())
                turned = M.at()
                part = lambda k: bank.ap[:, (k - k0) * T:(k - k0 + 1) * T]

                @block.scalar
                def _(act):
                    for due in unseen(act, gain_ready):
                        act.wait_ge(*due)
                    act.wait_ge(*turned)
                    for k in ks:
                        if gain is None:
                            act.copy(high[:, k, :], part(k)).then_inc(*S.tick())
                        else:
                            act.activation(high[:, k, :], part(k), ACT.Identity, scale=gain[:, k:k + 1]).then_inc(*S.tick())
                rounded = S.at()

                @block.vector
                def _(dve):
                    for due in unseen(dve, gain_ready):
                        dve.wait_ge(*due)
                    dve.wait_ge(*rounded)
                    for k in ks:
                        rest = high[:, k, :].bitcast(F32)
                        if gain is None:
                            dve.tensor_tensor(low[:, k, :], part(k), rest, ALU.subtract).then_inc(*V.tick())
                        else:
                            dve.scalar_tensor_tensor(out=low[:, k, :], in0=part(k), scalar=gain[:, k:k + 1], in1=rest,
                                                     op0=ALU.mult, op1=ALU.subtract).then_inc(*V.tick())
                bank.free = V.at()
            return V.at()

        def reciprocal_root(x, n, ready):
            @block.gpsimd
            def _(pool):
                for due in unseen(pool, ready):
                    pool.wait_ge(*due)
                pool.tensor_tensor(x, x, const("minus_half")[:, 0:n], ALU.pow).then_inc(*G.tick())
            return G.at()

        def row_rstd(src, n, ready, eps=EPS):
            square = room(n)
            rstd = room(TT)

            @block.scalar
            def _(act):
                for due in unseen(act, ready):
                    act.wait_ge(*due)
                for t in range(TT):
                    for due in unseen(act, S.at() if t else None):
                        act.wait_ge(*due)
                    act.activation(square, src[:, t, :], ACT.Square, accum_out=rstd[:, t:t + 1]).then_inc(*S.tick())
            summed = S.at()

            @block.vector
            def _(dve):
                dve.wait_ge(*summed)
                dve.tensor_scalar(rstd, rstd, 1.0 / n, eps, ALU.mult, ALU.add).then_inc(*V.tick())
            return rstd, reciprocal_root(rstd, TT, V.at())

        def norm_rows(src, n, ready, eps=EPS):
            rstd, have = row_rstd(src, n, ready, eps)
            scaled = room3(TT, n)

            @block.vector
            def _(dve):
                dve.wait_ge(*have)
                for t in range(TT):
                    dve.tensor_scalar(scaled[:, t, :], src[:, t, :], rstd[:, t:t + 1], None,
                                      ALU.mult).then_inc(*V.tick())
            return scaled, V.at()

        def norm_turned(src, n, ready, dst, gain, gain_ready):
            scaled, have = norm_rows(src, n, ready)
            if not isinstance(dst, tuple):
                return transpose_tiles(scaled, n // P, have, dst, gain, gain_ready)
            return transpose_split(scaled, n // P, have, *dst, gain, gain_ready)

        def project(lhs, n_k, w, n_cols, ready, take, first_col=0, rows=P):
            chunk = 512 if n_k <= 8 else 256
            for c0 in range(0, n_cols, chunk):
                n = min(chunk, n_cols - c0)
                slot, view, _, landed = load_weights(w[:, first_col + c0:first_col + c0 + n], (rows, n_k, n))
                for t in range(TT):
                    bank = take_bank()

                    @block.tensor
                    def _(pe):
                        for due in unseen(pe, bank.free, ready, landed):
                            pe.wait_ge(*due)
                        for k in range(n_k):
                            last = pe.matmul(bank.ap[:, 0:n], lhs[0:rows, k, t * P:(t + 1) * P], view[:, k, :],
                                             start=(k == 0), stop=(k == n_k - 1))
                        last.then_inc(*M.tick())
                    slot.free = M.at()
                    bank.free = take(bank.ap[:, 0:n], M.at(), t, c0, n)

        on_pool = [True]

        def split_piece(view, low_view, shape, landed, after=None):
            at = piece_turn[0] % PIECES
            piece_turn[0] += 1
            n_p, n_k, n = shape
            high = piece_ring[0:n_p, at * PIECE:at * PIECE + n_k * n].rearrange("p (k n) -> p k n", n=n)

            @block.scalar
            def _(act):
                for due in unseen(act, landed, piece_free[at], after):
                    act.wait_ge(*due)
                act.copy(high, view).then_inc(*S.tick())
            rounded = S.at()

            def take_rest():
                if at % 2 or not on_pool[0]:
                    @block.vector
                    def _(dve):
                        dve.wait_ge(*rounded)
                        dve.tensor_tensor(low_view, view, high.bitcast(F32), ALU.subtract).then_inc(*V.tick())
                    return V.at()

                @block.gpsimd
                def _(pool):
                    pool.wait_ge(*rounded)
                    pool.tensor_tensor(low_view, view, high.bitcast(F32), ALU.subtract).then_inc(*G.tick())
                return G.at()
            return high, at, take_rest

        def run_ahead(i, count, split_one, split, parts_ready):
            if 0 <= i + PIECES - 1 < count:
                split_one(i + PIECES - 1)
            if 0 <= i + PIECES - 2 < count:
                parts_ready[i + PIECES - 2] = split[i + PIECES - 2][2]()

        def project_parts(lhs, n_k, w, n_cols, ready, take, first_col=0, after=None, during={}):
            rows = P
            chunk = 512 if n_k <= 8 else 256
            pieces, split, parts_ready = [], {}, {}
            for c0 in range(0, n_cols, chunk):
                n = min(chunk, n_cols - c0)
                each = max(1, PIECE // n)
                pieces += [(c0, n, k0, min(k0 + each, n_k)) for k0 in range(0, n_k, each)]
            slot_of_chunk = {}

            def split_one(i):
                c0, n, k0, k1 = pieces[i]
                if k0 == 0:
                    slot_of_chunk[c0] = load_weights(w[:, first_col + c0:first_col + c0 + n], (rows, n_k, n))
                _, view, low, landed = slot_of_chunk[c0]
                split[i] = split_piece(view[:, k0:k1, :], low[:, k0:k1, :], (rows, k1 - k0, n), landed, after)
            for i in range(1 - PIECES, 0):
                run_ahead(i, len(pieces), split_one, split, parts_ready)
            for i, (c0, n, k0, k1) in enumerate(pieces):
                run_ahead(i, len(pieces), split_one, split, parts_ready)
                if k0 == 0:
                    two = [take_bank() for _ in range(TT)]
                slot, _, low, _ = slot_of_chunk[c0]
                high, at, _ = split[i]

                @block.tensor
                def _(pe):
                    for due in unseen(pe, [b.free for b in two], ready, parts_ready[i]):
                        pe.wait_ge(*due)
                    for k in range(k0, k1):
                        for t in range(TT):
                            tok = slice(t * P, (t + 1) * P)
                            last = passes(pe, two[t].ap[:, 0:n], tuple(x[0:rows, k, tok] for x in lhs),
                                          (high[:, k - k0, :], low[:, k, :]), start=(k == 0), stop=(k == n_k - 1))
                    last.then_inc(*M.tick())
                piece_free[at] = slot.free = M.at()
                if k1 == n_k:
                    for t in range(TT):
                        two[t].free = take(two[t].ap[:, 0:n], slot.free, t, c0, n)
                if i in during:
                    during[i]()

        def project_few(w, first_col, n, ready, dst):
            slot, view, low, landed = load_weights(w[:, first_col:first_col + n], (P, KD, n))
            high, at, take_rest = split_piece(view, low, (P, KD, n), landed)
            parts_ready = take_rest()
            turned_sb = room(T)
            bank, bank2 = take_bank(), take_bank()

            @block.tensor
            def _(pe):
                for due in unseen(pe, bank.free, ready, parts_ready):
                    pe.wait_ge(*due)
                for k in range(KD):
                    last = passes(pe, bank.ap[0:n, 0:T], (high[:, k, :], low[:, k, :]),
                                  (x_high[:, k, :], x_low[:, k, :]), start=(k == 0), stop=(k == KD - 1))
                last.then_inc(*M.tick())
            piece_free[at] = slot.free = have = M.at()

            @block.scalar
            def _(act):
                act.wait_ge(*have)
                act.copy(turned_sb[0:n, :], bank.ap[0:n, 0:T]).then_inc(*S.tick())
            bank.free = copied = S.at()

            @block.tensor
            def _(pe):
                for due in unseen(pe, bank2.free):
                    pe.wait_ge(*due)
                pe.wait_ge(*copied)
                for t in range(TT):
                    last = pe.transpose(bank2.ap[:, t * n:(t + 1) * n], turned_sb[0:n, t * P:(t + 1) * P],
                                        ident[0:n, 0:n])
                last.then_inc(*M.tick())
            have = M.at()

            @block.vector
            def _(dve):
                dve.wait_ge(*have)
                dve.tensor_copy(dst, bank2.ap[:, 0:TT * n].rearrange("p (t n) -> p t n", t=TT)).then_inc(*V.tick())
            bank2.free = V.at()
            return V.at()

        flip = [0]

        def copy_out(dst):
            def take(ps, mark, t, c0, n):
                flip[0] += 1
                if flip[0] % 2:
                    @block.scalar
                    def _(act):
                        act.wait_ge(*mark)
                        act.copy(dst[:, t, c0:c0 + n], ps).then_inc(*S.tick())
                    return S.at()

                @block.vector
                def _(dve):
                    dve.wait_ge(*mark)
                    dve.tensor_copy(dst[:, t, c0:c0 + n], ps).then_inc(*V.tick())
                return V.at()
            return take

        def add_to_h(ps, mark, t, c0, n):
            @block.vector
            def _(dve):
                dve.wait_ge(*mark)
                dve.tensor_tensor(h[:, t, c0:c0 + n], h[:, t, c0:c0 + n], ps, ALU.add).then_inc(*V.tick())
            return V.at()

        def both():
            return [V.at(), S.at()]

        def per_head_rstd(x, n_heads, width, ready, mean, eps, scratch):
            r = room(n_heads)

            @block.vector
            def _(dve):
                for due in unseen(dve, ready):
                    dve.wait_ge(*due)
                dve.tensor_tensor(scratch, x, x, ALU.mult).then_inc(*V.tick())
                dve.wait_ge(*V.at())
                dve.tensor_reduce(r, scratch, AX, ALU.add).then_inc(*V.tick())
                dve.wait_ge(*V.at())
                dve.tensor_scalar(r, r, 1.0 / width if mean else 1.0, eps, ALU.mult, ALU.add).then_inc(*V.tick())
            return r, reciprocal_root(r, n_heads, V.at())

        def head_norm(x, n_heads, width, ready, gain, scratch):
            r, have = per_head_rstd(x, n_heads, width, ready, True, EPS, scratch)

            @block.vector
            def _(dve):
                dve.wait_ge(*have)
                dve.tensor_tensor(x, x, r.unsqueeze(2).to_broadcast([P, n_heads, width]), ALU.mult).then_inc(*V.tick())
                dve.wait_ge(*V.at())
                dve.tensor_tensor(x, x, gain.unsqueeze(1).to_broadcast([P, n_heads, width]), ALU.mult).then_inc(*V.tick())
            return V.at()

        def rotate(x1, x2, cos, sin, shape, ready, scratch):
            a1, a2 = scratch

            @block.vector
            def _(dve):
                for due in unseen(dve, ready):
                    dve.wait_ge(*due)
                dve.tensor_tensor(a1, x2, sin, ALU.mult).then_inc(*V.tick())
                dve.tensor_tensor(a2, x1, sin, ALU.mult).then_inc(*V.tick())
                dve.wait_ge(*V.at())
                dve.tensor_tensor(x1, x1, cos, ALU.mult).then_inc(*V.tick())
                dve.tensor_tensor(x2, x2, cos, ALU.mult).then_inc(*V.tick())
                dve.wait_ge(*V.at())
                dve.tensor_tensor(x1, x1, a1, ALU.subtract).then_inc(*V.tick())
                dve.tensor_tensor(x2, x2, a2, ALU.add).then_inc(*V.tick())
            return V.at()

        def attention(q, k, v, heads, d, dv, scale, y, ready, mask=None, causal=False, sink=None):
            bufs = [{n: room(512) for n in ("qk", "s", "p", "pt")} for _ in range(2)]
            small4 = [{n: room(TT) for n in ("m", "nm", "sum", "es")} for _ in range(4)]
            copied, weights, inverse, turned_p = {}, {}, {}, {}
            qk_used, p_used, pt_used, sum_used = {}, {}, {}, {}

            def turn_qk(i):
                qk = bufs[i % 2]["qk"]
                bank = take_bank()

                @block.tensor
                def _(pe):
                    for due in unseen(pe, bank.free, ready):
                        pe.wait_ge(*due)
                    for j, x in enumerate((q, k)):
                        for t in range(TT):
                            at = j * T + t * P
                            last = pe.transpose(bank.ap[0:d, at:at + P], x(t, i), ident)
                    last.then_inc(*M.tick())
                turned = M.at()

                @block.scalar
                def _(act):
                    for due in unseen(act, turned, qk_used.get(i - 2)):
                        act.wait_ge(*due)
                    act.copy(qk[0:d, :], bank.ap[0:d, :]).then_inc(*S.tick())
                bank.free = S.at()
                copied[i] = S.at()

            def scores(i):
                b, sm = bufs[i % 2], small4[i % 4]
                bank = take_bank()

                @block.tensor
                def _(pe):
                    for due in unseen(pe, bank.free, copied[i]):
                        pe.wait_ge(*due)
                    for t in range(TT):
                        last = pe.matmul(bank.ap[:, t * T:(t + 1) * T], b["qk"][0:d, t * P:(t + 1) * P],
                                         b["qk"][0:d, T:2 * T], start=True, stop=True)
                    last.then_inc(*M.tick())
                have = M.at()
                qk_used[i] = M.at()
                sv = b["s"].rearrange("p (t k) -> p t k", t=TT)

                @block.vector
                def _(dve):
                    for due in unseen(dve, have, weights.get(i - 2), sum_used.get(i - 4)):
                        dve.wait_ge(*due)
                    if mask is not None:
                        dve.scalar_tensor_tensor(out=b["s"], in0=bank.ap, scalar=scale, in1=mask,
                                                 op0=ALU.mult, op1=ALU.add).then_inc(*V.tick())
                    else:
                        dve.tensor_scalar(b["s"], bank.ap, scale, None, ALU.mult).then_inc(*V.tick())
                    dve.wait_ge(*V.at())
                    dve.tensor_reduce(sm["m"], sv, AX, ALU.max).then_inc(*V.tick())
                    dve.wait_ge(*V.at())
                    if sink is not None:
                        dve.tensor_scalar(sm["m"], sm["m"], sink[:, i:i + 1], None, ALU.max).then_inc(*V.tick())
                        dve.wait_ge(*V.at())
                    dve.tensor_scalar(sm["nm"], sm["m"], -1.0, None, ALU.mult).then_inc(*V.tick())
                bank.free = V.at()
                have = V.at()

                @block.scalar
                def _(act):
                    for due in unseen(act, have, p_used.get(i - 2)):
                        act.wait_ge(*due)
                    for t in range(TT):
                        act.activation(b["p"][:, t * T:(t + 1) * T], sv[:, t, :], ACT.Exp, bias=sm["nm"][:, t:t + 1],
                                       accum_out=sm["sum"][:, t:t + 1]).then_inc(*S.tick())
                    if sink is not None:
                        act.activation(sm["es"], sm["nm"], ACT.Exp, bias=sink[:, i:i + 1]).then_inc(*S.tick())
                weights[i] = S.at()

            def turn_weights(i):
                b, sm = bufs[i % 2], small4[i % 4]
                bank = take_bank()

                @block.vector
                def _(dve):
                    for due in unseen(dve, weights[i]):
                        dve.wait_ge(*due)
                    if sink is not None:
                        dve.tensor_tensor(sm["sum"], sm["sum"], sm["es"], ALU.add).then_inc(*V.tick())
                        dve.wait_ge(*V.at())
                    dve.reciprocal(sm["sum"], sm["sum"]).then_inc(*V.tick())
                inverse[i] = V.at()

                @block.tensor
                def _(pe):
                    for due in unseen(pe, bank.free, weights[i]):
                        pe.wait_ge(*due)
                    for kt in range(TT):
                        for t in range(TT):
                            at = kt * T + t * P
                            last = pe.transpose(bank.ap[:, at:at + P], b["p"][:, t * T + kt * P:t * T + (kt + 1) * P],
                                                ident)
                    last.then_inc(*M.tick())
                turned = M.at()
                p_used[i] = M.at()

                @block.scalar
                def _(act):
                    for due in unseen(act, turned, pt_used.get(i - 2)):
                        act.wait_ge(*due)
                    act.copy(b["pt"], bank.ap).then_inc(*S.tick())
                bank.free = S.at()
                turned_p[i] = S.at()

            def values(i):
                b, sm = bufs[i % 2], small4[i % 4]
                bank = take_bank()

                @block.tensor
                def _(pe):
                    for due in unseen(pe, bank.free, turned_p[i]):
                        pe.wait_ge(*due)
                    for t in range(TT):
                        kts = range(t + 1) if causal else range(TT)
                        for kt in kts:
                            at = kt * T + t * P
                            last = pe.matmul(bank.ap[:, t * dv:(t + 1) * dv], b["pt"][:, at:at + P], v(kt, i),
                                             start=(kt == 0), stop=(kt == kts[-1]))
                    last.then_inc(*M.tick())
                have = M.at()
                pt_used[i] = M.at()

                @block.vector
                def _(dve):
                    for due in unseen(dve, inverse[i]):
                        dve.wait_ge(*due)
                    dve.wait_ge(*have)
                    dve.tensor_tensor(y(i), bank.ap[:, 0:TT * dv].rearrange("p (t n) -> p t n", t=TT),
                                      sm["sum"].unsqueeze(2).to_broadcast([P, TT, dv]), ALU.mult).then_inc(*V.tick())
                bank.free = V.at()
                sum_used[i] = V.at()

            for n in range(heads + 3):
                for back, step in enumerate((turn_qk, scores, turn_weights, values)):
                    if 0 <= n - back < heads:
                        step(n - back)
            return V.at()

        def invert(groups):
            r4 = lambda ap: ap.rearrange("p (g n) -> p g n", g=4)
            wide = lambda ap: ap.unsqueeze(1).to_broadcast([P, 4, P])
            for g in groups:
                @block.vector
                def _(dve):
                    for due in unseen(dve, g["ready"]):
                        dve.wait_ge(*due)
                    dve.tensor_tensor(r4(g["X"]), r4(g["N"].ap), wide(const("pair")), ALU.mult).then_inc(*V.tick())
                    dve.tensor_tensor(r4(g["XT"]), g["NT"], wide(const("pair_t")), ALU.mult).then_inc(*V.tick())
                    dve.wait_ge(*V.at())
                    dve.tensor_tensor(r4(g["X"]), r4(g["X"]), wide(ident), ALU.add).then_inc(*V.tick())
                    dve.tensor_tensor(r4(g["XT"]), r4(g["XT"]), wide(ident), ALU.add).then_inc(*V.tick())
                g["N"].free = V.at()
                g["have"] = V.at()
            for n, s in enumerate(LEVELS):
                for g in groups:
                    @block.gpsimd
                    def _(pool):
                        for due in unseen(pool, g["ready"], g.get("level_used")):
                            pool.wait_ge(*due)
                        pool.tensor_tensor(r4(g["NL"]), g["NT"], wide(const(f"level{s}")), ALU.mult).then_inc(*G.tick())
                    level = G.at()
                    bank = take_bank()

                    @block.tensor
                    def _(pe):
                        for due in unseen(pe, bank.free, level, g["have"]):
                            pe.wait_ge(*due)
                        for j in range(4):
                            c = slice(j * P, (j + 1) * P)
                            last = pe.matmul(bank.ap[:, c], g["NL"][:, c], g["X"][:, c], start=True, stop=True)
                        last.then_inc(*M.tick())
                    g["level_used"] = M.at()
                    have = M.at()

                    @block.scalar
                    def _(act):
                        for due in unseen(act, g.get("y_used")):
                            act.wait_ge(*due)
                        act.wait_ge(*have)
                        act.copy(g["Y"], bank.ap).then_inc(*S.tick())
                    bank.free = S.at()
                    have = S.at()
                    bz, bzt = take_bank(), take_bank()
                    final = n == len(LEVELS) - 1

                    @block.tensor
                    def _(pe):
                        for due in unseen(pe, bz.free, bzt.free):
                            pe.wait_ge(*due)
                        pe.wait_ge(*have)
                        for j in range(4):
                            c = slice(j * P, (j + 1) * P)
                            if not final:
                                pe.matmul(bz.ap[:, c], g["XT"][:, c], g["Y"][:, c], start=True, stop=True)
                            last = pe.matmul(bzt.ap[:, c], g["Y"][:, c], g["XT"][:, c], start=True, stop=True)
                        last.then_inc(*M.tick())
                    have = M.at()
                    g["y_used"] = M.at()

                    @block.vector
                    def _(dve):
                        dve.wait_ge(*have)
                        if not final:
                            dve.tensor_tensor(g["X"], g["X"], bz.ap, ALU.add).then_inc(*V.tick())
                        dve.tensor_tensor(g["XT"], g["XT"], bzt.ap, ALU.add).then_inc(*V.tick())
                    if not final:
                        bz.free = V.at()
                    bzt.free = V.at()
                    g["have"] = V.at()

        def mla_and_rwkv():
            QR, KVR, RO, NO, HD = 384, 256, 32, 64, 96
            H = 8
            RW = 512
            MI = QR + KVR + RO
            IN = MI + 3 * RW + 256
            par = Params("mix0")
            g_in = par.cols(a["ev_norm"][0], D)
            g_q = par.cols(a["mla_q_norm"][0], QR)
            g_kv = par.cols(a["mla_kv_norm"][0], KVR)
            gh_q = par.rows(a["mla_q_hnorm"][0], HD)
            gh_k = par.rows(a["mla_k_hnorm"][0], HD)
            pos = par.load(par.space(TT, I32), a["positions"][0].rearrange("(t p) -> p t", p=P))
            yield
            enter("mix0")
            proj = room3(TT, IN)
            y = room3(TT, D)
            keep = top[0]
            normed = norm_turned(h, D, None, x_parts, g_in, par.landed())
            project_parts(x_parts, KD, a["ev_w_in"][0], IN, normed, copy_out(proj))
            have = both()
            load_the_rest()
            top[0] = 14200
            memory_once()

            top[0] = keep
            cqT = room(3 * T).rearrange("p (k t) -> p k t", t=T)
            ckvT = room(2 * T).rearrange("p (k t) -> p k t", t=T)
            q = room3(TT, H * HD)
            kv = room3(TT, H * 128)
            k = room3(TT, H * HD)
            ang = room3(TT, 16)
            turns = room3(TT, 16)
            tables = [room3(TT, 16), room3(TT, 16)]
            posf = room(TT)

            @block.vector
            def _(dve):
                dve.wait_ge(*par.landed())
                for due in unseen(dve, have):
                    dve.wait_ge(*due)
                dve.tensor_copy(posf, pos).then_inc(*V.tick())
                dve.wait_ge(*V.at())
                for t in range(TT):
                    dve.tensor_scalar(ang[:, t, :], const("inv_freq"), posf[:, t:t + 1], None, ALU.mult).then_inc(*V.tick())
                dve.wait_ge(*V.at())
                dve.tensor_scalar(turns, ang, 1 / TWO_PI, ROUND, ALU.mult, ALU.add).then_inc(*V.tick())
                dve.wait_ge(*V.at())
                dve.tensor_scalar(turns, turns, ROUND, None, ALU.subtract).then_inc(*V.tick())
                dve.wait_ge(*V.at())
                for c in (PI_C1, PI_C2):
                    dve.scalar_tensor_tensor(out=ang, in0=turns, scalar=-c, in1=ang, op0=ALU.mult,
                                             op1=ALU.add).then_inc(*V.tick())
                    dve.wait_ge(*V.at())
                dve.tensor_scalar(tables[0], ang, np.pi / 2, None, ALU.add).then_inc(*V.tick())
                dve.wait_ge(*V.at())
                dve.tensor_scalar(turns, tables[0], np.pi, -TWO_PI, ALU.is_gt, ALU.mult).then_inc(*V.tick())
                dve.wait_ge(*V.at())
                dve.tensor_tensor(tables[0], tables[0], turns, ALU.add).then_inc(*V.tick())
                dve.wait_ge(*V.at())
                for x, o in ((tables[0], tables[0]), (ang, tables[1])):
                    dve.tensor_scalar(o, x, 3.1415925, -3.1415925, ALU.min, ALU.max).then_inc(*V.tick())
            reduced = V.at()

            @block.scalar
            def _(act):
                act.wait_ge(*reduced)
                for x in tables:
                    act.activation(x, x, ACT.Sin).then_inc(*S.tick())
            rope_ready = S.at()

            before_norms = top[0]
            loaded, mu, mu_slot = rwkv_load(have)
            write_shift = rwkv_shift(proj[:, :, MI:IN], have, loaded[0], mu, mu_slot)
            top[0] = before_norms
            n1 = norm_turned(proj[:, :, 0:QR], QR, have, cqT, g_q, par.landed())
            project(cqT, 3, a["mla_w_uq"][0], H * HD, n1, copy_out(q))
            q_have = both()
            scratch = room(TT * H * HD).rearrange("p (n m) -> p n m", m=HD)
            flat = lambda x: x.rearrange("p t (h n) -> p (t h) n", n=HD)
            n2 = norm_turned(proj[:, :, QR:QR + KVR], KVR, have, ckvT, g_kv, par.landed())
            done_q = head_norm(flat(q), TT * H, HD, q_have, gh_q, scratch)
            project(ckvT, 2, a["mla_w_ukv"][0], H * 128, n2, copy_out(kv))
            kv_have = both()
            write_shift()
            kvh = [kv[:, t, :].rearrange("p (h n) -> p h n", h=H) for t in range(TT)]
            qh = [q[:, t, :].rearrange("p (h n) -> p h n", h=H) for t in range(TT)]
            kh = [k[:, t, :].rearrange("p (h n) -> p h n", h=H) for t in range(TT)]

            @block.gpsimd
            def _(pool):
                for due in unseen(pool, kv_have):
                    pool.wait_ge(*due)
                for t in range(TT):
                    pool.tensor_copy(kh[t][:, :, 0:NO], kvh[t][:, :, 0:NO]).then_inc(*G.tick())
                    pool.tensor_copy(kh[t][:, :, NO:HD], proj[:, t, QR + KVR:MI].unsqueeze(1).to_broadcast([P, H, RO])
                                     ).then_inc(*G.tick())
            k_have = G.at()
            done_k = head_norm(flat(k), TT * H, HD, k_have, gh_k, scratch)
            hs = [room(H * 16).rearrange("p (h n) -> p h n", h=H) for _ in range(2)]
            for xh in (qh, kh):
                for t in range(TT):
                    cos, sin = (x[:, t, :].unsqueeze(1).to_broadcast([P, H, 16]) for x in tables)
                    rotated = rotate(xh[t][:, :, NO:NO + 16], xh[t][:, :, NO + 16:HD], cos, sin, None,
                                     [done_q, done_k, rope_ready, V.at()], hs)
            top[0] = before_norms
            attention(lambda t, i: qh[t][:, i, :], lambda t, i: kh[t][:, i, :], lambda t, i: kvh[t][:, i, NO:128],
                      H, HD, 64, HD ** -0.5, lambda i: y[:, :, i * 64:(i + 1) * 64], rotated,
                      mask=const("causal"), causal=True)

            rwkv(proj[:, :, MI:IN], y[:, :, RW:2 * RW], keep, loaded)
            y_have = both()
            turned = transpose_split(y, KD, y_have, *x_parts, None, None)
            project_parts(x_parts, KD, a["ev_w_out"][0], D, turned, add_to_h, after=y_have)

        def rwkv_load(have):
            RW = 512
            par = Params("rwkv", local=True, by_sync=True)
            slot = take_slot()
            slot.lent = True

            @block.sync
            def _(sp):
                for due in unseen(sp, have, slot.free):
                    sp.wait_ge(*due)
            mu = par.load(slot.ap[:, 0:3 * RW + 256], a["rw_mu"][0].partition_broadcast(P))
            top[0] = ARENA - 3 * RW - 7 * RW
            w2a2 = [par.load(room(RW)[0:64, :], a[n][0]) for n in ("rw_w2", "rw_a2")]
            g2 = par.load(room(RW), a["rw_g2"][0])
            names = ("rw_w0", "rw_a0", "rw_k_k", "rw_k_a", "rw_ln_g", "rw_ln_b")
            dead_rows = arena[:, top[0]:top[0] + 4 * RW]
            rows = {n: par.rows(a[n][0], RW) for n in names}
            r_k = par.rows(a["rw_r_k"][0].rearrange("h n -> (h n)"), RW)
            return (par, rows, r_k, w2a2, g2, dead_rows), mu, slot

        def rwkv_shift(p, have, par, mu, mu_slot):
            slot = take_slot()
            slot.lent = True
            wide = p.shape[2]
            prev = slot.ap[:, 0:TT * wide].rearrange("p (t n) -> p t n", t=TT)
            shift_sem = new_semaphore("rwkv_shift_landed")

            @block.vector
            def _(dve):
                for due in unseen(dve, slot.free):
                    dve.wait_ge(*due)
                dve.memset(prev[0:1, 0, :], 0.0).then_inc(*V.tick())
            zeroed = V.at()

            @block.scalar
            def _(act):
                for due in unseen(act, have, slot.free):
                    act.wait_ge(*due)
                act.dma_start(prev[1:P, 0, :], p[0:P - 1, 0, :]).then_inc(shift_sem, 16)
                act.dma_start(prev[1:P, 1, :], p[0:P - 1, 1, :]).then_inc(shift_sem, 16)
                act.dma_start(prev[0:1, 1, :], p[P - 1:P, 0, :]).then_inc(shift_sem, 16)

            def write():
                @block.vector
                def _(dve):
                    for due in unseen(dve, (shift_sem, 48)):
                        dve.wait_ge(*due)
                    dve.wait_ge(*par.landed())
                    dve.wait_ge(*zeroed)
                    dve.tensor_tensor(prev, prev, p, ALU.subtract).then_inc(*V.tick())
                    dve.wait_ge(*V.at())
                    dve.tensor_tensor(prev, prev, mu.unsqueeze(1).to_broadcast([P, TT, wide]), ALU.mult).then_inc(*V.tick())
                    dve.wait_ge(*V.at())
                    dve.tensor_tensor(p, p, prev, ALU.add).then_inc(*V.tick())
                slot.free = mu_slot.free = V.at()
                slot.lent = mu_slot.lent = False
            return write

        def rwkv(p, y, keep, loaded):
            RW, H, N = 512, 8, 64
            enter("rwkv", keep)
            par, rows, r_k, w2a2, g2, dead_rows = loaded
            shifted = None
            decay, lr, gate, kk = (room3(TT, RW) for _ in range(4))
            base = top[0]
            r, k, v = (p[:, :, i * RW:(i + 1) * RW] for i in range(3))
            lora = p[:, :, 3 * RW:]

            @block.scalar
            def _(act):
                for due in unseen(act, shifted):
                    act.wait_ge(*due)
                act.activation(lora[:, :, 0:64], lora[:, :, 0:64], ACT.Tanh).then_inc(*S.tick())
                act.activation(lora[:, :, 128:256], lora[:, :, 128:256], ACT.Sigmoid).then_inc(*S.tick())
            squashed = S.at()
            lT = room(3 * T).rearrange("p (k t) -> p k t", t=T)
            widths = (64, 64, 128)
            for j, w in enumerate(widths):
                bank = take_bank()

                @block.tensor
                def _(pe):
                    for due in unseen(pe, bank.free):
                        pe.wait_ge(*due)
                    pe.wait_ge(*squashed)
                    for t in range(TT):
                        last = pe.transpose(bank.ap[0:w, t * P:(t + 1) * P], lora[:, t, j * 64:j * 64 + w], ident)
                    last.then_inc(*M.tick())
                turned = M.at()

                @block.vector
                def _(dve):
                    for due in unseen(dve, shifted):
                        dve.wait_ge(*due)
                    dve.wait_ge(*turned)
                    dve.tensor_copy(lT[0:w, j, :], bank.ap[0:w, 0:T]).then_inc(*V.tick())
                bank.free = V.at()
            turned = V.at()
            for j, (w, dst, bias) in enumerate(((64, decay, rows["rw_w0"]), (64, lr, rows["rw_a0"]), (128, gate, None))):
                wt = w2a2[j] if j < 2 else g2
                for t in range(TT):
                    bank = take_bank()

                    @block.tensor
                    def _(pe):
                        for due in unseen(pe, bank.free):
                            pe.wait_ge(*due)
                        pe.wait_ge(*turned)
                        pe.wait_ge(*par.landed())
                        pe.matmul(bank.ap, lT[0:w, j, t * P:(t + 1) * P], wt[0:w, :], start=True, stop=True).then_inc(*M.tick())
                    have = M.at()

                    @block.vector
                    def _(dve):
                        dve.wait_ge(*have)
                        if bias is not None:
                            dve.tensor_tensor(dst[:, t, :], bank.ap, bias, ALU.add).then_inc(*V.tick())
                        else:
                            dve.tensor_copy(dst[:, t, :], bank.ap).then_inc(*V.tick())
                    bank.free = V.at()
            have = V.at()

            @block.scalar
            def _(act):
                act.wait_ge(*have)
                act.activation(decay, decay, ACT.Sigmoid).then_inc(*S.tick())
                act.activation(lr, lr, ACT.Sigmoid).then_inc(*S.tick())
            sig = S.at()
            scratch = room3(TT, RW)
            by_head = lambda x: x.rearrange("p t (h n) -> p (t h) n", n=N)
            both_tiles = lambda x: x.unsqueeze(1).to_broadcast([P, TT, RW])
            norm = room(TT * H)

            @block.vector
            def _(dve):
                dve.wait_ge(*sig)
                dve.tensor_scalar(decay, decay, -float(np.exp(-0.5)), None, ALU.mult).then_inc(*V.tick())
                dve.tensor_tensor(kk, k, both_tiles(rows["rw_k_k"]), ALU.mult).then_inc(*V.tick())
                dve.wait_ge(*V.at())
                dve.tensor_tensor(scratch, kk, kk, ALU.mult).then_inc(*V.tick())
                dve.wait_ge(*V.at())
                dve.tensor_reduce(norm, by_head(scratch), AX, ALU.add).then_inc(*V.tick())
                dve.wait_ge(*V.at())
                dve.tensor_scalar(norm, norm, 1e-24, None, ALU.max).then_inc(*V.tick())
                dve.tensor_scalar(scratch, lr, 1.0, None, ALU.subtract).then_inc(*V.tick())
                dve.wait_ge(*V.at())
                dve.tensor_tensor(scratch, scratch, both_tiles(rows["rw_k_a"]), ALU.mult).then_inc(*V.tick())
                dve.wait_ge(*V.at())
                dve.scalar_tensor_tensor(out=k, in0=scratch, scalar=1.0, in1=k, op0=ALU.add, op1=ALU.mult).then_inc(*V.tick())
            log_decay = V.at()
            root = reciprocal_root(norm, TT * H, V.at())

            @block.vector
            def _(dve):
                dve.wait_ge(*root)
                dve.tensor_tensor(by_head(kk), by_head(kk), norm.unsqueeze(2).to_broadcast([P, TT * H, N]),
                                  ALU.mult).then_inc(*V.tick())
            have_kk = V.at()

            up, down = room3(TT, RW), room3(TT, RW)
            for t in range(TT):
                bank = take_bank()

                @block.tensor
                def _(pe):
                    for due in unseen(pe, bank.free, log_decay):
                        pe.wait_ge(*due)
                    pe.matmul(bank.ap, const("upto_mid"), decay[:, t, :], start=True, stop=True).then_inc(*M.tick())
                have = M.at()

                @block.scalar
                def _(act):
                    act.wait_ge(*have)
                    act.activation(up[:, t, :], bank.ap, ACT.Exp).then_inc(*S.tick())
                    act.activation(down[:, t, :], bank.ap, ACT.Exp, scale=-1.0).then_inc(*S.tick())

                @block.vector
                def _(dve):
                    for due in unseen(dve, S.at()):
                        dve.wait_ge(*due)
                    dve.wait_ge(*have)
                    dve.tensor_tensor(scratch[:, t, :], bank.ap, decay[:, t, :], ALU.subtract).then_inc(*V.tick())
                bank.free = [V.at(), S.at()]
            excl = V.at()

            @block.scalar
            def _(act):
                act.wait_ge(*excl)
                act.activation(scratch, scratch, ACT.Exp).then_inc(*S.tick())
            powers = S.at()
            bank = take_bank()
            carry = room(H)

            @block.tensor
            def _(pe):
                for due in unseen(pe, bank.free, log_decay):
                    pe.wait_ge(*due)
                for i in range(H):
                    c = slice(i * N, (i + 1) * N)
                    pe.matmul(bank.ap[0:N, i:i + 1], decay[:, 0, c], const("halves")[:, 1:2], start=True, stop=False)
                    last = pe.matmul(bank.ap[0:N, i:i + 1], decay[:, 1, c], const("halves")[:, 0:1], start=False, stop=True)
                last.then_inc(*M.tick())
            have = M.at()

            @block.scalar
            def _(act):
                act.wait_ge(*have)
                act.activation(carry[0:N, :], bank.ap[0:N, 0:H], ACT.Exp).then_inc(*S.tick())
            bank.free = S.at()
            carried = S.at()
            bonus = room(TT * H)
            rk = room3(TT, RW)

            @block.vector
            def _(dve):
                for due in unseen(dve, log_decay):
                    dve.wait_ge(*due)
                dve.tensor_tensor(rk, r, k, ALU.mult).then_inc(*V.tick())
                dve.wait_ge(*V.at())
                dve.tensor_tensor(rk, rk, both_tiles(r_k), ALU.mult).then_inc(*V.tick())
                dve.wait_ge(*V.at())
                dve.tensor_reduce(bonus, by_head(rk), AX, ALU.add).then_inc(*V.tick())
                for due in unseen(dve, powers, have_kk, V.at()):
                    dve.wait_ge(*due)
                dve.tensor_tensor(lr, lr, kk, ALU.mult).then_inc(*V.tick())
                dve.wait_ge(*V.at())
                dve.tensor_tensor(lr, lr, down, ALU.mult).then_inc(*V.tick())
                dve.scalar_tensor_tensor(out=kk, in0=kk, scalar=-1.0, in1=scratch, op0=ALU.mult,
                                         op1=ALU.mult).then_inc(*V.tick())
                dve.tensor_tensor(k, k, down, ALU.mult).then_inc(*V.tick())
                dve.tensor_tensor(r, r, up, ALU.mult).then_inc(*V.tick())
            scaled = V.at()
            top[0] = base
            keep_small = room(TT * H)
            small2 = room(H)

            @block.vector
            def _(dve):
                for due in unseen(dve, scaled, carried):
                    dve.wait_ge(*due)
                dve.tensor_copy(small2[0:N, :], carry[0:N, :]).then_inc(*V.tick())
                dve.tensor_copy(keep_small, bonus).then_inc(*V.tick())
            bonus, carry = keep_small, small2
            scaled = V.at()
            stats = room(TT * H)
            state = room(H * N)
            state_ready = None
            names = ("X", "XT", "Y", "NL")
            homes = (xT_sb, dead_rows)
            work = [{n: homes[g][:, j * 512:(j + 1) * 512] for j, n in enumerate(names)} | {"turned": room(4 * 512), "TTm": room(4 * 512), "rhs": room(256),
                                                      "sa": room(256)} for g in range(2)]
            idle = [None, None]
            for t in range(TT):
                groups = []
                for g in range(2):
                    w = work[g]
                    heads = range(4 * g, 4 * g + 4)
                    tv = w["turned"].rearrange("p (h n) -> p h n", h=4)
                    mv = w["TTm"].rearrange("p (h n) -> p h n", h=4)
                    for j, i in enumerate(heads):
                        c = slice(i * N, (i + 1) * N)
                        bank = take_bank()

                        @block.tensor
                        def _(pe):
                            for due in unseen(pe, bank.free, scaled):
                                pe.wait_ge(*due)
                            for m, x in enumerate((lr, k, kk, r)):
                                last = pe.transpose(bank.ap[0:N, m * P:(m + 1) * P], x[:, t, c], ident)
                            last.then_inc(*M.tick())
                        turned = M.at()

                        @block.scalar
                        def _(act):
                            for due in unseen(act, turned, idle[g], scaled):
                                act.wait_ge(*due)
                            act.copy(tv[0:N, j, :], bank.ap[0:N, :]).then_inc(*S.tick())
                        bank.free = S.at()
                        copied = S.at()
                        bank = take_bank()

                        @block.tensor
                        def _(pe):
                            for due in unseen(pe, bank.free):
                                pe.wait_ge(*due)
                            pe.wait_ge(*copied)
                            pe.matmul(bank.ap[:, 0:256], tv[0:N, j, 0:P], tv[0:N, j, 256:512], start=True, stop=True)
                            pe.matmul(bank.ap[:, 256:512], tv[0:N, j, P:256], tv[0:N, j, 256:512], start=True,
                                      stop=True).then_inc(*M.tick())
                        have = M.at()

                        @block.vector
                        def _(dve):
                            for due in unseen(dve, have, idle[g]):
                                dve.wait_ge(*due)
                            dve.tensor_tensor(mv[:, j, :], bank.ap, const("quad"), ALU.mult).then_inc(*V.tick())
                        bank.free = V.at()
                    groups.append(dict(w, NT=mv[:, :, 0:P], masked=V.at(), copied=copied, tv=tv, mv=mv))
                for w in groups:
                    w["N"] = bank = take_bank()
                    tv = w["tv"]

                    @block.tensor
                    def _(pe):
                        for due in unseen(pe, bank.free, w["copied"]):
                            pe.wait_ge(*due)
                        for j in range(4):
                            last = pe.matmul(bank.ap[:, j * P:(j + 1) * P], tv[0:N, j, 256:384], tv[0:N, j, 0:P],
                                             start=True, stop=True)
                        last.then_inc(*M.tick())
                    w["ready"] = [w["masked"], M.at()]
                invert(groups)
                for g, w in enumerate(groups):
                    tv, mv = w["tv"], w["mv"]
                    hv = slice(4 * g * N, 4 * (g + 1) * N)
                    bank = take_bank()

                    @block.tensor
                    def _(pe):
                        for due in unseen(pe, bank.free, w["have"], state_ready):
                            pe.wait_ge(*due)
                        for j in range(4):
                            c = slice((4 * g + j) * N, (4 * g + j + 1) * N)
                            last = pe.matmul(bank.ap[:, j * N:(j + 1) * N], mv[:, j, 256:384], v[:, t, c],
                                             start=True, stop=(t == 0))
                            if t:
                                last = pe.matmul(bank.ap[:, j * N:(j + 1) * N], tv[0:N, j, 256:384], state[0:N, c],
                                                 start=False, stop=True)
                        last.then_inc(*M.tick())
                    have = M.at()

                    @block.scalar
                    def _(act):
                        act.wait_ge(*have)
                        act.copy(w["rhs"], bank.ap[:, 0:256]).then_inc(*S.tick())
                    bank.free = S.at()
                    have = S.at()
                    bank = take_bank()

                    @block.tensor
                    def _(pe):
                        for due in unseen(pe, bank.free):
                            pe.wait_ge(*due)
                        pe.wait_ge(*have)
                        for j in range(4):
                            last = pe.matmul(bank.ap[:, j * N:(j + 1) * N], w["XT"][:, j * P:(j + 1) * P],
                                             w["rhs"][:, j * N:(j + 1) * N], start=True, stop=True)
                        last.then_inc(*M.tick())
                    have = M.at()

                    @block.scalar
                    def _(act):
                        act.wait_ge(*have)
                        act.copy(w["sa"], bank.ap[:, 0:256]).then_inc(*S.tick())
                    bank.free = S.at()
                    have = S.at()
                    bank = take_bank()
                    bank2 = take_bank()

                    @block.tensor
                    def _(pe):
                        for due in unseen(pe, bank.free, bank2.free):
                            pe.wait_ge(*due)
                        pe.wait_ge(*have)
                        for j in range(4):
                            c = slice((4 * g + j) * N, (4 * g + j + 1) * N)
                            sa = w["sa"][:, j * N:(j + 1) * N]
                            o = bank.ap[:, j * N:(j + 1) * N]
                            pe.matmul(o, mv[:, j, P:256], sa, start=True, stop=False)
                            last = pe.matmul(o, mv[:, j, 384:512], v[:, t, c], start=False, stop=(t == 0))
                            if t:
                                last = pe.matmul(o, tv[0:N, j, 384:512], state[0:N, c], start=False, stop=True)
                            else:
                                o = bank2.ap[0:N, j * N:(j + 1) * N]
                                pe.matmul(o, lr[:, t, c], sa, start=True, stop=False)
                                last = pe.matmul(o, k[:, t, c], v[:, t, c], start=False, stop=True)
                        last.then_inc(*M.tick())
                    have = M.at()
                    idle[g] = M.at()

                    @block.scalar
                    def _(act):
                        act.wait_ge(*have)
                        act.copy(y[:, t, hv], bank.ap[:, 0:256]).then_inc(*S.tick())
                    bank.free = S.at()
                    if t == 0:
                        @block.vector
                        def _(dve):
                            dve.wait_ge(*have)
                            dve.tensor_tensor(state[0:N, hv].rearrange("p (h n) -> p h n", h=4),
                                              bank2.ap[0:N, 0:256].rearrange("p (h n) -> p h n", h=4),
                                              carry[0:N, 4 * g:4 * g + 4].unsqueeze(2).to_broadcast([N, 4, N]),
                                              ALU.mult).then_inc(*V.tick())
                        bank2.free = V.at()
                if t == 0:
                    state_ready = V.at()
            out_ready = S.at()
            yh = [y[:, t, :].rearrange("p (h n) -> p h n", n=N) for t in range(TT)]
            vh = [v[:, t, :].rearrange("p (h n) -> p h n", n=N) for t in range(TT)]
            sv = stats.rearrange("p (t h) -> p t h", t=TT)
            bv = bonus.rearrange("p (t h) -> p t h", t=TT)
            spare = kk
            sh = [spare[:, t, :].rearrange("p (h n) -> p h n", n=N) for t in range(TT)]
            wide = lambda x: x.unsqueeze(2).to_broadcast([P, H, N])

            @block.vector
            def _(dve):
                for due in unseen(dve, out_ready, idle[0], idle[1]):
                    dve.wait_ge(*due)
                for t in range(TT):
                    dve.tensor_reduce(sv[:, t, :], yh[t], AX, ALU.add).then_inc(*V.tick())
                dve.wait_ge(*V.at())
                dve.tensor_scalar(stats, stats, 1.0 / N, None, ALU.mult).then_inc(*V.tick())
                dve.wait_ge(*V.at())
                for t in range(TT):
                    dve.tensor_tensor(yh[t], yh[t], wide(sv[:, t, :]), ALU.subtract).then_inc(*V.tick())
                dve.wait_ge(*V.at())
                dve.tensor_tensor(spare, y, y, ALU.mult).then_inc(*V.tick())
                dve.wait_ge(*V.at())
                for t in range(TT):
                    dve.tensor_reduce(sv[:, t, :], sh[t], AX, ALU.add).then_inc(*V.tick())
                dve.wait_ge(*V.at())
                dve.tensor_scalar(stats, stats, 1.0 / N, 64e-5, ALU.mult, ALU.add).then_inc(*V.tick())
            root = reciprocal_root(stats, TT * H, V.at())

            @block.vector
            def _(dve):
                dve.wait_ge(*root)
                for t in range(TT):
                    dve.tensor_tensor(yh[t], yh[t], wide(sv[:, t, :]), ALU.mult).then_inc(*V.tick())
                    dve.tensor_tensor(sh[t], vh[t], wide(bv[:, t, :]), ALU.mult).then_inc(*V.tick())
                dve.wait_ge(*V.at())
                dve.tensor_tensor(y, y, both_tiles(rows["rw_ln_g"]), ALU.mult).then_inc(*V.tick())
                dve.tensor_tensor(spare, spare, both_tiles(rows["rw_ln_b"]), ALU.add).then_inc(*V.tick())
                dve.wait_ge(*V.at())
                dve.tensor_tensor(y, y, spare, ALU.add).then_inc(*V.tick())
                dve.wait_ge(*V.at())
                dve.tensor_tensor(y, y, gate, ALU.mult).then_inc(*V.tick())

        after_take = []

        def project_turned(w, first_col, n_tiles, ready, take):
            behind = []
            for c0 in range(0, n_tiles, 4):
                slot, view, _, landed = load_weights(w[:, first_col + c0 * P:first_col + (c0 + 4) * P], (P, KD, 4 * P))
                for j in range(4):
                    bank = take_bank()

                    @block.tensor
                    def _(pe):
                        for due in unseen(pe, bank.free, ready, landed):
                            pe.wait_ge(*due)
                        for k in range(KD):
                            last = pe.matmul(bank.ap[:, 0:T], view[:, k, j * P:(j + 1) * P], xT[:, k, :],
                                             start=(k == 0), stop=(k == KD - 1))
                        last.then_inc(*M.tick())
                    slot.free = M.at()
                    bank.free = take(c0 + j, bank.ap[:, 0:T], M.at())
                    behind.append(after_take.pop() if after_take else None)
                    if len(behind) > 2 and behind[-3]:
                        behind[-3]()
            for later in behind[-2:]:
                if later:
                    later()

        def project_turned_parts(w, first_col, n_tiles, ready, take):
            behind, split, parts_ready, loaded = [], {}, {}, {}

            def split_one(i):
                c0, j = i // 4 * 4, i % 4
                if j == 0:
                    loaded[c0] = load_weights(w[:, first_col + c0 * P:first_col + (c0 + 4) * P], (P, KD, 4 * P))
                _, view, low, landed = loaded[c0]
                cols = slice(j * P, (j + 1) * P)
                split[i] = split_piece(view[:, :, cols], low[:, :, cols], (P, KD, P), landed)
            for i in range(1 - PIECES, 0):
                run_ahead(i, n_tiles, split_one, split, parts_ready)
            for i in range(n_tiles):
                run_ahead(i, n_tiles, split_one, split, parts_ready)
                slot, _, low, _ = loaded[i // 4 * 4]
                high, at, _ = split[i]
                j = i % 4
                bank = take_bank()

                @block.tensor
                def _(pe):
                    for due in unseen(pe, bank.free, ready, parts_ready[i]):
                        pe.wait_ge(*due)
                    for k in range(KD):
                        last = passes(pe, bank.ap[:, 0:T], (high[:, k, :], low[:, k, j * P:(j + 1) * P]),
                                      (x_high[:, k, :], x_low[:, k, :]), start=(k == 0), stop=(k == KD - 1))
                    last.then_inc(*M.tick())
                piece_free[at] = slot.free = M.at()
                bank.free = take(i, bank.ap[:, 0:T], M.at())
                behind.append(after_take.pop() if after_take else None)
                if len(behind) > 2 and behind[-3]:
                    behind[-3]()
            for later in behind[-2:]:
                if later:
                    later()

        def conv_project(w, first_col, n_tiles, taps, bias, params_ready, ready, func, finish, turned_by=project_turned):
            raw = [room(T) for _ in range(4)]
            done = [room(T) for _ in range(4)]
            raw_free, done_free = [None] * 4, [None] * 4

            def take(i, ps, mark):
                b = i % 4

                @block.vector
                def _(dve):
                    for due in unseen(dve, mark, params_ready, raw_free[b]):
                        dve.wait_ge(*due)
                    if bias is not None:
                        dve.tensor_scalar(raw[b], ps, taps[:, i, 3:4], bias[:, i:i + 1], ALU.mult,
                                          ALU.add).then_inc(*V.tick())
                    else:
                        dve.tensor_scalar(raw[b], ps, taps[:, i, 3:4], None, ALU.mult).then_inc(*V.tick())
                    for back in (1, 2, 3):
                        dve.wait_ge(*V.at())
                        dve.scalar_tensor_tensor(out=raw[b][:, back:T], in0=ps[:, 0:T - back],
                                                 scalar=taps[:, i, 3 - back:4 - back], in1=raw[b][:, back:T],
                                                 op0=ALU.mult, op1=ALU.add).then_inc(*V.tick())
                have = V.at()

                def squash(dst, after):
                    @block.scalar
                    def _(act):
                        for due in unseen(act, after):
                            act.wait_ge(*due)
                        act.wait_ge(*have)
                        act.activation(dst, raw[b], func).then_inc(*S.tick())
                    raw_free[b] = S.at()
                    return S.at()

                def keep_mark(mark):
                    done_free[b] = mark
                finish(i, squash, done[b], done_free[b], keep_mark)
                return have
            turned_by(w, first_col, n_tiles, ready, take)

        def softplus(x, scratch, ready):
            e, w, lw = scratch

            @block.vector
            def _(dve):
                for due in unseen(dve, ready):
                    dve.wait_ge(*due)
                dve.scalar_tensor_tensor(out=e, in0=x, scalar=-1.0, in1=x, op0=ALU.mult, op1=ALU.max).then_inc(*V.tick())
                dve.wait_ge(*V.at())
                dve.tensor_scalar(x, x, 0.0, None, ALU.max).then_inc(*V.tick())
            have = V.at()

            @block.scalar
            def _(act):
                act.wait_ge(*have)
                act.activation(e, e, ACT.Exp, scale=-1.0).then_inc(*S.tick())
            have = S.at()

            @block.vector
            def _(dve):
                dve.wait_ge(*have)
                dve.tensor_scalar(w, e, 1.0, None, ALU.add).then_inc(*V.tick())
            have = V.at()

            @block.scalar
            def _(act):
                act.wait_ge(*have)
                act.activation(lw, w, ACT.Ln).then_inc(*S.tick())
            have = S.at()

            @block.vector
            def _(dve):
                dve.wait_ge(*have)
                dve.tensor_scalar(w, w, 1.0, None, ALU.subtract).then_inc(*V.tick())
                dve.wait_ge(*V.at())
                dve.scalar_tensor_tensor(out=lw, in0=w, scalar=0.0, in1=lw, op0=ALU.is_equal, op1=ALU.add).then_inc(*V.tick())
                dve.wait_ge(*V.at())
                dve.scalar_tensor_tensor(out=w, in0=w, scalar=0.0, in1=w, op0=ALU.is_equal, op1=ALU.add).then_inc(*V.tick())
                dve.wait_ge(*V.at())
                dve.reciprocal(w, w).then_inc(*V.tick())
                dve.wait_ge(*V.at())
                dve.tensor_tensor(lw, lw, w, ALU.mult).then_inc(*V.tick())
                dve.wait_ge(*V.at())
                dve.tensor_tensor(lw, lw, e, ALU.mult).then_inc(*V.tick())
                dve.wait_ge(*V.at())
                dve.tensor_tensor(x, x, lw, ALU.add).then_inc(*V.tick())
            return V.at()

        def mamba():
            INNER, NH, HDM, GR, NS = 2048, 32, 64, 4, 128
            CONV = INNER + 2 * GR * NS
            par = Params("mamba")
            g_in = par.cols(a["od_norm"][0], D)
            taps = par.space(24 * 4).rearrange("p (i j) -> p i j", j=4)
            for j in range(4):
                par.load(taps[:, :, j], a["ssm_conv_w"][0][j].rearrange("(i p) -> p i", p=P))
            bias = par.cols(a["ssm_conv_b"][0], CONV)
            dtb = par.rows(a["ssm_dt_bias"][0], NH)
            alog = par.rows(a["ssm_a_log"][0], NH)
            dsk = par.rows(a["ssm_d"][0], NH)
            g_out = par.cols(a["ssm_gnorm"][0], INNER)
            yield
            enter("mamba")
            dt = room3(TT, NH)
            top[0] = keep = -(-top[0] // 8) * 8
            normed = norm_turned(h, D, None, x_parts, g_in, par.landed())
            top[0] = keep
            have_x = normed
            x = room3(TT, INNER)
            x_at = top[0] - TT * INNER
            BT = room(GR * T).rearrange("p (g t) -> p g t", t=T)
            CT = room(GR * T).rearrange("p (g t) -> p g t", t=T)
            z = room3(TT, INNER)

            def finish(i, squash, done, free, keep_mark):
                if i >= 16:
                    dst = (BT if i < 20 else CT)[:, (i - 16) % 4, :]
                    squash(dst, normed)
                    return
                ready = squash(done, [free, normed])

                def turn():
                    bank = take_bank()

                    @block.tensor
                    def _(pe):
                        for due in unseen(pe, bank.free, ready):
                            pe.wait_ge(*due)
                        for t in range(TT):
                            last = pe.transpose(bank.ap[:, t * P:(t + 1) * P], done[:, t * P:(t + 1) * P], ident)
                        last.then_inc(*M.tick())
                    turned = M.at()

                    @block.scalar
                    def _(act):
                        act.wait_ge(*turned)
                        act.copy(x[:, :, i * P:(i + 1) * P], bank.ap[:, 0:T].rearrange("p (t n) -> p t n", t=TT)).then_inc(*S.tick())
                    bank.free = S.at()
                    keep_mark(turned)
                after_take.append(turn)

            dt_have = project_few(a["od_w_in"][0], INNER + CONV, NH, normed, dt)
            conv_project(a["od_w_in"][0], INNER, 24, taps, bias, par.landed(), normed, ACT.Silu, finish,
                         project_turned_parts)
            soft = [room3(TT, NH) for _ in range(3)]
            dA = room3(TT, NH)
            wide = lambda r: r.unsqueeze(1).to_broadcast([P, TT, NH])

            made = {}

            def step_sizes():
                @block.vector
                def _(dve):
                    for due in unseen(dve, dt_have):
                        dve.wait_ge(*due)
                    dve.tensor_tensor(dt, dt, wide(dtb), ALU.add).then_inc(*V.tick())

                @block.scalar
                def _(act):
                    act.activation(alog, alog, ACT.Exp).then_inc(*S.tick())
                rate = S.at()
                have = softplus(dt, soft, V.at())

                @block.vector
                def _(dve):
                    for due in unseen(dve, rate):
                        dve.wait_ge(*due)
                    dve.wait_ge(*have)
                    dve.scalar_tensor_tensor(out=dA, in0=dt, scalar=-1.0, in1=wide(alog), op0=ALU.mult,
                                             op1=ALU.mult).then_inc(*V.tick())
                have = V.at()
                made["dA"] = have

            def sums():
                made["cumT"], made["cum"] = cumulate(dA, NH, made["dA"])
            project_parts(x_parts, KD, a["od_w_in"][0], INNER, None, copy_out(z), during={1: step_sizes, 10: sums})
            have, cumT, cum = made["dA"], made["cumT"], made["cum"]
            z_have = both()
            y = z
            top[0] = -(-top[0] // 8) * 8
            xdt_at = top[0]
            xdt = room3(TT, INNER)
            xh = lambda ap, t: ap[:, t, :].rearrange("p (h n) -> p h n", n=HDM)

            @block.gpsimd
            def _(pool):
                pool.wait_ge(*have)
                for t in range(TT):
                    pool.tensor_tensor(xh(xdt, t), xh(x, t), dt[:, t, :].unsqueeze(2).to_broadcast([P, NH, HDM]),
                                       ALU.mult).then_inc(*G.tick())
            scaled = G.at()

            @block.vector
            def _(dve):
                for due in unseen(dve, scaled):
                    dve.wait_ge(*due)
                for t in range(TT):
                    dve.tensor_tensor(xh(x, t), xh(x, t), dsk.unsqueeze(2).to_broadcast([P, NH, HDM]),
                                      ALU.mult).then_inc(*V.tick())
            skip_ready = V.at()

            @block.scalar
            def _(act):
                for due in unseen(act, z_have):
                    act.wait_ge(*due)
                act.activation(z, z, ACT.Silu).then_inc(*S.tick())
            gate_ready = S.at()
            cb = [room(384) for _ in range(GR)]
            for g in range(GR):
                bank = take_bank()

                @block.tensor
                def _(pe):
                    for due in unseen(pe, bank.free):
                        pe.wait_ge(*due)
                    pe.matmul(bank.ap[:, 0:T], BT[:, g, 0:P], CT[:, g, :], start=True, stop=True)
                    pe.matmul(bank.ap[:, T:T + P], BT[:, g, P:T], CT[:, g, P:T], start=True, stop=True).then_inc(*M.tick())
                have = M.at()

                @block.scalar
                def _(act):
                    act.wait_ge(*have)
                    act.copy(cb[g], bank.ap[:, 0:384]).then_inc(*S.tick())
                bank.free = S.at()
            cb_ready = S.at()
            AHEAD = 4
            seg = [room(384) for _ in range(AHEAD + 2)]
            seg_free = [None] * len(seg)
            ready = {}

            def decays(i):
                b = i % len(seg)
                bank = take_bank_of(6, 0)

                @block.tensor
                def _(pe):
                    for due in unseen(pe, bank.free, cumT["ready"]):
                        pe.wait_ge(*due)
                    pe.matmul(bank.ap[:, 0:T], ident[0:NH, i:i + 1].to_broadcast([NH, P]), cumT["ap"][0:NH, :],
                              start=True, stop=True).then_inc(*M.tick())
                have = M.at()

                @block.vector
                def _(dve):
                    for due in unseen(dve, seg_free[b], cum["ready"]):
                        dve.wait_ge(*due)
                    dve.wait_ge(*have)
                    dve.scalar_tensor_tensor(out=seg[b][:, 0:P], in0=bank.ap[:, 0:P], scalar=cum["ap"][:, 0, i:i + 1],
                                             in1=const("after_neg"), op0=ALU.subtract, op1=ALU.add).then_inc(*V.tick())
                    dve.tensor_scalar(seg[b][:, P:T], bank.ap[:, P:T], cum["ap"][:, 0, i:i + 1], None,
                                      ALU.subtract).then_inc(*V.tick())
                    dve.scalar_tensor_tensor(out=seg[b][:, T:T + P], in0=bank.ap[:, P:T],
                                             scalar=cum["ap"][:, 1, i:i + 1], in1=const("after_neg"),
                                             op0=ALU.subtract, op1=ALU.add).then_inc(*V.tick())
                bank.free = V.at()
                have = V.at()

                @block.scalar
                def _(act):
                    act.wait_ge(*have)
                    act.activation(seg[b], seg[b], ACT.Exp).then_inc(*S.tick())
                have = S.at()

                @block.gpsimd
                def _(pool):
                    for due in unseen(pool, cb_ready):
                        pool.wait_ge(*due)
                    pool.wait_ge(*have)
                    pool.tensor_tensor(seg[b], seg[b], cb[i // 8], ALU.mult).then_inc(*G.tick())
                ready[i] = G.at()

            def head_products(i, ybank):
                b = i % len(seg)
                have = ready[i]

                @block.tensor
                def _(pe):
                    for due in unseen(pe, ybank.free, scaled):
                        pe.wait_ge(*due)
                    pe.wait_ge(*have)
                    c = slice(i * HDM, (i + 1) * HDM)
                    j = i % 4
                    pe.matmul(ybank.ap[:, j * HDM:(j + 1) * HDM], seg[b][:, 0:P], xdt[:, 0, c], start=True, stop=True)
                    o = ybank.ap[:, 256 + j * HDM:256 + (j + 1) * HDM]
                    pe.matmul(o, seg[b][:, P:T], xdt[:, 0, c], start=True, stop=False)
                    pe.matmul(o, seg[b][:, T:T + P], xdt[:, 1, c], start=False, stop=True).then_inc(*M.tick())
                seg_free[b] = M.at()
                if i % 4 == 3:
                    have = M.at()
                    c = slice((i - 3) * HDM, (i + 1) * HDM)

                    @block.vector
                    def _(dve):
                        for due in unseen(dve, skip_ready, gate_ready):
                            dve.wait_ge(*due)
                        dve.wait_ge(*have)
                        dve.tensor_tensor(x[:, :, c], x[:, :, c], ybank.ap.rearrange("p (t n) -> p t n", t=TT),
                                          ALU.add).then_inc(*V.tick())
                        dve.wait_ge(*V.at())
                        dve.tensor_tensor(y[:, :, c], y[:, :, c], x[:, :, c], ALU.mult).then_inc(*V.tick())
                    ybank.free = V.at()
            square, r = room(512), room3(TT, GR)
            for i in range(NH + AHEAD):
                if i < NH:
                    decays(i)
                if i >= AHEAD:
                    if i % 4 == 0:
                        ybank = take_bank_of(2, 6)
                    head_products(i - AHEAD, ybank)
                    if (i - AHEAD) % 8 == 7:
                        g, have = (i - AHEAD) // 8, V.at()

                        @block.scalar
                        def _(act):
                            act.wait_ge(*have)
                            for t in range(TT):
                                for due in unseen(act, S.at()):
                                    act.wait_ge(*due)
                                act.activation(square, y[:, t, g * 512:(g + 1) * 512], ACT.Square,
                                               accum_out=r[:, t, g:g + 1]).then_inc(*S.tick())
            summed = S.at()
            y8 = y.rearrange("p t (g n) -> p (t g) n", n=512)
            r = r.rearrange("p t g -> p (t g)")

            @block.vector
            def _(dve):
                dve.wait_ge(*summed)
                dve.tensor_scalar(r, r, 1.0 / 512, EPS, ALU.mult, ALU.add).then_inc(*V.tick())
            root = reciprocal_root(r, TT * GR, V.at())

            @block.vector
            def _(dve):
                dve.wait_ge(*root)
                dve.tensor_tensor(y8, y8, r.unsqueeze(2).to_broadcast([P, TT * GR, 512]), ALU.mult).then_inc(*V.tick())
            have = V.at()
            yT = [in_three(nc.alloc_sbuf_tensor_at(f"mamba_y_{part}", [P, 16 * T], F32R, offset=arena_base + 4 * at))
                  for part, at in (("high", x_at), ("low", xdt_at))]
            turned = transpose_split(y, 16, have, *yT, g_out, None)
            project_parts(yT, 16, a["od_w_out"][0], D, turned, add_to_h, after=have)

        def cumulate(x, n, ready):
            cum = room3(TT, n)
            cumT = room(T)
            bank = take_bank()

            @block.tensor
            def _(pe):
                for due in unseen(pe, bank.free, ready):
                    pe.wait_ge(*due)
                pe.matmul(bank.ap[:, 0:n], const("upto"), x[:, 0, :], start=True, stop=True)
                pe.matmul(bank.ap[:, n:2 * n], const("ones"), x[:, 0, :], start=True, stop=False)
                pe.matmul(bank.ap[:, n:2 * n], const("upto"), x[:, 1, :], start=False, stop=True).then_inc(*M.tick())
            have = M.at()

            @block.vector
            def _(dve):
                dve.wait_ge(*have)
                dve.tensor_copy(cum, bank.ap[:, 0:2 * n].rearrange("p (t n) -> p t n", t=TT)).then_inc(*V.tick())
            bank.free = V.at()
            copied = V.at()
            bank = take_bank()

            @block.tensor
            def _(pe):
                for due in unseen(pe, bank.free):
                    pe.wait_ge(*due)
                pe.wait_ge(*copied)
                for t in range(TT):
                    last = pe.transpose(bank.ap[0:n, t * P:(t + 1) * P], cum[:, t, :], ident)
                last.then_inc(*M.tick())
            have = M.at()

            @block.vector
            def _(dve):
                dve.wait_ge(*have)
                dve.tensor_copy(cumT[0:n, :], bank.ap[0:n, 0:T]).then_inc(*V.tick())
            bank.free = V.at()
            return {"ap": cumT, "ready": V.at()}, {"ap": cum, "ready": copied}

        def cross(layer):
            H, N = 4, 128
            par = Params(f"cross{layer}")
            g_x = par.cols(a["xa_norm_x"][layer], D)
            g_m = par.cols(a["xa_norm_mem"][layer], D)
            gq = par.rows(a["xa_q_hnorm"][layer], N)
            gk = par.rows(a["xa_k_hnorm"][layer], N)
            yield
            enter(f"cross{layer}")
            q = room3(TT, H * N)
            kv = room3(TT, 2 * H * N)
            y = room3(TT, H * N)
            yT = room(4 * T).rearrange("p (k t) -> p k t", t=T)
            mT = room(KD * T).rearrange("p (k t) -> p k t", t=T)

            @block.vector
            def _(dve):
                dve.wait_ge(*par.landed())
                for k in range(KD):
                    dve.tensor_scalar(mT[:, k, :], memT[:, k, :], g_m[:, k:k + 1], None, ALU.mult).then_inc(*V.tick())
            m_have = V.at()
            scaled, scaled_ready = norm_rows(h, D, None)
            project(mT, KD, a["xa_wkv"][layer], 2 * H * N, m_have, copy_out(kv))
            kv_have = both()
            normed = transpose_tiles(scaled, KD, scaled_ready, xT, g_x, par.landed())
            project(xT, KD, a["xa_wq"][layer], H * N, normed, copy_out(q))
            q_have = both()
            scratch = room(TT * H * N).rearrange("p (n m) -> p n m", m=N)
            parts = {}
            for t in range(TT):
                kt = kv[:, t, 0:H * N].rearrange("p (h n) -> p h n", n=N)
                parts[t] = head_norm(kt, H, N, [kv_have, V.at()], gk, scratch[:, 0:H, :])
            q_done = head_norm(q.rearrange("p t (h n) -> p (t h) n", n=N), TT * H, N, [q_have, V.at()], gq, scratch)
            have = attention(lambda t, i: q[:, t, i * N:(i + 1) * N], lambda t, i: kv[:, t, i * N:(i + 1) * N],
                             lambda t, i: kv[:, t, (H + i) * N:(H + i + 1) * N], H, N, N, N ** -0.5,
                             lambda i: y[:, :, i * N:(i + 1) * N], [q_done, parts[1]])
            turned = transpose_tiles(y, 4, have, yT)
            project(yT, 4, a["xa_wo"][layer], D, turned, add_to_h)

        def memory_once():
            mem = room3(TT, D)
            par = Params("mem", local=True)
            par.load(mem, a["mem"][0].rearrange("(t p) d -> p t d", p=P))
            rstd, have = row_rstd(mem, D, par.landed())

            @block.vector
            def _(dve):
                dve.wait_ge(*have)
                for t in range(TT):
                    dve.tensor_scalar(mem[:, t, :], mem[:, t, :], rstd[:, t:t + 1], None, ALU.mult).then_inc(*V.tick())
            return transpose_tiles(mem, KD, V.at(), memT)

        def swiglu(stage, gain, src, n_pairs):
            par = Params(stage)
            g = par.cols(gain, D)
            yield
            enter(stage)
            sg = [room(T) for _ in range(4)]
            hid = [room(T) for _ in range(4)]
            hh, hl = ([split_room(f"{stage}_hidden{j}_{part}", T) for j in range(4)] for part in ("high", "low"))
            xh, xl = (split_room(f"{stage}_x_{part}", KD * T).rearrange("p (k t) -> p k t", t=T)
                      for part in ("high", "low"))
            scaled, scaled_ready = norm_rows(h, D, None)
            normed = transpose_split(scaled, KD, scaled_ready, xh, xl, g, par.landed())
            high = [split_room(f"{stage}_weights{b}_high", UNIT) for b in range(2)]
            steps = 2 * n_pairs
            up_landed = [new_semaphore(f"{stage}_up{b}_landed") for b in range(2)]
            down_landed = [new_semaphore(f"{stage}_down{b}_landed") for b in range(2)]
            up_done, silu_done, product_done, hh_done, hl_done, down_done = (
                new_semaphore(f"{stage}_{n}_done") for n in ("up", "silu", "product", "hidden_high", "hidden_low", "down"))
            up_high, up_low, down_high, down_low = (
                new_semaphore(f"{stage}_{n}_done") for n in ("up_high", "up_low", "down_high", "down_low"))
            units = [ring[:, b * UNIT:(b + 1) * UNIT] for b in range(2)]
            low = [ring_low[:, b * UNIT:(b + 1) * UNIT] for b in range(2)]
            cut = lambda u, lo, hi, n: u[:, lo:hi].rearrange("p (k n) -> p k n", n=n)
            wg, wu, wd = ([cut(u, *part) for u in units] for part in ((0, 2048, 256), (2048, 4096, 256), (4096, 6144, D)))
            gate_w, up_w, down_w = ([(cut(high[b], *part), cut(low[b], *part)) for b in range(2)]
                                    for part in ((0, 2048, 256), (2048, 4096, 256), (4096, 6144, D)))
            up_banks, acc = banks[0:4], banks[4:8]
            ring_before = [s.free for s in slots]
            banks_before = [b.free for b in banks]

            def run(body, eng):
                assert steps % 4 == 2
                body(0, True, 4)
                with eng.Fori(1, steps // 4) as i:
                    body(i, False, 4)
                body(steps // 4, False, 2)

            @block.sync
            def _(sp):
                for due in unseen(sp, ring_before):
                    sp.wait_ge(*due)

                def up_columns(i, b):
                    c = i * (4 * P) + b * (2 * P)
                    if not (isinstance(i, int) and i == 0):
                        sp.wait_ge(up_done, i * 4 + (2 * b - 2))
                    sp.dma_start(wg[b], src("gate", c).rearrange("(k p) n -> p k n", p=P)).then_inc(up_landed[b], 16)
                    sp.dma_start(wu[b], src("up", c).rearrange("(k p) n -> p k n", p=P)).then_inc(up_landed[b], 16)

                def body(i, first, count):
                    for b in range(count // 2):
                        if count == 4:
                            up_columns(i + b, 1 - b)
                        c = i * (4 * P) + b * (2 * P)
                        if not first:
                            sp.wait_ge(down_done, i * 4 + (2 * b - 2))
                        sp.dma_start(wd[b], src("down", c).rearrange("(k p) n -> p k n", p=P)).then_inc(down_landed[b], 16)
                up_columns(0, 0)
                run(body, sp)

            @block.tensor
            def _(pe):
                for due in unseen(pe, normed, banks_before):
                    pe.wait_ge(*due)

                def up(i, first, j):
                    b = j // 2
                    if not first:
                        pe.wait_ge(product_done, i * 4 + (j - 3))
                    ps = up_banks[j].ap
                    for which, w in enumerate((gate_w, up_w)):
                        if j % 2 == 0:
                            pe.wait_ge(up_low, i * 4 + (j + which + 1))
                        for k in range(KD):
                            c = slice((j % 2) * P, (j % 2 + 1) * P)
                            wh, wl = w[b]
                            last = passes(pe, ps[:, which * T:(which + 1) * T], (wh[:, k, c], wl[:, k, c]),
                                          (xh[:, k, :], xl[:, k, :]), start=(k == 0), stop=(k == KD - 1))
                    last.then_inc(up_done, 1)

                def down(i, j, start=False, stop=False):
                    b = j // 2
                    if j % 2 == 0:
                        pe.wait_ge(down_low, i * 2 + (b + 1))
                    pe.wait_ge(hl_done, i * 4 + (j + 1))
                    for t in range(TT):
                        for n in range(2):
                            rows, cols = slice(t * P, (t + 1) * P), slice(n * 512, (n + 1) * 512)
                            last = passes(pe, acc[t * 2 + n].ap, (hh[j][:, rows], hl[j][:, rows]),
                                          tuple(w[:, j % 2, cols] for w in down_w[b]), start=start, stop=stop)
                    last.then_inc(down_done, 1)

                def body(i, first, count):
                    for j in range(count):
                        up(i, first, j)
                        if j >= 2:
                            down(i, j - 2, start=(first and j == 2))
                        elif not first:
                            down(i - 1, j + 2)
                run(body, pe)
                down(steps // 4, 0)
                down(steps // 4, 1, stop=True)

            @block.scalar
            def _(act):
                def up_parts(i, b):
                    act.wait_ge(up_landed[b], i * 32 + 32)
                    if not (isinstance(i, int) and i == 0):
                        act.wait_ge(up_done, i * 4 + (2 * b - 2))
                    for n in range(2):
                        c = slice(n * 2048, (n + 1) * 2048)
                        act.copy(high[b][:, c], units[b][:, c]).then_inc(up_high, 1)

                def body(i, first, count):
                    if first:
                        up_parts(0, 0)
                    for j in range(count):
                        b = j // 2
                        if j == 0 and count == 4:
                            up_parts(i, 1)
                        if j == 2:
                            up_parts(i + 1, 0)
                        act.wait_ge(up_done, i * 4 + (j + 1))
                        act.activation(sg[j], up_banks[j].ap[:, 0:T], ACT.Silu).then_inc(silu_done, 1)
                        act.wait_ge(product_done, i * 4 + (j + 1))
                        act.copy(hh[j], hid[j]).then_inc(hh_done, 1)
                        if j % 2 == 1:
                            act.wait_ge(down_landed[b], i * 16 + 16)
                            act.copy(high[b][:, 4096:6144], units[b][:, 4096:6144]).then_inc(down_high, 1)
                run(body, act)

            @block.vector
            def _(dve):
                def up_parts(i, b):
                    for n in range(2):
                        c = slice(n * 2048, (n + 1) * 2048)
                        dve.wait_ge(up_high, i * 4 + (2 * b + n + 1))
                        dve.tensor_tensor(low[b][:, c], units[b][:, c], high[b][:, c].bitcast(F32),
                                          ALU.subtract).then_inc(up_low, 1)

                def body(i, first, count):
                    if first:
                        up_parts(0, 0)
                    for j in range(count):
                        b = j // 2
                        if j == 0 and count == 4:
                            up_parts(i, 1)
                        if j == 2:
                            up_parts(i + 1, 0)
                        dve.wait_ge(silu_done, i * 4 + (j + 1))
                        if not first:
                            dve.wait_ge(down_done, i * 4 + (j - 3))
                        dve.tensor_tensor(hid[j], sg[j], up_banks[j].ap[:, T:2 * T], ALU.mult).then_inc(product_done, 1)
                        dve.wait_ge(hh_done, i * 4 + (j + 1))
                        dve.tensor_tensor(hl[j], hid[j], hh[j].bitcast(F32), ALU.subtract).then_inc(hl_done, 1)
                        if j % 2 == 1:
                            dve.wait_ge(down_high, i * 2 + (b + 1))
                            dve.tensor_tensor(low[b][:, 4096:6144], units[b][:, 4096:6144],
                                              high[b][:, 4096:6144].bitcast(F32), ALU.subtract).then_inc(down_low, 1)
                run(body, dve)
                dve.wait_ge(down_done, steps)
                for t in range(TT):
                    for n in range(2):
                        c = slice(n * 512, (n + 1) * 512)
                        dve.tensor_tensor(h[:, t, c], h[:, t, c], acc[t * 2 + n].ap, ALU.add).then_inc(*V.tick())
            for b in banks:
                b.free = V.at()
            for s in slots:
                s.free = (down_done, steps)

        def experts_by_tile():
            E, FE, C = 8, 3584, 512
            NC = FE // C
            MAX_TILES = TT * 2 + E - 1
            TILES = MAX_TILES + 1
            par = Params("moe")
            g_col = par.cols(a["ln_ffn_2"][1], D)
            rt = par.load(par.space(KD * E).rearrange("p (k n) -> p k n", n=E), a["o_router_2"][0].rearrange("(k p) n -> p k n", p=P))
            yield
            enter("route")
            par_row = Params("moe_row", local=True)
            g_row = par_row.rows(a["ln_ffn_2"][1], D)
            slot_of, gate_of = room3(TT, TILES), room3(TT, TILES)
            expert_row = room(TILES, I32)
            n_tiles_cell = room(4, I32)
            pick, pick_gate = room3(TT, P), room3(TT, P)
            combine = room(T)
            silu, hid, y_sb = room(C), room(C), room(D)
            rows = room3(TT, D)
            split_at = top[0]
            rstd, have = row_rstd(h, D, None)

            @block.vector
            def _(dve):
                dve.wait_ge(*have)
                for t in range(TT):
                    dve.tensor_scalar(rows[:, t, :], h[:, t, :], rstd[:, t:t + 1], None, ALU.mult).then_inc(*V.tick())
            normed = transpose_tiles(rows, KD, V.at(), xT, g_col, par.landed())

            @block.vector
            def _(dve):
                dve.wait_ge(*normed)
                dve.wait_ge(*par_row.landed())
                dve.tensor_tensor(rows, rows, g_row.unsqueeze(1).to_broadcast([P, TT, D]), ALU.mult).then_inc(*V.tick())
            logits, gates, chosen = room3(TT, E), room3(TT, E), room3(TT, E)
            best, second = room3(TT, E), room3(TT, E)
            index, rank = room(TT * E, U32).rearrange("p (t e) -> p t e", t=TT), room3(TT, E)
            w1, w2 = room(TT), room(TT)
            bank = take_bank()

            @block.tensor
            def _(pe):
                for due in unseen(pe, bank.free):
                    pe.wait_ge(*due)
                pe.wait_ge(*normed)
                for t in range(TT):
                    for k in range(KD):
                        last = pe.matmul(bank.ap[:, t * E:(t + 1) * E], xT[:, k, t * P:(t + 1) * P], rt[:, k, :],
                                         start=(k == 0), stop=(k == KD - 1))
                last.then_inc(*M.tick())
            have = M.at()

            @block.vector
            def _(dve):
                dve.wait_ge(*have)
                dve.tensor_copy(logits, bank.ap[:, 0:TT * E].rearrange("p (t e) -> p t e", t=TT)).then_inc(*V.tick())
                dve.wait_ge(*V.at())
                for t in range(TT):
                    dve.max(best[:, t, :], logits[:, t, :]).then_inc(*V.tick())
                dve.wait_ge(*V.at())
                for t in range(TT):
                    dve.max_index(index[:, t, :], best[:, t, :], logits[:, t, :]).then_inc(*V.tick())
                dve.tensor_tensor(w2, best[:, :, 1], best[:, :, 0], ALU.subtract).then_inc(*V.tick())
            bank.free = V.at()
            have = V.at()

            @block.scalar
            def _(act):
                act.wait_ge(*have)
                act.activation(w2, w2, ACT.Exp).then_inc(*S.tick())
            have = S.at()

            @block.vector
            def _(dve):
                dve.wait_ge(*have)
                dve.tensor_copy(rank, index).then_inc(*V.tick())
                dve.tensor_scalar(w1, w2, 1.0, None, ALU.add).then_inc(*V.tick())
                dve.wait_ge(*V.at())
                dve.reciprocal(w1, w1).then_inc(*V.tick())
                dve.wait_ge(*V.at())
                dve.tensor_tensor(w2, w2, w1, ALU.mult).then_inc(*V.tick())
                dve.wait_ge(*V.at())
                for t in range(TT):
                    for n, w in enumerate((w1, w2)):
                        dve.tensor_scalar((gates, second)[n][:, t, :], const("ramp")[:, 0:E], rank[:, t, n:n + 1],
                                          w[:, t:t + 1], ALU.is_equal, ALU.mult).then_inc(*V.tick())
                        dve.tensor_scalar((chosen, logits)[n][:, t, :], const("ramp")[:, 0:E], rank[:, t, n:n + 1],
                                          None, ALU.is_equal).then_inc(*V.tick())
                dve.wait_ge(*V.at())
                dve.tensor_tensor(gates, gates, second, ALU.add).then_inc(*V.tick())
                dve.tensor_tensor(chosen, chosen, logits, ALU.add).then_inc(*V.tick())
            have = V.at()
            bank = take_bank()

            @block.tensor
            def _(pe):
                for due in unseen(pe, bank.free):
                    pe.wait_ge(*due)
                pe.wait_ge(*have)
                pe.matmul(bank.ap[:, 0:E], const("before"), chosen[:, 0, :], start=True, stop=True)
                pe.matmul(bank.ap[:, E:2 * E], const("ones"), chosen[:, 0, :], start=True, stop=False)
                pe.matmul(bank.ap[:, E:2 * E], const("before"), chosen[:, 1, :], start=False, stop=True)
                pe.matmul(bank.ap[:, 2 * E:3 * E], const("ones"), chosen[:, 0, :], start=True, stop=False)
                pe.matmul(bank.ap[:, 2 * E:3 * E], const("ones"), chosen[:, 1, :], start=False, stop=True).then_inc(*M.tick())
            have = M.at()
            place = room3(TT, E)
            count, tiles, over, first, zero = (room(E) for _ in range(5))
            off, low = (room(TILES * E).rearrange("p (n e) -> p n e", e=E) for _ in range(2))
            eid = room(TILES)
            tile_ramp = const("ramp")[:, 0:TILES]
            by_tile = lambda x: x.unsqueeze(1).to_broadcast([P, TILES, E])

            @block.vector
            def _(dve):
                dve.wait_ge(*have)
                dve.memset(zero, 0.0).then_inc(*V.tick())
                dve.tensor_copy(count, bank.ap[:, 2 * E:3 * E]).then_inc(*V.tick())
                dve.tensor_copy(place, bank.ap[:, 0:2 * E].rearrange("p (t e) -> p t e", t=TT)).then_inc(*V.tick())
                dve.wait_ge(*V.at())
                dve.tensor_scalar(over, count, float(P), None, ALU.is_gt).then_inc(*V.tick())
                dve.wait_ge(*V.at())
                dve.scalar_tensor_tensor(out=tiles, in0=count, scalar=0.0, in1=over, op0=ALU.is_gt, op1=ALU.add).then_inc(*V.tick())
                dve.wait_ge(*V.at())
                dve.tensor_tensor_scan(first, tiles, zero, 0.0, ALU.add, ALU.add).then_inc(*V.tick())
                dve.wait_ge(*V.at())
                dve.tensor_copy(n_tiles_cell[:, 0:1], first[:, E - 1:E]).then_inc(*V.tick())
                dve.tensor_scalar(n_tiles_cell[:, 1:2], first[:, E - 1:E], 1.0, None, ALU.subtract).then_inc(*V.tick())
                dve.tensor_tensor(over, first, tiles, ALU.subtract).then_inc(*V.tick())
                dve.wait_ge(*V.at())
                dve.scalar_tensor_tensor(out=place, in0=over.unsqueeze(1).to_broadcast([P, TT, E]), scalar=float(P),
                                         in1=place, op0=ALU.mult, op1=ALU.add).then_inc(*V.tick())
                dve.wait_ge(*V.at())
                dve.scalar_tensor_tensor(out=place, in0=place, scalar=1.0, in1=chosen, op0=ALU.add, op1=ALU.mult).then_inc(*V.tick())
                dve.wait_ge(*V.at())
                dve.tensor_scalar(place, place, 1.0, None, ALU.subtract).then_inc(*V.tick())
                dve.tensor_tensor(off, tile_ramp.unsqueeze(2).to_broadcast([P, TILES, E]), by_tile(first),
                                  ALU.is_ge).then_inc(*V.tick())
                dve.wait_ge(*V.at())
                dve.tensor_reduce(eid, off, AX, ALU.add).then_inc(*V.tick())
                dve.wait_ge(*V.at())
                dve.tensor_scalar(eid, eid, float(E - 1), None, ALU.min).then_inc(*V.tick())
                dve.wait_ge(*V.at())
                dve.tensor_copy(expert_row, eid).then_inc(*V.tick())
                for t in range(TT):
                    dve.scalar_tensor_tensor(out=off, in0=tile_ramp.unsqueeze(2).to_broadcast([P, TILES, E]),
                                             scalar=-float(P), in1=by_tile(place[:, t, :]), op0=ALU.mult,
                                             op1=ALU.add).then_inc(*V.tick())
                    dve.wait_ge(*V.at())
                    dve.tensor_scalar(low, off, float(P), None, ALU.is_lt).then_inc(*V.tick())
                    dve.wait_ge(*V.at())
                    dve.scalar_tensor_tensor(out=low, in0=off, scalar=0.0, in1=low, op0=ALU.is_ge,
                                             op1=ALU.mult).then_inc(*V.tick())
                    dve.wait_ge(*V.at())
                    dve.scalar_tensor_tensor(out=off, in0=off, scalar=1.0, in1=low, op0=ALU.add,
                                             op1=ALU.mult).then_inc(*V.tick())
                    dve.tensor_tensor(low, low, by_tile(gates[:, t, :]), ALU.mult).then_inc(*V.tick())
                    dve.wait_ge(*V.at())
                    dve.tensor_reduce(slot_of[:, t, :], off, AX, ALU.add).then_inc(*V.tick())
                    dve.tensor_reduce(gate_of[:, t, :], low, AX, ALU.add).then_inc(*V.tick())
                    dve.wait_ge(*V.at())
                dve.tensor_scalar(slot_of, slot_of, 1.0, None, ALU.subtract).then_inc(*V.tick())
                dve.wait_ge(*V.at())
                for t in range(TT):
                    dve.tensor_scalar(pick[:, t, :], const("ramp"), slot_of[:, t, 0:1], None, ALU.is_equal).then_inc(*V.tick())
            before_moe = V.at()
            enter("moe", split_at)

            def tiles_on(eng):
                return eng.value_load(n_tiles_cell[0:1, 0:1], min_val=4, max_val=MAX_TILES)

            def last_tile_on(eng):
                return eng.value_load(n_tiles_cell[0:1, 1:2], min_val=3, max_val=MAX_TILES - 1)

            top[0] = split_at
            NB = 6
            hi, lo = split_room("moe_weights_high", NB * 1024), split_room("moe_weights_low", NB * 1024)
            xh, xl = split_room("moe_rows_high", D), split_room("moe_rows_low", D)
            hh, hl = split_room("moe_hidden_high", C), split_room("moe_hidden_low", C)
            HALVES, HALF = 42, SLOT // 2
            SLOTS_HERE = 7
            raw = [ring[:, s * HALF:(s + 1) * HALF] for s in range(SLOTS_HERE)]
            names = ("hi_done", "lo_done", "sub_used", "silu_done", "hid_done", "turn_done", "hh_done", "hl_done",
                     "pick_done", "gather_done", "xh_done", "xl_done", "y_done", "combine_turned", "combine_done",
                     "products_done", "combine_copied")
            sems = {n: new_semaphore(f"moe_{n}") for n in names}
            landed = [new_semaphore(f"moe_raw{s}_landed") for s in range(SLOTS_HERE)]
            G_, U_, D_ = range(3)
            pieces = [(G_, 0), (U_, 0)]
            for c in range(1, NC):
                pieces += [(G_, c), (U_, c), (D_, c - 1)]
            pieces.append((D_, NC - 1))
            SUBS = 4 * len(pieces)
            assert HALVES == 2 * len(pieces) and HALVES % SLOTS_HERE == 0
            end = {piece: 4 * n + 4 for n, piece in enumerate(pieces)}
            bg, bu, bt, by0, by1, bc0, bc1, bx = (b.ap for b in banks)
            banks_before = [b.free for b in banks]
            ring_before = [s.free for s in slots]

            @block.sync
            def _(sp):
                for due in unseen(sp, ring_before, before_moe):
                    sp.wait_ge(*due)

                def body(i, first):
                    e = sp.value_load(expert_row[0:1, bass.ds(i, 1)], min_val=0, max_val=E - 1)
                    for u in range(HALVES):
                        p, c = pieces[u // 2]
                        part, s = u % 2, u % SLOTS_HERE
                        if not first or u >= SLOTS_HERE:
                            sp.wait_ge(sems["lo_done"], i * SUBS + 2 * (u - SLOTS_HERE + 1))
                        w = a[("o_moe_w_gate_2", "o_moe_w_up_2", "o_moe_w_down_2")[p]][0].rearrange("e r n -> (e r) n")
                        if p == D_:
                            src = w[bass.ds(e * FE + (c * C + part * C // 2), C // 2), :]
                            width = D
                        else:
                            src = w[bass.ds(e * D + part * D // 2, D // 2), c * C:(c + 1) * C]
                            width = C
                        sp.dma_start(raw[s].rearrange("p (k n) -> p k n", n=width),
                                     src.rearrange("(k p) n -> p k n", p=P)).then_inc(landed[s], 16)
                body(0, True)
                with sp.Fori(1, tiles_on(sp)) as i:
                    body(i, False)

            @block.tensor
            def _(pe):
                def gather():
                    for k in range(KD):
                        out_ = (bc0, bc1)[k // 4][:, (k % 4) * P:(k % 4 + 1) * P]
                        for t in range(TT):
                            last = pe.matmul(out_, rows[:, t, k * P:(k + 1) * P], pick[:, t, :], start=(t == 0),
                                             stop=(t == TT - 1))
                    last.then_inc(sems["gather_done"], 1)

                def combine_products(i):
                    pe.wait_ge(sems["y_done"], i + 1)
                    for n in range(4):
                        t, half = n // 2, n % 2
                        if n >= 2:
                            pe.wait_ge(sems["combine_done"], i * 4 + n - 1)
                        pe.matmul((bc0, bc1)[half], combine[:, t * P:(t + 1) * P], y_sb[:, half * 512:(half + 1) * 512],
                                  start=True, stop=True).then_inc(sems["products_done"], 1)

                def body(i, first):
                    for n, (p, c) in enumerate(pieces):
                        if p == G_ and c == 0:
                            pe.wait_ge(sems["xl_done"], i + 1)
                        if p == G_ and not (first and c == 0):
                            pe.wait_ge(sems["silu_done"], i * NC + c)
                        if p == U_ and not (first and c == 0):
                            pe.wait_ge(sems["hid_done"], i * NC + c)
                        if p == D_ and c == 0 and not first:
                            pe.wait_ge(sems["y_done"], i)
                        if p == D_:
                            pe.wait_ge(sems["hl_done"], i * NC + c + 1)
                        for s in range(4):
                            m = 4 * n + s
                            b = slice((m % NB) * 1024, (m % NB) * 1024 + 1024)
                            pe.wait_ge(sems["lo_done"], i * SUBS + m + 1)
                            if p == D_:
                                f = slice(s * P, (s + 1) * P)
                                wh, wl = (w[:, b].rearrange("p (n c) -> p n c", n=2) for w in (hi, lo))
                                for half in range(2):
                                    last = passes(pe, (by0, by1)[half], (hh[:, f], hl[:, f]), (wh[:, half], wl[:, half]),
                                                  start=(c == 0 and s == 0), stop=(c == NC - 1 and s == 3))
                            else:
                                wh, wl = (w[:, b].rearrange("p (k c) -> p k c", k=2) for w in (hi, lo))
                                for k2 in range(2):
                                    k = slice((2 * s + k2) * P, (2 * s + k2 + 1) * P)
                                    last = passes(pe, (bg, bu)[p], (xh[:, k], xl[:, k]), (wh[:, k2], wl[:, k2]),
                                                  start=(s == 0 and k2 == 0), stop=(s == 3 and k2 == 1))
                            last.then_inc(sems["sub_used"], 1)
                        if p == U_ and c == 0 and not first:
                            combine_products(i - 1)
                        if p == U_ and c == NC - 2:
                            pe.wait_ge(sems["pick_done"], i + 1)
                            if not first:
                                pe.wait_ge(sems["combine_copied"], i)
                            for t in range(TT):
                                last = pe.transpose(bx[:, t * P:(t + 1) * P], pick_gate[:, t, :], ident)
                            last.then_inc(sems["combine_turned"], 1)
                        if p == U_ and c == NC - 1:
                            pe.wait_ge(sems["pick_done"], i + 1)
                            if not first:
                                pe.wait_ge(sems["combine_done"], i * 4)
                            gather()
                        if (p == G_ and c) or (p == D_ and c == NC - 2):
                            ct = c - 1 if p == G_ else NC - 1
                            pe.wait_ge(sems["hid_done"], i * NC + ct + 1)
                            if not (first and ct == 0):
                                pe.wait_ge(sems["hl_done"], i * NC + ct)
                            for s in range(4):
                                last = pe.transpose(bt[:, s * P:(s + 1) * P], hid[:, s * P:(s + 1) * P], ident)
                            last.then_inc(sems["turn_done"], 1)

                for due in unseen(pe, banks_before):
                    pe.wait_ge(*due)
                gather()
                body(0, True)
                with pe.Fori(1, tiles_on(pe)) as i:
                    body(i, False)
                combine_products(last_tile_on(pe))

            @block.scalar
            def _(act):
                def rows_high(i):
                    act.wait_ge(sems["gather_done"], i + 1)
                    for n, b in enumerate((bc0, bc1)):
                        last = act.copy(xh[:, n * 512:(n + 1) * 512], b)
                    last.then_inc(sems["xh_done"], 1)

                def y_out(i):
                    act.wait_ge(sems["sub_used"], i * SUBS + SUBS)
                    act.copy(y_sb[:, 0:512], by0)
                    act.copy(y_sb[:, 512:1024], by1).then_inc(sems["y_done"], 1)

                def body(i, first):
                    for m in range(SUBS):
                        p, c = pieces[m // 4]
                        b = m % NB
                        u = m // 2
                        piece = raw[u % SLOTS_HERE][:, (m % 2) * 1024:(m % 2 + 1) * 1024]
                        if m % 2 == 0:
                            act.wait_ge(landed[u % SLOTS_HERE], i * (16 * HALVES // SLOTS_HERE) + 16 * (u // SLOTS_HERE + 1))
                        if not (first and m < NB):
                            act.wait_ge(sems["sub_used"], i * SUBS + m - NB + 1)
                        act.copy(hi[:, b * 1024:(b + 1) * 1024], piece).then_inc(sems["hi_done"], 1)
                        if m == 5 and not first:
                            y_out(i - 1)
                        for cc in range(NC):
                            if m == end[G_, cc] + 3:
                                act.wait_ge(sems["sub_used"], i * SUBS + end[G_, cc])
                                if not (first and cc == 0):
                                    act.wait_ge(sems["hid_done"], i * NC + cc)
                                act.activation(silu, bg, ACT.Silu).then_inc(sems["silu_done"], 1)
                            turned_at = end[G_, cc + 1] + 4 if cc < NC - 1 else SUBS - 1
                            if m == turned_at:
                                act.wait_ge(sems["turn_done"], i * NC + cc + 1)
                                act.copy(hh, bt).then_inc(sems["hh_done"], 1)
                        if m == end[U_, NC - 1] + 5:
                            rows_high(i + 1)
                        if m == end[U_, NC - 2] + 3:
                            act.wait_ge(sems["combine_turned"], i + 1)
                            act.copy(combine, bx[:, 0:T]).then_inc(sems["combine_copied"], 1)

                rows_high(0)
                body(0, True)
                with act.Fori(1, tiles_on(act)) as i:
                    body(i, False)
                y_out(last_tile_on(act))

            @block.vector
            def _(dve):
                def rows_low(i):
                    dve.wait_ge(sems["xh_done"], i + 1)
                    for n, b in enumerate((bc0, bc1)):
                        last = dve.tensor_tensor(xl[:, n * 512:(n + 1) * 512], b, xh[:, n * 512:(n + 1) * 512].bitcast(F32),
                                                 ALU.subtract)
                    last.then_inc(sems["xl_done"], 1)

                def add_rows(i):
                    for n in range(4):
                        t, c = n // 2, slice((n % 2) * 512, (n % 2 + 1) * 512)
                        dve.wait_ge(sems["products_done"], i * 4 + n + 1)
                        dve.tensor_tensor(h[:, t, c], h[:, t, c], (bc0, bc1)[n % 2], ALU.add).then_inc(sems["combine_done"], 1)

                def body(i, first):
                    for m in range(SUBS):
                        p, c = pieces[m // 4]
                        b = slice((m % NB) * 1024, (m % NB + 1) * 1024)
                        dve.wait_ge(sems["hi_done"], i * SUBS + m + 1)
                        piece = raw[(m // 2) % SLOTS_HERE][:, (m % 2) * 1024:(m % 2 + 1) * 1024]
                        dve.tensor_tensor(lo[:, b], piece, hi[:, b].bitcast(F32),
                                          ALU.subtract).then_inc(sems["lo_done"], 1)
                        for cc in range(NC):
                            if m == end[U_, cc] + 3:
                                dve.wait_ge(sems["sub_used"], i * SUBS + end[U_, cc])
                                dve.wait_ge(sems["silu_done"], i * NC + cc + 1)
                                if not (first and cc == 0):
                                    dve.wait_ge(sems["turn_done"], i * NC + cc)
                                dve.tensor_tensor(hid, silu, bu, ALU.mult).then_inc(sems["hid_done"], 1)
                            turned_at = end[G_, cc + 1] + 4 if cc < NC - 1 else SUBS - 1
                            if m == turned_at:
                                dve.wait_ge(sems["hh_done"], i * NC + cc + 1)
                                dve.tensor_tensor(hl, bt, hh.bitcast(F32), ALU.subtract).then_inc(sems["hl_done"], 1)
                        if m == end[U_, 0] + 4 and not first:
                            add_rows(i - 1)
                        if m == end[U_, 2] + 6:
                            if not first:
                                dve.wait_ge(sems["combine_turned"], i)
                            dve.wait_ge(sems["gather_done"], i + 1)
                            for t in range(TT):
                                dve.tensor_scalar(pick_gate[:, t, :], const("ramp"), slot_of[:, t, bass.ds(i, 1)],
                                                  gate_of[:, t, bass.ds(i, 1)], ALU.is_equal, ALU.mult)
                                last = dve.tensor_scalar(pick[:, t, :], const("ramp"), slot_of[:, t, bass.ds(i + 1, 1)],
                                                         None, ALU.is_equal)
                            last.then_inc(sems["pick_done"], 1)
                        if m == end[U_, NC - 1] + 5:
                            rows_low(i + 1)

                rows_low(0)
                body(0, True)
                with dve.Fori(1, tiles_on(dve)) as i:
                    body(i, False)
                add_rows(last_tile_on(dve))
                dve.memset(hid[:, 0:1], 0.0).then_inc(*V.tick())

        def lru_and_window():
            LW, H, KVH, N = 512, 8, 2, 64
            NT4 = LW // P
            par = Params("mix2")
            g_in = par.cols(a["ln_mix_2"][0], D)
            taps = par.space(NT4 * 4).rearrange("p (i j) -> p i j", j=4)
            for j in range(4):
                par.load(taps[:, :, j], a["e_lru_conv_w_2"][0][j].rearrange("(i p) -> p i", p=P))
            bias = par.cols(a["e_lru_conv_b_2"][0], LW)
            b_a = par.cols(a["e_lru_b_a_2"][0], LW)
            b_i = par.cols(a["e_lru_b_i_2"][0], LW)
            lam = par.cols(a["e_lru_lambda_2"][0], LW)
            gq = par.rows(a["e_q_norm_2"][0], N)
            gk = par.rows(a["e_k_norm_2"][0], N)
            sinks = par.rows(a["e_sinks_2"][0], H)
            yield
            enter("mix2")
            blocks_a, blocks_i = room3(NT4, P), room3(NT4, P)

            @block.vector
            def _(dve):
                dve.memset(blocks_a, 0.0).then_inc(*V.tick())
                dve.memset(blocks_i, 0.0).then_inc(*V.tick())
            zeroed = V.at()

            @block.gpsimd
            def _(pool):
                pool.wait_ge(*zeroed)
            par_blocks = Params("mix2_blocks", local=True)
            for dst, src in ((blocks_a, a["e_lru_w_a_2"][0]), (blocks_i, a["e_lru_w_i_2"][0])):
                for half in range(2):
                    r = slice(half * N, (half + 1) * N)
                    par_blocks.load(dst[r, :, r], src.rearrange("(i two) p q -> two p i q", two=2)[half])
            soft = [room(NT4) for _ in range(3)]

            @block.vector
            def _(dve):
                dve.wait_ge(*par.landed())
                dve.tensor_scalar(lam, lam, -1.0, None, ALU.mult).then_inc(*V.tick())
            lam_ready = softplus(lam, soft, V.at())
            yT = room3(KD, T)
            x = room3(NT4, T)
            gate = room3(NT4, T)
            qkv = room3(TT, (H + 2 * KVH) * N)
            y = room3(TT, H * N)
            keep = top[0]
            normed = norm_turned(h, D, None, xT, g_in, par.landed())

            project(xT, KD, a["e_w_in_2"][0], (H + 2 * KVH) * N, normed, copy_out(qkv), first_col=2 * LW)
            qkv_have = both()
            HK = H + KVH
            scratch = room(HK * N).rearrange("p (n m) -> p n m", m=N)
            halves = [room(HK * 32).rearrange("p (n m) -> p n m", m=32) for _ in range(2)]
            view = [qkv[:, t, :].rearrange("p (n m) -> p n m", m=N) for t in range(TT)]
            for t in range(TT):
                head_norm(view[t][:, 0:H, :], H, N, [qkv_have, V.at()], gq, scratch[:, 0:H, :])
                done = head_norm(view[t][:, H:HK, :], KVH, N, V.at(), gk, scratch[:, 0:KVH, :])
                cos, sin = (const(n).rearrange("p (t m) -> p t m", t=TT)[:, t, :].unsqueeze(1).to_broadcast([P, HK, 32])
                            for n in ("rope_cos", "rope_sin"))
                rotated = rotate(view[t][:, 0:HK, 0:32], view[t][:, 0:HK, 32:64], cos, sin, None, done, halves)

            def finish(i, squash, done, free, keep_mark):
                squash(x[:, i, :], normed)
            conv_project(a["e_w_in_2"][0], 0, NT4, taps, bias, par.landed(), normed, ACT.Identity, finish)
            x_ready = S.at()

            def take(i, ps, mark):
                @block.scalar
                def _(act):
                    act.wait_ge(*mark)
                    act.activation(gate[:, i, :], ps, ACT.Gelu_apprx_tanh).then_inc(*S.tick())
                return S.at()
            project_turned(a["e_w_in_2"][0], LW, NT4, normed, take)
            gate_ready = S.at()
            r, gi = room3(NT4, T), room3(NT4, T)
            for i in range(NT4):
                bank = take_bank()

                @block.tensor
                def _(pe):
                    for due in unseen(pe, bank.free, x_ready, qkv_have):
                        pe.wait_ge(*due)
                    pe.wait_ge(*par_blocks.landed())
                    pe.matmul(bank.ap[:, 0:T], blocks_a[:, i, :], x[:, i, :], start=True, stop=True)
                    pe.matmul(bank.ap[:, T:2 * T], blocks_i[:, i, :], x[:, i, :], start=True, stop=True).then_inc(*M.tick())
                have = M.at()

                @block.scalar
                def _(act):
                    for due in unseen(act, qkv_have):
                        act.wait_ge(*due)
                    act.wait_ge(*have)
                    act.activation(r[:, i, :], bank.ap[:, 0:T], ACT.Sigmoid, bias=b_a[:, i:i + 1]).then_inc(*S.tick())
                    act.activation(gi[:, i, :], bank.ap[:, T:2 * T], ACT.Sigmoid, bias=b_i[:, i:i + 1]).then_inc(*S.tick())
                bank.free = S.at()
            have = S.at()
            root = room3(NT4, T)

            @block.vector
            def _(dve):
                for due in unseen(dve, lam_ready):
                    dve.wait_ge(*due)
                dve.wait_ge(*have)
                for i in range(NT4):
                    dve.tensor_scalar(r[:, i, :], r[:, i, :], lam[:, i:i + 1], -8.0, ALU.mult, ALU.mult).then_inc(*V.tick())
                dve.tensor_tensor(gi, gi, x, ALU.mult).then_inc(*V.tick())
            have = V.at()

            @block.scalar
            def _(act):
                act.wait_ge(*have)
                act.activation(root, r, ACT.Tanh).then_inc(*S.tick())
                act.wait_ge(*S.at())
                act.activation(r, r, ACT.Exp).then_inc(*S.tick())
            have = S.at()

            @block.vector
            def _(dve):
                dve.wait_ge(*have)
                dve.tensor_scalar(x, root, -1.0, 1.0, ALU.mult, ALU.add).then_inc(*V.tick())
                dve.wait_ge(*V.at())
                dve.reciprocal(x, x).then_inc(*V.tick())
                dve.wait_ge(*V.at())
                dve.scalar_tensor_tensor(out=root, in0=root, scalar=-2.0, in1=x, op0=ALU.mult, op1=ALU.mult).then_inc(*V.tick())
                dve.wait_ge(*V.at())
                dve.tensor_scalar(root, root, 1e-30, None, ALU.max).then_inc(*V.tick())
            have = V.at()

            @block.scalar
            def _(act):
                act.wait_ge(*have)
                act.activation(root, root, ACT.Sqrt).then_inc(*S.tick())
            have = S.at()

            @block.vector
            def _(dve):
                for due in unseen(dve, gate_ready):
                    dve.wait_ge(*due)
                dve.wait_ge(*have)
                dve.tensor_tensor(gi, gi, root, ALU.mult).then_inc(*V.tick())
                dve.wait_ge(*V.at())
                for i in range(NT4):
                    dve.tensor_tensor_scan(x[:, i, :], r[:, i, :], gi[:, i, :], 0.0, ALU.mult, ALU.add).then_inc(*V.tick())
                dve.wait_ge(*V.at())
                dve.tensor_tensor(yT[:, 0:NT4, :], x, gate, ALU.mult).then_inc(*V.tick())
            lru_ready = V.at()

            have = attention(lambda t, i: view[t][:, i, :], lambda t, i: view[t][:, H + i // (H // KVH), :],
                             lambda t, i: view[t][:, HK + i // (H // KVH), :], H, N, N, N ** -0.5,
                             lambda i: y[:, :, i * N:(i + 1) * N], rotated, mask=const("band"), causal=True, sink=sinks)
            turned = transpose_tiles(y, 4, have, yT[:, NT4:KD, :])
            project(yT, KD, a["e_w_out_2"][0], D, [turned, lru_ready], add_to_h)

        def deltanet():
            H, N, W = 8, 128, 1024
            par = Params("gdn")
            g_in = par.cols(a["ln_mix_2"][1], D)
            taps = par.space(24 * 4).rearrange("p (i j) -> p i j", j=4)
            for j in range(4):
                par.load(taps[:, :, j], a["o_conv_w_2"][0][j].rearrange("(i p) -> p i", p=P))
            alog = par.rows(a["o_a_log_2"][0], H)
            dtb = par.rows(a["o_dt_bias_2"][0], H)
            g_out = par.rows(a["o_out_norm_2"][0], N)
            yield
            enter("gdn")
            qkv = room3(TT, 3 * W)
            gab = room3(TT, W + 2 * H)
            small = {n: room3(TT, H) for n in ("log_decay", "beta", "cum", "grow", "to_end")}
            soft = [room3(TT, H) for _ in range(3)]
            cumT, betaT = room(T), room(T)
            keep = top[0]
            normed = norm_turned(h, D, None, x_parts, g_in, par.landed())
            top[0] = keep

            def finish(i, squash, done, free, keep_mark):
                ready = squash(done, [free, normed])

                def turn():
                    bank = take_bank()

                    @block.tensor
                    def _(pe):
                        for due in unseen(pe, bank.free, ready):
                            pe.wait_ge(*due)
                        for t in range(TT):
                            last = pe.transpose(bank.ap[:, t * P:(t + 1) * P], done[:, t * P:(t + 1) * P], ident)
                        last.then_inc(*M.tick())
                    turned = M.at()

                    @block.scalar
                    def _(act):
                        act.wait_ge(*turned)
                        act.copy(qkv[:, :, i * P:(i + 1) * P], bank.ap[:, 0:T].rearrange("p (t n) -> p t n", t=TT)).then_inc(*S.tick())
                    bank.free = S.at()
                    keep_mark(turned)
                after_take.append(turn)
            small_have = project_few(a["o_w_in_2"][0], 4 * W, 2 * H, normed, gab[:, :, W:])
            conv_project(a["o_w_in_2"][0], 0, 24, taps, None, par.landed(), normed, ACT.Silu, finish,
                         project_turned_parts)
            conv_done, conv_used = S.at(), [M.at(), V.at()]
            qk = qkv[:, :, 0:2 * W]
            ld, beta, cum, grow, to_end = (small[n] for n in ("log_decay", "beta", "cum", "grow", "to_end"))
            wide = lambda r: r.unsqueeze(1).to_broadcast([P, TT, H])

            made = {}

            def log_decays():
                @block.vector
                def _(dve):
                    for due in unseen(dve, small_have):
                        dve.wait_ge(*due)
                    dve.tensor_tensor(ld, gab[:, :, W:W + H], wide(dtb), ALU.add).then_inc(*V.tick())
                have = softplus(ld, soft, V.at())

                @block.scalar
                def _(act):
                    for due in unseen(act, small_have):
                        act.wait_ge(*due)
                    act.activation(alog, alog, ACT.Exp).then_inc(*S.tick())
                    act.activation(beta, gab[:, :, W + H:W + 2 * H], ACT.Sigmoid).then_inc(*S.tick())
                rate = S.at()

                @block.vector
                def _(dve):
                    for due in unseen(dve, rate):
                        dve.wait_ge(*due)
                    dve.wait_ge(*have)
                    dve.scalar_tensor_tensor(out=ld, in0=ld, scalar=-1.0, in1=wide(alog), op0=ALU.mult,
                                             op1=ALU.mult).then_inc(*V.tick())
                have = V.at()
                made["rate"], made["ld"] = rate, have

            def take_gate(ps, mark, t, c0, n):
                @block.scalar
                def _(act):
                    act.wait_ge(*mark)
                    act.activation(gab[:, t, c0:c0 + n], ps, ACT.Silu).then_inc(*S.tick())
                return S.at()
            scratch = room3(TT, W)

            def norm_of(j, t):
                def write():
                    x = qkv[:, :, j * W:(j + 1) * W].rearrange("p t (h n) -> p t h n", n=N)
                    xt = x[:, t]
                    r, root = per_head_rstd(xt, H, N, [conv_done, V.at()], False, EPS,
                                            scratch[:, t, :].rearrange("p (h n) -> p h n", n=N))

                    @block.vector
                    def _(dve):
                        dve.wait_ge(*root)
                        if j == 0:
                            dve.tensor_scalar(r, r, N ** -0.5, None, ALU.mult).then_inc(*V.tick())
                            dve.wait_ge(*V.at())
                        dve.tensor_tensor(xt, xt, r.unsqueeze(2).to_broadcast([P, H, N]), ALU.mult).then_inc(*V.tick())
                    made["qk"] = V.at()
                return write
            project_parts(x_parts, KD, a["o_w_in_2"][0], W, normed, take_gate, first_col=3 * W,
                          during={0: log_decays, 2: norm_of(0, 0), 3: norm_of(0, 1), 4: norm_of(1, 0), 5: norm_of(1, 1)})
            gate_have = S.at()
            qk_done, rate, have = made["qk"], made["rate"], made["ld"]
            top[0] = keep
            qkT = room3(16, T)
            turned = transpose_tiles(qk, 16, [qk_done, conv_used], qkT)
            bank = take_bank()

            @block.tensor
            def _(pe):
                for due in unseen(pe, bank.free):
                    pe.wait_ge(*due)
                pe.wait_ge(*have)
                flat = ld.rearrange("p t h -> p (t h)")
                pe.matmul(bank.ap[:, 0:2 * H], const("upto"), flat, start=True, stop=True)
                pe.matmul(bank.ap[:, 2 * H:4 * H], const("ones"), flat, start=True, stop=True).then_inc(*M.tick())
            have = M.at()

            @block.vector
            def _(dve):
                dve.wait_ge(*have)
                dve.tensor_copy(cum, bank.ap[:, 0:2 * H].rearrange("p (t h) -> p t h", t=TT)).then_inc(*V.tick())
                dve.wait_ge(*V.at())
                dve.tensor_tensor(to_end, bank.ap[:, 2 * H:4 * H].rearrange("p (t h) -> p t h", t=TT), cum,
                                  ALU.subtract).then_inc(*V.tick())
            bank.free = V.at()
            have = V.at()

            @block.scalar
            def _(act):
                act.wait_ge(*have)
                act.activation(grow, cum, ACT.Exp).then_inc(*S.tick())
                act.activation(to_end, to_end, ACT.Exp).then_inc(*S.tick())
            exp_done = S.at()
            bank = take_bank()

            @block.tensor
            def _(pe):
                for due in unseen(pe, bank.free, rate):
                    pe.wait_ge(*due)
                pe.wait_ge(*have)
                for j, x in enumerate((cum, beta)):
                    for t in range(TT):
                        at = j * T + t * P
                        last = pe.transpose(bank.ap[0:H, at:at + P], x[:, t, :], ident)
                last.then_inc(*M.tick())
            have = M.at()

            @block.vector
            def _(dve):
                dve.wait_ge(*have)
                dve.tensor_copy(cumT[0:H, :], bank.ap[0:H, 0:T]).then_inc(*V.tick())
                dve.tensor_copy(betaT[0:H, :], bank.ap[0:H, T:2 * T]).then_inc(*V.tick())
            bank.free = V.at()
            rows_ready = V.at()
            qT, kT = qkT[:, 0:8, :], qkT[:, 8:16, :]
            q, k, v = (qkv[:, :, j * W:(j + 1) * W] for j in range(3))
            y = q

            @block.vector
            def _(dve):
                for due in unseen(dve, exp_done):
                    dve.wait_ge(*due)
                dve.wait_ge(*turned)
                kh = k[:, 0, :].rearrange("p (h n) -> p h n", n=N)
                dve.tensor_tensor(kh, kh, to_end[:, 0, :].unsqueeze(2).to_broadcast([P, H, N]), ALU.mult).then_inc(*V.tick())
            decayed = V.at()
            state = room(H * N)
            state_ready = None
            names = ("X", "XT", "Y", "NL", "NT", "QK", "DT", "DS", "rhs", "new")
            work = [{n: room(512) for n in names} for _ in range(2)]
            idle = [None, None]
            r4 = lambda ap: ap.rearrange("p (g n) -> p g n", g=4)
            for t in range(TT):
                tok = slice(t * P, (t + 1) * P)
                groups = []
                for g in range(2):
                    w = dict(work[g])
                    hs = range(4 * g, 4 * g + 4)
                    cols = slice(4 * g * N, 4 * (g + 1) * N)
                    bank = take_bank()

                    @block.tensor
                    def _(pe):
                        for due in unseen(pe, bank.free, rows_ready):
                            pe.wait_ge(*due)
                        for j, i in enumerate(hs):
                            last = pe.matmul(bank.ap[:, j * P:(j + 1) * P], ident[0:H, i:i + 1].to_broadcast([H, P]),
                                             cumT[0:H, tok], start=True, stop=True)
                        last.then_inc(*M.tick())
                    have = M.at()

                    @block.vector
                    def _(dve):
                        for due in unseen(dve, have, idle[g]):
                            dve.wait_ge(*due)
                        for j, i in enumerate(hs):
                            c = slice(j * P, (j + 1) * P)
                            dve.scalar_tensor_tensor(out=w["DT"][:, c], in0=bank.ap[:, c], scalar=cum[:, t, i:i + 1],
                                                     in1=const("after_neg"), op0=ALU.subtract,
                                                     op1=ALU.add).then_inc(*V.tick())
                    bank.free = V.at()
                    have = V.at()

                    @block.scalar
                    def _(act):
                        act.wait_ge(*have)
                        act.activation(w["DT"], w["DT"], ACT.Exp).then_inc(*S.tick())
                    have = S.at()

                    @block.gpsimd
                    def _(pool):
                        for due in unseen(pool, have, idle[g]):
                            pool.wait_ge(*due)
                        pool.tensor_tensor(r4(w["DS"]), r4(w["DT"]), const("before").unsqueeze(1).to_broadcast([P, 4, P]),
                                           ALU.mult).then_inc(*G.tick())
                    strict = G.at()
                    bk, bq, bb = take_bank(), take_bank(), take_bank()

                    @block.tensor
                    def _(pe):
                        for due in unseen(pe, bk.free, bq.free, bb.free):
                            pe.wait_ge(*due)
                        pe.wait_ge(*turned)
                        for j, i in enumerate(hs):
                            c = slice(j * P, (j + 1) * P)
                            pe.matmul(bk.ap[:, c], kT[:, i, tok], kT[:, i, tok], start=True, stop=True)
                            pe.matmul(bq.ap[:, c], kT[:, i, tok], qT[:, i, tok], start=True, stop=True)
                            last = pe.matmul(bb.ap[:, c], ident[0:H, i:i + 1].to_broadcast([H, P]), betaT[0:H, tok],
                                             start=True, stop=True)
                        last.then_inc(*M.tick())
                    have = M.at()

                    @block.vector
                    def _(dve):
                        for due in unseen(dve, strict):
                            dve.wait_ge(*due)
                        dve.wait_ge(*have)
                        dve.scalar_tensor_tensor(out=w["NT"], in0=bk.ap, scalar=-1.0, in1=w["DS"], op0=ALU.mult,
                                                 op1=ALU.mult).then_inc(*V.tick())
                        dve.tensor_tensor(w["QK"], bq.ap, w["DT"], ALU.mult).then_inc(*V.tick())
                        dve.wait_ge(*V.at())
                        dve.tensor_tensor(w["NT"], w["NT"], bb.ap, ALU.mult).then_inc(*V.tick())
                    bk.free = bq.free = bb.free = V.at()
                    w.update(made=V.at(), hs=hs, cols=cols)
                    groups.append(w)
                for w in groups:
                    w["N"] = bank = take_bank()

                    @block.tensor
                    def _(pe):
                        for due in unseen(pe, bank.free, w["made"]):
                            pe.wait_ge(*due)
                        for j in range(4):
                            c = slice(j * P, (j + 1) * P)
                            last = pe.transpose(bank.ap[:, c], w["NT"][:, c], ident)
                        last.then_inc(*M.tick())
                    w["ready"] = [w["made"], M.at()]
                    w["NT"] = r4(w["NT"])
                invert(groups)
                for g, w in enumerate(groups):
                    hs, cols = w["hs"], w["cols"]
                    have = None
                    vt = v[:, t, cols]
                    if t:
                        bank = take_bank()

                        @block.tensor
                        def _(pe):
                            for due in unseen(pe, bank.free, state_ready):
                                pe.wait_ge(*due)
                            for j, i in enumerate(hs):
                                last = pe.matmul(bank.ap[:, j * P:(j + 1) * P], kT[:, i, tok], state[:, i * N:(i + 1) * N],
                                                 start=True, stop=True)
                            last.then_inc(*M.tick())
                        have = M.at()

                    @block.vector
                    def _(dve):
                        for due in unseen(dve, have, idle[g]):
                            dve.wait_ge(*due)
                        if t:
                            dve.tensor_tensor(r4(w["rhs"]), r4(bank.ap), grow[:, t, hs[0]:hs[0] + 4].unsqueeze(2).to_broadcast([P, 4, N]),
                                              ALU.mult).then_inc(*V.tick())
                            dve.wait_ge(*V.at())
                            dve.tensor_tensor(w["rhs"], vt, w["rhs"], ALU.subtract).then_inc(*V.tick())
                            dve.wait_ge(*V.at())
                        dve.tensor_tensor(r4(w["rhs"]), r4(w["rhs"] if t else vt),
                                          beta[:, t, hs[0]:hs[0] + 4].unsqueeze(2).to_broadcast([P, 4, N]),
                                          ALU.mult).then_inc(*V.tick())
                    if t:
                        bank.free = V.at()
                    have = V.at()
                    bank = take_bank()

                    @block.tensor
                    def _(pe):
                        for due in unseen(pe, bank.free, w["have"]):
                            pe.wait_ge(*due)
                        pe.wait_ge(*have)
                        for j in range(4):
                            c = slice(j * P, (j + 1) * P)
                            last = pe.matmul(bank.ap[:, c], w["XT"][:, c], w["rhs"][:, c], start=True, stop=True)
                        last.then_inc(*M.tick())
                    have = M.at()

                    @block.scalar
                    def _(act):
                        for due in unseen(act, have, idle[g]):
                            act.wait_ge(*due)
                        act.copy(w["new"], bank.ap).then_inc(*S.tick())
                    bank.free = S.at()
                    have = S.at()
                    bo, bs = take_bank(), take_bank()

                    @block.tensor
                    def _(pe):
                        for due in unseen(pe, bo.free, bs.free, decayed):
                            pe.wait_ge(*due)
                        pe.wait_ge(*have)
                        for j, i in enumerate(hs):
                            c = slice(j * P, (j + 1) * P)
                            hc = slice(i * N, (i + 1) * N)
                            pe.matmul(bo.ap[:, c], w["QK"][:, c], w["new"][:, c], start=True, stop=True)
                            if t:
                                last = pe.matmul(bs.ap[:, c], qT[:, i, tok], state[:, hc], start=True, stop=True)
                            else:
                                last = pe.matmul(bs.ap[:, c], k[:, 0, hc], w["new"][:, c], start=True, stop=True)
                        last.then_inc(*M.tick())
                    have = M.at()
                    idle[g] = M.at()

                    @block.scalar
                    def _(act):
                        act.wait_ge(*have)
                        act.copy(y[:, t, cols], bo.ap).then_inc(*S.tick())
                        if not t:
                            act.copy(state[:, cols], bs.ap).then_inc(*S.tick())
                    bo.free = bs.free = S.at()
                    if t:
                        have = S.at()

                        @block.vector
                        def _(dve):
                            dve.wait_ge(*have)
                            dve.tensor_tensor(r4(w["rhs"]), r4(bs.ap), grow[:, t, hs[0]:hs[0] + 4].unsqueeze(2).to_broadcast([P, 4, N]),
                                              ALU.mult).then_inc(*V.tick())
                            dve.wait_ge(*V.at())
                            dve.tensor_tensor(y[:, t, cols], y[:, t, cols], w["rhs"], ALU.add).then_inc(*V.tick())
                        bs.free = V.at()
                state_ready = S.at()
            have = both()
            top[0] = keep
            scratch = v[:, :, :].rearrange("p t (h n) -> p t h n", n=N)
            for t in range(TT):
                yt = y[:, t, :].rearrange("p (h n) -> p h n", n=N)
                head_norm(yt, H, N, [have, idle[0], idle[1], V.at()], g_out, scratch[:, t])

            @block.vector
            def _(dve):
                for due in unseen(dve, V.at(), gate_have):
                    dve.wait_ge(*due)
                dve.tensor_tensor(y, y, gab[:, :, 0:W], ALU.mult).then_inc(*V.tick())
            y_have = V.at()
            turned = transpose_split(y, KD, y_have, *x_parts, None, None)
            project_parts(x_parts, KD, a["o_w_out_2"][0], D, turned, add_to_h, after=y_have)

        enter("start")
        const_sem = new_semaphore("constants_landed")
        x_sem = new_semaphore("x_landed")

        @block.sync
        def _(sp):
            sp.dma_start(consts[:], a["constants"]).then_inc(const_sem, 16)
            sp.dma_start(h, a["x"][0].rearrange("(t p) d -> p t d", p=P)).then_inc(x_sem, 16)

        @block.vector
        def _(dve):
            dve.wait_ge(const_sem, 16)
            dve.wait_ge(x_sem, 16)

        @block.scalar
        def _(act):
            act.wait_ge(const_sem, 16)
            act.wait_ge(x_sem, 16)

        @block.tensor
        def _(pe):
            pe.wait_ge(const_sem, 16)
            pe.wait_ge(x_sem, 16)

        @block.gpsimd
        def _(pool):
            pool.wait_ge(const_sem, 16)
            pool.wait_ge(x_sem, 16)
        F = 2816

        def ffn_src(layer):
            w13, w2 = a["ffn_w13"][layer], a["ffn_w2"][layer]

            def src(which, c):
                if which == "down":
                    return w2[bass.ds(c, 256), :]
                return w13[:, bass.ds(c if which == "gate" else c + F, 256)]
            return src

        def dense_src(which, c):
            if which == "down":
                return a["e_ffn_w_down_2"][0][bass.ds(c, 256), :]
            return a[f"e_ffn_w_{which}_2"][0][:, bass.ds(c, 256)]

        plan = {
            "mix0": mla_and_rwkv,
            "cross0": lambda: cross(0),
            "ffn0": lambda: swiglu("ffn0", a["ffn_norm"][0], ffn_src(0), F // 256),
            "mamba": mamba,
            "cross1": lambda: cross(1),
            "ffn1": lambda: swiglu("ffn1", a["ffn_norm"][1], ffn_src(1), F // 256),
            "mix2": lru_and_window,
            "ffn2": lambda: swiglu("ffn2", a["ln_ffn_2"][0], dense_src, F // 256),
            "gdn": deltanet,
            "moe": experts_by_tile,
        }
        plan = {name: emit() for name, emit in plan.items() if stages is None or name in stages}
        names = list(plan)
        next(plan[names[0]])

        def load_the_rest():
            for name in names[1:]:
                next(plan[name])
        if names[0] != "mix0":
            load_the_rest()
            if "cross0" in names or "cross1" in names:
                memory_once()
        for name in names:
            next(plan[name], None)
        stored = new_semaphore("output_stored")
        last = [lane.at() for lane in (V, S, M, G) if lane.count]

        @block.sync
        def _(sp):
            for due in unseen(sp, last):
                sp.wait_ge(*due)
            sp.dma_start(out[0].rearrange("(t p) d -> p t d", p=P), h).then_inc(stored, 16)
            sp.wait_ge(stored, 16)


def kernel(**inputs):
    from concourse import bacc
    from concourse.bass_utils import run_bass_kernel_spmd

    nc = bacc.Bacc("TRN2", target_bir_lowering=False, num_devices=1)
    arrays, aps = {}, {}
    for name, value in [*inputs.items(), ("constants", CONSTANTS)]:
        value = np.ascontiguousarray(value)
        arrays[f"in_{name}"] = value
        aps[name] = nc.dram_tensor(f"in_{name}", value.shape, mybir.dt.from_np(value.dtype), kind="ExternalInput").ap()
    out = nc.dram_tensor("out", (1, T, D), F32, kind="ExternalOutput").ap()
    build(nc, aps, out)
    result = run_bass_kernel_spmd(nc, [arrays], core_ids=[0])
    return result.results[0]["out"]
```
